# Optimizing a Trainium2 kernel written in Bass

```python
import math
import jax, jax.numpy as jnp
from jax import lax
import numpy as np

D_MODEL = 1024
BATCH = 1
SEQ = 256
DEPTH = 1

DA_HEADS = 8
DA_HEAD_DIM = 64
DA_V_DIM = 2 * DA_HEAD_DIM
DA_QK_W = DA_HEADS * 2 * DA_HEAD_DIM
DA_V_W = DA_HEADS * DA_V_DIM
Q_BLOCK = 128
DIL_PAIRS = ((128, 1), (512, 4), (2048, 16))
DIL_HEADS_PER_GROUP = 4
DIL_HEADS = DIL_HEADS_PER_GROUP * len(DIL_PAIRS)
DIL_HEAD_DIM = 64
DIL_W = DIL_HEADS * DIL_HEAD_DIM
DIL_OUT_W = DIL_HEADS_PER_GROUP * DIL_HEAD_DIM
N_BRANCH = 2
IN_COLS = 2 * DA_QK_W + DA_V_W + 3 * DIL_W + N_BRANCH * D_MODEL
ROPE_THETA = 500000.0
ROT_DIM = 16
D_FF = 2816
EPS = 1e-6
NEG = -1e30


def rmsnorm(x, g):
    xf = x.astype(jnp.float32)
    y = xf * lax.rsqrt(jnp.mean(xf * xf, axis=-1, keepdims=True) + EPS)
    return (y * g.astype(jnp.float32)).astype(x.dtype)

def rope_tables(positions, dtype):
    inv = ROPE_THETA ** (-(jnp.arange(0, ROT_DIM, 2, dtype=jnp.float32) / ROT_DIM))
    ang = positions.astype(jnp.float32)[..., None] * inv
    return jnp.cos(ang)[:, :, None, :].astype(dtype), jnp.sin(ang)[:, :, None, :].astype(dtype)

def partial_rope(t, cos, sin):
    half = ROT_DIM // 2
    t1, t2, tp = t[..., :half], t[..., half:ROT_DIM], t[..., ROT_DIM:]
    return jnp.concatenate([t1 * cos - t2 * sin, t2 * cos + t1 * sin, tp], axis=-1)

def swiglu(h, w_gu, w_down):
    g, u = jnp.split(h @ w_gu, 2, axis=-1)
    return (jax.nn.silu(g) * u) @ w_down

def diff_attention(q, k, v, lam):
    B, S, H, _, dh = q.shape
    nblk = S // Q_BLOCK
    scale = 1.0 / math.sqrt(dh)
    qb = q.reshape(B, nblk, Q_BLOCK, H, 2, dh).transpose(1, 0, 2, 3, 4, 5)

    def block(qblk):
        s = jnp.einsum('bqhcd,bkhcd->bhcqk', qblk, k, preferred_element_type=jnp.float32) * scale
        p = jax.nn.softmax(s, axis=-1)
        a = p[:, :, 0] - lam * p[:, :, 1]
        return jnp.einsum('bhqk,bkhe->bqhe', a.astype(v.dtype), v,
                          preferred_element_type=jnp.float32).astype(v.dtype)

    o = lax.map(block, qb)
    return o.transpose(1, 0, 2, 3, 4).reshape(B, S, H, 2 * dh)

def dilated_window_attention(q, k, v, dil, half):
    B, S, Hg, dh = q.shape
    L = S // dil
    N = B * dil
    blk = half
    nb = -(-L // blk)
    Lp = nb * blk
    scale = 1.0 / math.sqrt(dh)

    def fold(t):
        return t.reshape(B, L, dil, Hg, dh).transpose(0, 2, 1, 3, 4).reshape(N, L, Hg, dh)

    qf, kf, vf = fold(q), fold(k), fold(v)
    qb = jnp.pad(qf, ((0, 0), (0, Lp - L), (0, 0), (0, 0))).reshape(N, nb, blk, Hg, dh)

    def ctx(t):
        tp = jnp.pad(t, ((0, 0), (blk, Lp - L + blk), (0, 0), (0, 0))).reshape(N, nb + 2, blk, Hg, dh)
        return jnp.concatenate([tp[:, :-2], tp[:, 1:-1], tp[:, 2:]], axis=2)

    kc, vc = ctx(kf), ctx(vf)
    s = jnp.einsum('nbqhd,nbkhd->nbhqk', qb, kc, preferred_element_type=jnp.float32) * scale
    qpos = jnp.arange(nb)[:, None] * blk + jnp.arange(blk)[None, :]
    kpos = (jnp.arange(nb)[:, None] - 1) * blk + jnp.arange(3 * blk)[None, :]
    valid = ((jnp.abs(kpos[:, None, :] - qpos[:, :, None]) <= half)
             & (kpos >= 0)[:, None, :] & (kpos < L)[:, None, :])
    s = jnp.where(valid[None, :, None], s, NEG)
    m = jnp.max(s, axis=-1, keepdims=True)
    e = jnp.exp(s - m)
    l = jnp.sum(e, axis=-1)
    o = jnp.einsum('nbhqk,nbkhd->nbqhd', e.astype(v.dtype), vc, preferred_element_type=jnp.float32)
    o = o / l.transpose(0, 1, 3, 2)[..., None]
    lse = (m[..., 0] + jnp.log(l)).transpose(0, 1, 3, 2)

    def unfold(t):
        t = t.reshape((N, Lp) + t.shape[3:])[:, :L]
        t = t.reshape((B, dil, L) + t.shape[2:])
        return jnp.swapaxes(t, 1, 2).reshape((B, S) + t.shape[3:])

    return unfold(o).astype(q.dtype), unfold(lse)

def first_inputs(seed: int = 0) -> dict:
    key = jax.random.key(seed)
    ks = jax.random.split(key, 24)
    f32 = jnp.float32

    def w(k, shape, fan_in):
        return jax.random.normal(k, shape, f32) * fan_in ** -0.5

    def gain(k, shape):
        return 1.0 + 0.05 * jax.random.normal(k, shape, f32)

    return {
        "x": jax.random.normal(ks[0], (BATCH, SEQ, D_MODEL), f32),
        "positions": jnp.broadcast_to(jnp.arange(SEQ, dtype=jnp.int32), (BATCH, SEQ)),
        "w_in": w(ks[1], (DEPTH, D_MODEL, IN_COLS), D_MODEL),
        "lambda_q1": 0.1 * jax.random.normal(ks[2], (DEPTH, DA_HEAD_DIM), f32),
        "lambda_k1": 0.1 * jax.random.normal(ks[3], (DEPTH, DA_HEAD_DIM), f32),
        "lambda_q2": 0.1 * jax.random.normal(ks[4], (DEPTH, DA_HEAD_DIM), f32),
        "lambda_k2": 0.1 * jax.random.normal(ks[5], (DEPTH, DA_HEAD_DIM), f32),
        "g_subln": gain(ks[6], (DEPTH, DA_V_DIM)),
        "w_proj_a": w(ks[7], (DEPTH, DA_V_W, D_MODEL), DA_V_W),
        "w_proj_b": w(ks[8], (DEPTH, DIL_OUT_W, D_MODEL), DIL_OUT_W),
        "w_out": w(ks[9], (DEPTH, D_MODEL, D_MODEL), D_MODEL),
        "w_gu1": w(ks[10], (DEPTH, D_MODEL, 2 * D_FF), D_MODEL),
        "w_down1": w(ks[11], (DEPTH, D_FF, D_MODEL), D_FF),
        "w_gu2": w(ks[12], (DEPTH, D_MODEL, 2 * D_FF), D_MODEL),
        "w_down2": w(ks[13], (DEPTH, D_FF, D_MODEL), D_FF),
        "g_pre_ffn1": gain(ks[14], (DEPTH, D_MODEL)),
        "g_post_ffn1": gain(ks[15], (DEPTH, D_MODEL)),
        "g_pre_mix": gain(ks[16], (DEPTH, D_MODEL)),
        "g_post_mix": gain(ks[17], (DEPTH, D_MODEL)),
        "g_pre_ffn2": gain(ks[18], (DEPTH, D_MODEL)),
        "g_post_ffn2": gain(ks[19], (DEPTH, D_MODEL)),
    }

def first_block(x, positions, w_in, lambda_q1, lambda_k1, lambda_q2, lambda_k2, g_subln,
              w_proj_a, w_proj_b, w_out, w_gu1, w_down1, w_gu2, w_down2,
              g_pre_ffn1, g_post_ffn1, g_pre_mix, g_post_mix, g_pre_ffn2, g_post_ffn2):
    B, S, D = x.shape
    cos, sin = rope_tables(positions, x.dtype)
    cuts = [int(c) for c in np.cumsum([DA_QK_W, DA_QK_W, DA_V_W, DIL_W, DIL_W, DIL_W, D_MODEL])]

    for l in range(DEPTH):
        lambda_init = 0.8 - 0.6 * math.exp(-0.3 * l)

        h = rmsnorm(x, g_pre_ffn1[l])
        x = x + 0.5 * rmsnorm(swiglu(h, w_gu1[l], w_down1[l]), g_post_ffn1[l])

        h = rmsnorm(x, g_pre_mix[l])
        z = h @ w_in[l]
        qa, ka, va, qd, kd, vd, ga, gb = jnp.split(z, cuts, axis=-1)

        qa = partial_rope(qa.reshape(B, S, 2 * DA_HEADS, DA_HEAD_DIM), cos, sin)
        ka = partial_rope(ka.reshape(B, S, 2 * DA_HEADS, DA_HEAD_DIM), cos, sin)
        qa = qa.reshape(B, S, DA_HEADS, 2, DA_HEAD_DIM)
        ka = ka.reshape(B, S, DA_HEADS, 2, DA_HEAD_DIM)
        va = va.reshape(B, S, DA_HEADS, DA_V_DIM)
        lam = (jnp.exp(jnp.dot(lambda_q1[l], lambda_k1[l]).astype(jnp.float32))
               - jnp.exp(jnp.dot(lambda_q2[l], lambda_k2[l]).astype(jnp.float32)) + lambda_init)
        oa = diff_attention(qa, ka, va, lam)
        oa = (rmsnorm(oa, g_subln[l]) * (1.0 - lambda_init)).reshape(B, S, DA_V_W)

        qd = partial_rope(qd.reshape(B, S, DIL_HEADS, DIL_HEAD_DIM), cos, sin)
        kd = partial_rope(kd.reshape(B, S, DIL_HEADS, DIL_HEAD_DIM), cos, sin)
        vd = vd.reshape(B, S, DIL_HEADS, DIL_HEAD_DIM)
        outs, lses = [], []
        for gi, (win, dil) in enumerate(DIL_PAIRS):
            hs = slice(gi * DIL_HEADS_PER_GROUP, (gi + 1) * DIL_HEADS_PER_GROUP)
            o_g, lse_g = dilated_window_attention(qd[:, :, hs], kd[:, :, hs], vd[:, :, hs],
                                                  dil, win // (2 * dil))
            outs.append(o_g)
            lses.append(lse_g)
        wts = jax.nn.softmax(jnp.stack(lses, axis=0), axis=0)
        od = jnp.sum(wts[..., None].astype(x.dtype) * jnp.stack(outs, axis=0), axis=0)
        od = od.reshape(B, S, DIL_OUT_W)

        merged = jax.nn.sigmoid(ga) * (oa @ w_proj_a[l]) + jax.nn.sigmoid(gb) * (od @ w_proj_b[l])
        x = x + rmsnorm(merged @ w_out[l], g_post_mix[l])

        h = rmsnorm(x, g_pre_ffn2[l])
        x = x + 0.5 * rmsnorm(swiglu(h, w_gu2[l], w_down2[l]), g_post_ffn2[l])

    return x


N_META = 16

D_HY = 512
HY_GROUPS = 8
HY_SHORT = 3
HY_EMB = 33
HY_BANDS = (HY_EMB - 1) // 2
HY_FFN = 64
HY_TARGET = 1e-2
HY_DECAY_HI = 0.3
HY_DECAY_LO = 1.5

D_RG = 1024
RG_HEADS = 8
RG_HEAD_DIM = D_RG // RG_HEADS
RG_CONV = 4
RG_C = 8.0

PEER_HEADS = 8
N_KEYS = 128
N_EXPERTS = N_KEYS * N_KEYS
D_KEY = 256
D_HALF = D_KEY // 2
PEER_TOPK = 16
PEER_CHUNK = 16

D_IN = 3 * D_HY + 2 * D_RG + 2 * D_MODEL


def rmsnorm_2(x, g):
    xf = x.astype(jnp.float32)
    y = xf * lax.rsqrt(jnp.mean(xf * xf, axis=-1, keepdims=True) + EPS)
    return (y * g.astype(jnp.float32)).astype(x.dtype)

def hyena_filter(L, w1, b1, w2, b2, w3, b3, freq):
    f32 = jnp.float32
    t = jnp.linspace(0.0, 1.0, L, dtype=f32)[:, None]
    w = (2.0 * math.pi / L) * jnp.arange(L, dtype=f32)[:, None]
    bands = jnp.linspace(1e-4, HY_BANDS - 1, HY_BANDS, dtype=f32)[None, :]
    z = jnp.concatenate([t, jnp.cos(bands * w), -jnp.sin(bands * w)], axis=-1)
    freq = freq.astype(f32)
    hdn = jnp.sin(freq[0] * (z @ w1.astype(f32) + b1.astype(f32)))
    hdn = jnp.sin(freq[1] * (hdn @ w2.astype(f32) + b2.astype(f32)))
    k = (hdn @ w3.astype(f32) + b3.astype(f32)).reshape(L, 2, D_HY)
    deltas = jnp.abs(jnp.linspace(math.log(HY_TARGET) / HY_DECAY_HI,
                                  math.log(HY_TARGET) / HY_DECAY_LO, D_HY, dtype=f32))
    k = k * jnp.exp(-t * deltas)[:, None, :]
    k_fwd, k_bwd = k[:, 0], k[:, 1]
    return jnp.concatenate([k_fwd, jnp.zeros((1, D_HY), f32), k_bwd[:0:-1]], axis=0)

def fft_long_conv(u, k_full, skip):
    L = u.shape[1]
    uf = u.astype(jnp.float32)
    U = jnp.fft.rfft(uf, n=2 * L, axis=1)
    K = jnp.fft.rfft(k_full, axis=0)
    y = jnp.fft.irfft(U * K[None], n=2 * L, axis=1)[:, :L]
    return (y + uf * skip.astype(jnp.float32)).astype(u.dtype)

def hyena_branch(hy_in, conv_w, conv_b, w1, b1, w2, b2, w3, b3, freq, skip, w_proj):
    B, L, _ = hy_in.shape
    hp = jnp.pad(hy_in, ((0, 0), (1, 1), (0, 0)))
    u = hp[:, 0:L] * conv_w[0] + hp[:, 1:L + 1] * conv_w[1] + hp[:, 2:L + 2] * conv_w[2] + conv_b
    x0, x1, v = u[..., :D_HY], u[..., D_HY:2 * D_HY], u[..., 2 * D_HY:]
    k_full = hyena_filter(L, w1, b1, w2, b2, w3, b3, freq)
    y = fft_long_conv(v * x1, k_full, skip) * x0
    return y @ w_proj

def rglru_direction(x, conv_w, conv_b, gate_w, gate_b, lam):
    B, L, _ = x.shape
    xp = jnp.pad(x, ((0, 0), (RG_CONV - 1, 0), (0, 0)))
    xc = conv_b + sum(xp[:, RG_CONV - 1 - j:RG_CONV - 1 - j + L] * conv_w[j] for j in range(RG_CONV))
    xh = xc.reshape(B, L, RG_HEADS, RG_HEAD_DIM)
    gates = jnp.einsum('blhi,ghij->gblhj', xh, gate_w).reshape(2, B, L, D_RG)
    gates = gates.astype(jnp.float32) + gate_b.astype(jnp.float32)[:, None, None, :]
    r = jax.nn.sigmoid(gates[0])
    i = jax.nn.sigmoid(gates[1])
    log_a = -RG_C * r * jax.nn.softplus(-lam.astype(jnp.float32))
    a = jnp.exp(log_a)
    mult = jnp.sqrt(-jnp.expm1(2.0 * log_a))
    mult = mult.at[:, 0].set(1.0)
    b = mult * i * xc.astype(jnp.float32)

    def combine(p, q):
        a1, b1 = p
        a2, b2 = q
        return a1 * a2, a2 * b1 + b2

    _, h = lax.associative_scan(combine, (a, b), axis=1)
    return h.astype(x.dtype)

def rglru_branch(rg_x, rg_g, conv_w, conv_b, gate_w, gate_b, lam, w_proj):
    h_f = rglru_direction(rg_x, conv_w[0], conv_b[0], gate_w[0], gate_b[0], lam[0])
    h_b = rglru_direction(rg_x[:, ::-1], conv_w[1], conv_b[1], gate_w[1], gate_b[1], lam[1])[:, ::-1]
    y = (h_f + h_b) * jax.nn.gelu(rg_g)
    return y @ w_proj

def peer(x, wq, keys, u_tab, v_tab):
    B, L, D = x.shape
    K = PEER_TOPK
    q = (x @ wq).reshape(B, L, PEER_HEADS, 2, D_HALF)
    s = jnp.einsum('blhpd,hpkd->blhpk', q, keys).astype(jnp.float32)
    ts, ti = lax.top_k(s, K)
    cand = ts[..., 0, :, None] + ts[..., 1, None, :]
    cs, ci = lax.top_k(cand.reshape(B, L, PEER_HEADS, K * K), K)
    e1 = jnp.take_along_axis(ti[..., 0, :], ci // K, axis=-1)
    e2 = jnp.take_along_axis(ti[..., 1, :], ci % K, axis=-1)
    experts = e1 * N_KEYS + e2
    g = jax.nn.softmax(cs, axis=-1).astype(x.dtype)

    nc = L // PEER_CHUNK
    hk = PEER_HEADS * K

    def to_chunks(a, last):
        return a.reshape(B, nc, PEER_CHUNK, last).transpose(1, 0, 2, 3).reshape(nc, B * PEER_CHUNK, last)

    xs = (to_chunks(x, D), to_chunks(experts.reshape(B, L, hk), hk), to_chunks(g.reshape(B, L, hk), hk))

    def chunk_fn(args):
        xt, et, gt = args
        act = jax.nn.gelu(jnp.einsum('td,tkd->tk', xt, u_tab[et])) * gt
        return jnp.einsum('tk,tkd->td', act, v_tab[et])

    out = lax.map(chunk_fn, xs)
    return out.reshape(nc, B, PEER_CHUNK, D).transpose(1, 0, 2, 3).reshape(B, L, D)

def second_inputs(seed: int = 0) -> dict:
    key = jax.random.key(seed)
    ks = iter(jax.random.split(key, 40))
    f32 = jnp.float32

    def nrm(shape, scale):
        return jax.random.normal(next(ks), shape, f32) * scale

    L_TOT = SEQ + N_META
    x = nrm((BATCH, SEQ, D_MODEL), 1.0)
    meta = nrm((N_META, D_MODEL), 1.0)
    g_final = 1.0 + nrm((D_MODEL,), 0.02)
    g_mix = 1.0 + nrm((DEPTH, D_MODEL), 0.02)
    w_in = nrm((DEPTH, D_MODEL, D_IN), D_MODEL ** -0.5)
    b_gate = nrm((DEPTH, 2 * D_MODEL), 0.02)
    hy_conv_w = nrm((DEPTH, HY_SHORT, 3 * D_HY), HY_SHORT ** -0.5)
    hy_conv_b = nrm((DEPTH, 3 * D_HY), 0.02)
    hy_w1 = nrm((DEPTH, HY_EMB, HY_FFN), HY_EMB ** -0.5)
    hy_b1 = nrm((DEPTH, HY_FFN), 0.1)
    hy_w2 = nrm((DEPTH, HY_FFN, HY_FFN), HY_FFN ** -0.5)
    hy_b2 = nrm((DEPTH, HY_FFN), 0.1)
    hy_w3 = nrm((DEPTH, HY_FFN, 2 * D_HY), (HY_FFN * L_TOT / 4.0) ** -0.5)
    hy_b3 = nrm((DEPTH, 2 * D_HY), L_TOT ** -0.5)
    hy_freq = 1.0 + nrm((DEPTH, 2, HY_FFN), 0.02)
    hy_skip = nrm((DEPTH, D_HY), 1.0)
    hy_out = nrm((DEPTH, D_HY, D_MODEL), D_HY ** -0.5)
    rg_conv_w = nrm((DEPTH, 2, RG_CONV, D_RG), RG_CONV ** -0.5)
    rg_conv_b = nrm((DEPTH, 2, D_RG), 0.02)
    rg_gate_w = nrm((DEPTH, 2, 2, RG_HEADS, RG_HEAD_DIM, RG_HEAD_DIM), RG_HEAD_DIM ** -0.5)
    rg_gate_b = nrm((DEPTH, 2, 2, D_RG), 0.02)
    a_c = jax.random.uniform(next(ks), (DEPTH, 2, D_RG), f32, minval=0.9, maxval=0.999)
    a_base = a_c ** (1.0 / RG_C)
    rg_lambda = jnp.log(a_base) - jnp.log1p(-a_base)
    rg_out = nrm((DEPTH, D_RG, D_MODEL), D_RG ** -0.5)
    w_out = nrm((DEPTH, D_MODEL, D_MODEL), D_MODEL ** -0.5)
    g_ffn = 1.0 + nrm((DEPTH, D_MODEL), 0.02)
    peer_wq = nrm((DEPTH, D_MODEL, PEER_HEADS * D_KEY), D_MODEL ** -0.5)
    peer_keys = nrm((DEPTH, PEER_HEADS, 2, N_KEYS, D_HALF), D_HALF ** -0.5)
    peer_u = nrm((DEPTH, N_EXPERTS, D_MODEL), D_MODEL ** -0.5)
    peer_v = nrm((DEPTH, N_EXPERTS, D_MODEL), PEER_HEADS ** -0.5)
    return {'x': x, 'meta': meta, 'g_final': g_final, 'g_mix': g_mix, 'w_in': w_in, 'b_gate': b_gate,
            'hy_conv_w': hy_conv_w, 'hy_conv_b': hy_conv_b, 'hy_w1': hy_w1, 'hy_b1': hy_b1,
            'hy_w2': hy_w2, 'hy_b2': hy_b2, 'hy_w3': hy_w3, 'hy_b3': hy_b3, 'hy_freq': hy_freq,
            'hy_skip': hy_skip, 'hy_out': hy_out, 'rg_conv_w': rg_conv_w, 'rg_conv_b': rg_conv_b,
            'rg_gate_w': rg_gate_w, 'rg_gate_b': rg_gate_b, 'rg_lambda': rg_lambda, 'rg_out': rg_out,
            'w_out': w_out, 'g_ffn': g_ffn, 'peer_wq': peer_wq, 'peer_keys': peer_keys,
            'peer_u': peer_u, 'peer_v': peer_v}

def second_block(x, meta, g_final, g_mix, w_in, b_gate, hy_conv_w, hy_conv_b, hy_w1, hy_b1, hy_w2, hy_b2,
              hy_w3, hy_b3, hy_freq, hy_skip, hy_out, rg_conv_w, rg_conv_b, rg_gate_w, rg_gate_b,
              rg_lambda, rg_out, w_out, g_ffn, peer_wq, peer_keys, peer_u, peer_v):
    B = x.shape[0]
    h = jnp.concatenate([jnp.broadcast_to(meta.astype(x.dtype)[None], (B, N_META, D_MODEL)), x], axis=1)
    s_hy = 3 * D_HY
    s_rx = s_hy + D_RG
    s_rg = s_rx + D_RG
    for l in range(DEPTH):
        n = rmsnorm_2(h, g_mix[l])
        proj = n @ w_in[l]
        y_hy = hyena_branch(proj[..., :s_hy], hy_conv_w[l], hy_conv_b[l], hy_w1[l], hy_b1[l], hy_w2[l],
                            hy_b2[l], hy_w3[l], hy_b3[l], hy_freq[l], hy_skip[l], hy_out[l])
        y_rg = rglru_branch(proj[..., s_hy:s_rx], proj[..., s_rx:s_rg], rg_conv_w[l], rg_conv_b[l],
                            rg_gate_w[l], rg_gate_b[l], rg_lambda[l], rg_out[l])
        gl = proj[..., s_rg:] + b_gate[l]
        merged = jax.nn.sigmoid(gl[..., :D_MODEL]) * y_hy + jax.nn.sigmoid(gl[..., D_MODEL:]) * y_rg
        h = h + merged @ w_out[l]
        h = h + peer(rmsnorm_2(h, g_ffn[l]), peer_wq[l], peer_keys[l], peer_u[l], peer_v[l])
    h = rmsnorm_2(h, g_final)
    return h[:, N_META:]


def setup_inputs(seed=0):
    out = dict(first_inputs(seed))
    for name, value in second_inputs(seed + 1).items():
        if name != "x":
            out[name + "_2"] = value
    return out


def reference(
    x, positions, w_in, lambda_q1, lambda_k1, lambda_q2, lambda_k2, g_subln, w_proj_a, w_proj_b,
    w_out, w_gu1, w_down1, w_gu2, w_down2, g_pre_ffn1, g_post_ffn1, g_pre_mix, g_post_mix,
    g_pre_ffn2, g_post_ffn2, meta_2, g_final_2, g_mix_2, w_in_2, b_gate_2, hy_conv_w_2,
    hy_conv_b_2, hy_w1_2, hy_b1_2, hy_w2_2, hy_b2_2, hy_w3_2, hy_b3_2, hy_freq_2, hy_skip_2,
    hy_out_2, rg_conv_w_2, rg_conv_b_2, rg_gate_w_2, rg_gate_b_2, rg_lambda_2, rg_out_2,
    w_out_2, g_ffn_2, peer_wq_2, peer_keys_2, peer_u_2, peer_v_2,
):
    x = first_block(
        x, positions, w_in, lambda_q1, lambda_k1, lambda_q2, lambda_k2, g_subln, w_proj_a,
        w_proj_b, w_out, w_gu1, w_down1, w_gu2, w_down2, g_pre_ffn1, g_post_ffn1, g_pre_mix,
        g_post_mix, g_pre_ffn2, g_post_ffn2,
    )
    return second_block(
        x, meta_2, g_final_2, g_mix_2, w_in_2, b_gate_2, hy_conv_w_2, hy_conv_b_2, hy_w1_2,
        hy_b1_2, hy_w2_2, hy_b2_2, hy_w3_2, hy_b3_2, hy_freq_2, hy_skip_2, hy_out_2,
        rg_conv_w_2, rg_conv_b_2, rg_gate_w_2, rg_gate_b_2, rg_lambda_2, rg_out_2, w_out_2,
        g_ffn_2, peer_wq_2, peer_keys_2, peer_u_2, peer_v_2,
    )


_drawn_inputs = setup_inputs


def setup_inputs(seed=0):
    import zlib

    import numpy as np

    out = dict(_drawn_inputs(seed))
    spreads = {}
    factors = {'g_final_2': 8.287,
     'g_mix_2': 2.815,
     'b_gate_2': 7.675,
     'hy_conv_b_2': 2.895,
     'hy_b1_2': 2.889,
     'hy_freq_2': 8.0,
     'rg_gate_b_2': 27.47,
     'g_ffn_2': 30.728,
     'rg_conv_b_2': 6.03}
    for name, (base, spread) in spreads.items():
        noise = np.random.default_rng([zlib.crc32(name.encode()), seed]).standard_normal(out[name].shape)
        drawn = base * np.exp(spread * noise) if base else spread * noise
        out[name] = __import__('jax').numpy.asarray(drawn.astype(out[name].dtype))
    for name, factor in factors.items():
        out[name] = (out[name] * factor).astype(out[name].dtype)
    return out
```

```python
import math
from contextlib import ExitStack

import numpy as np

import concourse.bass as bass
from concourse import mybir

F32 = mybir.dt.float32
F32R = mybir.dt.float32r
I32 = mybir.dt.int32
U32 = mybir.dt.uint32
ALU = mybir.AluOpType
ACT = mybir.ActivationFunctionType
AX = mybir.AxisListType

P = 128
D = 1024
KT = D // P
T = 256
NM = 16
L = T + NM
FF = 2816
FT = FF // P
EPS = 1e-6

DA_H = 8
DH = 64
DIL = ((1, 64), (4, 64), (16, 64))
DIL_H = 4
NEG = -1e30
ROT = 16
THETA = 500000.0
LAMBDA_INIT = 0.8 - 0.6 * math.exp(0.0)

HY = 512
HYT = HY // P
HB = 16
FW = 64
RT = D // P
RG_C = 8.0

PH = 8
NK = 128
TOPK = 16

NS = 6
NX = 3
NW = 3
CW = 1024
STAGES = [
    ("ffn1", 3 * FT), ("qk", 28), ("va", KT), ("vd", KT), ("gates", 16), ("proj_b", 2), ("proj_a", 8),
    ("out1", 8), ("ffn2", 3 * FT), ("rgx", 8), ("hyena", 12), ("rggate", 4), ("rgg", 8), ("gl", 16),
    ("hyout", 4), ("rgout", 8), ("out2", 8), ("wq", 16), ("keys", 2), ("experts", 2 * NK),
]
START, N_CHUNKS = {}, 0
for _name, _n in STAGES:
    START[_name] = N_CHUNKS
    N_CHUNKS += _n

COLUMNS = [
    ("g_pre_ffn1", 8), ("g_post_ffn1", 8), ("g_pre_mix", 8), ("g_post_mix", 8), ("g_pre_ffn2", 8),
    ("g_post_ffn2", 8), ("g_mix_2", 8), ("g_ffn_2", 8), ("g_final_2", 8), ("g_subln", 1),
    ("b_gate_2", 16), ("hy_conv_w_2", 36), ("hy_conv_b_2", 12), ("hy_skip_2", 4), ("rg_conv_w_2", 64),
    ("rg_conv_b_2", 16), ("rg_gate_b_2", 32), ("rg_lambda_2", 16), ("hy_b1_2", 1), ("hy_b2_2", 1),
    ("hy_freq_2", 2), ("lambda_q1", 1), ("lambda_k1", 1), ("lambda_q2", 1), ("lambda_k2", 1),
    ("rope_inv", 1), ("rope_sign", 1),
]
COL, N_COLS = {}, 0
for _name, _n in COLUMNS:
    COL[_name] = N_COLS
    N_COLS += _n

LT = [(0, P), (P, P), (2 * P, NM)]

NORMS = ["g_pre_ffn1", "g_post_ffn1", "g_pre_mix", "g_post_mix", "g_pre_ffn2", "g_post_ffn2", "g_mix_2",
         "g_ffn_2", "g_final_2"]
TWO_PI = 2.0 * math.pi
ROUND = 1.5 * 2.0 ** 23
PI1 = 6.28125
PI2 = float(np.float32(np.round((TWO_PI - PI1) * 2 ** 21) / 2 ** 21))
PI3 = float(np.float32(TWO_PI - PI1 - PI2))
PI_IN = 3.1415925


def build(nc, x_d, meta_d, pos_d, stream_d, cols_d, w1_d, w2_d, w3_d, zt_d, decay_d, dft_d, idft_d, mask_d, sq_d, out_d):
    with ExitStack() as ctx:
        place = {}

        def sb(name, shape, dt=F32):
            place[name] = -(-nc.sbuf_base // 32) * 32
            return ctx.enter_context(nc.sbuf_tensor(name, shape, dt))

        def over(name, under, at, shape):
            return nc.alloc_sbuf_tensor_at(name, shape, dtype=F32R, offset=place[under] + 4 * at)

        def sem(name):
            return ctx.enter_context(nc.semaphore(name))

        ring = sb("ring", [P, NS, CW])
        x = sb("x", [P, KT, L])
        h = sb("h", [P, KT, L])
        sq = sb("sq", [P, KT, L])
        cols = sb("cols", [P, N_COLS])
        square = sb("square", [P, 3, P])
        ident, swap, ones = square[:, 0, :], square[:, 1, :], square[:, 2, :]
        stat = sb("stat", [P, 2, L])
        var, std, rstd = stat[:, 0, :], stat[:, 0, :], stat[:, 1, :]
        small = sb("small", [P, 256])
        arena = sb("arena", [P, NK * T])
        aux = sb("aux", [P, 6240])
        FFN_AT, FFN_N = 9984, NW * 2 * CW + 2 * KT * T + 4 * T
        ffn_split = over("ffn_split", "arena", FFN_AT, [P, FFN_N])
        peer_hi = over("peer_hi", "ring", NX * CW, [P, NW, CW])
        peer_split = over("peer_split", "aux", 0, [P, NW * CW + 4 * T])
        peer_h = over("peer_h_hi", "sq", 0, [P, KT, L]), over("peer_h_lo", "h", 0, [P, KT, L])
        ps = ctx.enter_context(nc.psum_tensor("ps", [P, 8, 512], F32))

        class Space:

            def __init__(self, base, at=0):
                self.base, self.at = base, at

            def take(self, *shape):
                n = int(np.prod(shape))
                piece = self.base[:, self.at:self.at + n]
                self.at += n
                assert self.at <= self.base.shape[1], (self.at, self.base.shape)
                if len(shape) == 2:
                    piece = piece.rearrange("p (a b) -> p a b", a=shape[0])
                if len(shape) == 3:
                    piece = piece.rearrange("p (a b c) -> p a b c", a=shape[0], b=shape[1])
                return piece

        def col(name, n=0):
            at = COL[name] + n
            return cols[:, at:at + 1]

        def split_pair(s, *shape):
            return s.take(*shape), s.take(*shape)

        s = Space(aux)
        kre, kim = s.take(3, HY), s.take(3, HY)
        dft = s.take(3, 2, L)
        idft = s.take(3, 2, T)
        s = Space(aux)
        sel_b, sel_a = s.take(8, NK), s.take(8, NK)
        s.take(2 * CW)
        e1t, e2t, gt = s.take(T), s.take(T), s.take(T)
        iota = s.take(NK)
        ge_p, act_p = s.take(2, T), s.take(2, T)
        s = Space(peer_split)
        peer_lo = s.take(NW, CW)
        peer_w = [(peer_hi[:, n, :], peer_lo[:, (n + 2) % NW, :]) for n in range(NW)]
        peer_part = split_pair(s, 2, T)

        s = Space(arena, 23360)
        assert FFN_AT + FFN_N <= s.at
        zt, w1, w2, w3 = s.take(L), s.take(FW), s.take(FW), s.take(2 * HY)
        arg, turn, hdn = s.take(L), s.take(L), s.take(L)
        decay = s.take(3, 2, HY)
        kfb, ksum, kdif = s.take(2, HY), s.take(3, HY), s.take(3, HY)
        s = Space(arena)
        rope_c, rope_s = s.take(T), s.take(T)
        posi = s.take(T)
        ang, angq = s.take(T), s.take(T)
        silu, act = s.take(2, T), s.take(2, T)
        first = s.at
        raw, rot = s.take(2, T), s.take(2, T)
        qk = s.take(28, T)
        va, vd = s.take(2, D), s.take(2, 3 * DIL_H * DH)
        sg = s.take(16, T)
        mask = s.take(3, 2, T)
        da_p, da_a, da_t = s.take(2, 4, T), s.take(2, 2, T), s.take(2, T)
        da_at, ot = s.take(2, 2 * T), s.take(DA_H, T)
        dl_p, dl_pt = s.take(3, 2, T), s.take(3, 2, T)
        odt = s.take(2, T)
        s = Space(ffn_split)
        ffn_w = [split_pair(s, CW) for _ in range(NW)]
        ffn_h, ffn_act = split_pair(s, KT, T), split_pair(s, 2, T)
        s = Space(arena, first + 4 * T)
        oa, srstd, merged = s.take(DA_H, T), s.take(DA_H, T), s.take(KT, T)
        s = Space(arena)
        rgx = s.take(RT, L)
        xc = [s.take(RT, L), s.take(RT, T)]
        r_g = [s.take(RT, L), s.take(RT, T)]
        i_g = [s.take(RT, L), s.take(RT, T)]
        m_g = [s.take(RT, L), s.take(RT, T)]
        hu = s.take(12, L)
        ys = s.take(3, 2, HY)
        gg = s.take(RT, T)
        sgl = s.take(16, T)
        s = Space(arena, 0)
        merged2 = s.take(KT, T)
        vt = sq[:, :, :].rearrange("p a b -> p (a b)")[:, 0:3 * HY].rearrange("p (a b) -> p a b", a=3)
        s = Space(arena)
        pq = s.take(16, T)
        sc = s.take(2, 16, NK)
        scr = s.take(2 * NK)
        tv, ti, tif = s.take(2, 16, TOPK), s.take(2, 16, TOPK), s.take(2, 16, TOPK)
        cand = s.take(2, PH, TOPK * TOPK)
        cv, ci = s.take(2, PH, TOPK), s.take(2, PH, TOPK)
        cij, cijf = s.take(2, 2, PH * TOPK), s.take(2, 2, PH * TOPK)
        hot = s.take(PH * TOPK, TOPK)
        ew = s.take(3, 2, PH * TOPK)
        io16 = s.take(TOPK)
        gates_all = arena[:, :].rearrange("p (e t) -> p e t", t=T)

        landed = [sem(f"landed{i}") for i in range(NS)]
        chunk_done = sem("chunk_done")
        expert_landed = [sem(f"expert_landed{i}") for i in range(NX)]
        hi_ready = sem("hi_ready")
        lo_up, lo_down = sem("lo_up"), sem("lo_down")
        h_hi, h_lo = sem("h_hi"), sem("h_lo")
        loaded_mask = sem("loaded_mask")
        loaded_const = sem("loaded_const")
        loaded_x = sem("loaded_x")
        iota_ready = sem("iota_ready")
        dve_step = sem("dve_step")
        act_step = sem("act_step")
        sq_ready, ssq_ready, var_ready, std_ready = sem("sq_ready"), sem("ssq_ready"), sem("var_ready"), sem("std_ready")
        h_ready, x_ready = sem("h_ready"), sem("x_ready")
        flt_pe, flt_arg, flt_sin, flt_k = sem("flt_pe"), sem("flt_arg"), sem("flt_sin"), sem("flt_k")
        lam_prod, lam_sum, lam_exp = sem("lam_prod"), sem("lam_sum"), sem("lam_exp")
        rope_arg, rope_sin = sem("rope_arg"), sem("rope_sin")
        silu_ready, act_ready = sem("silu_ready"), sem("act_ready")
        act_gated, act_hi = sem("act_gated"), sem("act_hi")
        raw_copied, swapped, qk_ready = sem("raw_copied"), sem("swapped"), sem("qk_ready")
        v_copied, gate_copied = sem("v_copied"), sem("gate_copied")
        da_scores, da_nbias, da_exp, da_mixed = sem("da_scores"), sem("da_nbias"), sem("da_exp"), sem("da_mixed")
        da_turned, da_tcopied, da_out, ot_ready = sem("da_turned"), sem("da_tcopied"), sem("da_out"), sem("ot_ready")
        dl_scores, dl_nbias, dl_exp, dl_prob = sem("dl_scores"), sem("dl_nbias"), sem("dl_exp"), sem("dl_prob")
        dl_turned, dl_tcopied, dl_out, od_ready = sem("dl_turned"), sem("dl_tcopied"), sem("dl_out"), sem("od_ready")
        sub_sq, sub_sum, sub_var, sub_std, oa_ready = sem("sub_sq"), sem("sub_sum"), sem("sub_var"), sem("sub_std"), sem("oa_ready")
        sg_ready, merged_ready = sem("sg_ready"), sem("merged_ready")
        in2_copied, hy_conv, rg_conv, vx_ready = sem("in2_copied"), sem("hy_conv"), sem("rg_conv"), sem("vx_ready")
        vt_turned, vt_ready, spec_ready, ys_ready = sem("vt_turned"), sem("vt_ready"), sem("spec_ready"), sem("ys_ready")
        conv_out, hy_ready = sem("conv_out"), sem("hy_ready")
        rg_gated, rg_tanh, rg_den, rg_sqrt, rg_ready, decay_ready = (
            sem("rg_gated"), sem("rg_tanh"), sem("rg_den"), sem("rg_sqrt"), sem("rg_ready"), sem("decay_ready"))
        merged2_ready = sem("merged2_ready")
        lam_e, sp_ready = sem("lam_e"), sem("sp_ready")
        pq_copied, sc_out, sc_copied = sem("pq_copied"), sem("sc_out"), sem("sc_copied")
        cv_ready, ce_ready, ew_ready, ew_turned, ewt_ready = (
            sem("cv_ready"), sem("ce_ready"), sem("ew_ready"), sem("ew_turned"), sem("ewt_ready"))
        ab_ready, g_token, g_copied = sem("ab_ready"), sem("g_token"), sem("g_copied")
        gelu_ready, peer_act = sem("gelu_ready"), sem("peer_act")
        stored = sem("stored")
        N_CONST = 11

        def acc(n):
            return ps[:, n // 2, (n % 2) * T:(n % 2 + 1) * T]

        def real(buf, k):
            return buf[:, k, NM:L]

        def ffn_up(base, j):
            return base + (1 if j == 0 else 3 * j)

        def ffn_down(base, j):
            return base + (3 * FT - 1 if j == FT - 1 else 3 * j + 4)

        HI_EXPERTS, UP_EXPERTS, DOWN_EXPERTS = 2 * 3 * FT, 2 * 2 * FT, 2 * FT

        def expert_u(base, e):
            return base + (0 if e == 0 else 2 * e - 1)

        def expert_v(base, e):
            return base + (2 * NK - 1 if e == NK - 1 else 2 * e + 2)

        def tmp_spec(fn, n):
            return rgx[0:fn, :, :].rearrange("p a b -> p (a b)")[:, n * HY:(n + 1) * HY]

        def tmp_mix(n):
            return ys[:, 0, 0, n * T:(n + 1) * T]

        def i_tmp(d):
            return rgx[:, :, 0:(L if d == 0 else T)]

        def gl_tile(pe, tile, m):
            pe.wait_ge(in2_copied, 5 * RT + RT + m - 1)
            tile(START["gl"] + m, ps[:, 4 + m % 2, 0:T], lambda k: real(h, k)).then_inc(chunk_done, 1)

        block = ctx.enter_context(nc.Block())

        @block.sync
        def _(sp):
            sp.dma_start(x[:, :, NM:L], x_d).then_inc(loaded_x, 16)
            for c in range(NS):
                sp.dma_start(ring[:, c, :], stream_d[c]).then_inc(landed[c], 16)
            base = START["experts"]
            whole = (base - NS) // NS
            with sp.Fori(0, whole) as i:
                for m in range(NS):
                    sp.wait_ge(chunk_done, i * NS + (m + 1))
                    sp.dma_start(ring[:, m, :], stream_d[bass.ds(i * NS + (NS + m), 1), :, :].rearrange("a p n -> p (a n)")).then_inc(landed[m], 16)
            for c in range(NS + whole * NS, base):
                sp.wait_ge(chunk_done, c - NS + 1)
                sp.dma_start(ring[:, c % NS, :], stream_d[c]).then_inc(landed[c % NS], 16)
            for c in range(NX):
                sp.wait_ge(chunk_done, max(n for n in range(base) if n % NS == c) + 1)
                sp.dma_start(ring[:, c, :], stream_d[base + c]).then_inc(expert_landed[c], 16)
            sp.wait_ge(lo_up, UP_EXPERTS + 1)
            sp.dma_start(ring[:, 0, :], stream_d[base + NX]).then_inc(expert_landed[0], 16)
            with sp.Fori(0, (NK - 2) // 3) as i:
                for m in range(6):
                    if m % 2 == 0:
                        sp.wait_ge(lo_up, i * 3 + (UP_EXPERTS + 2 + m // 2))
                    else:
                        sp.wait_ge(lo_down, i * 3 + (DOWN_EXPERTS + 1 + m // 2))
                    slot = (NX + 1 + m) % NX
                    sp.dma_start(ring[:, slot, :], stream_d[bass.ds(i * 6 + (base + NX + 1 + m), 1), :, :].rearrange("a p n -> p (a n)")).then_inc(expert_landed[slot], 16)
            sp.wait_ge(h_ready, 8 * 6)
            sp.dma_start(out_d, h[:, :, NM:L]).then_inc(stored, 16)
            sp.wait_ge(stored, 16)

        @block.gpsimd
        def _(pool):
            def lo(r, done, made, slot, split):
                if made is not None:
                    pool.wait_ge(lo_up, made)
                pool.wait_ge(hi_ready, done)
                nc.gpsimd.tensor_tensor(split[r % NW][1], ring[:, slot, :], split[r % NW][0].bitcast(F32), ALU.subtract).then_inc(lo_up, 1)

            def ffn(f, base):
                for r in range(4):
                    lo(r, f * 3 * FT + r + 1, f * 2 * FT + r if f or r else None, (base + r) % NS, ffn_w)
                with pool.Fori(0, (FT - 2) // 2) as i:
                    for m in (2, 3):
                        for half, r in enumerate((3 * m - 1, 3 * m)):
                            lo(r, i * 6 + (f * 3 * FT + r + 1), i * 4 + (f * 2 * FT + 2 * m + half), (base + r) % NS, ffn_w)

            nc.gpsimd.memset(hdn[64:65, :], 1.0).then_inc(iota_ready, 1)
            pool.wait_ge(iota_ready, 1)
            ffn(0, START["ffn1"])
            ffn(1, START["ffn2"])
            pool.wait_ge(lo_up, UP_EXPERTS)
            pool.wait_ge(x_ready, 8 * 4)
            nc.gpsimd.iota(iota, pattern=[[1, NK]], base=0, channel_multiplier=0, allow_small_or_imprecise_dtypes=True).then_inc(iota_ready, 1)
            pool.wait_ge(iota_ready, 2)
            nc.gpsimd.iota(io16, pattern=[[1, TOPK]], base=0, channel_multiplier=0, allow_small_or_imprecise_dtypes=True).then_inc(iota_ready, 1)
            pool.wait_ge(iota_ready, 3)
            pool.wait_ge(chunk_done, START["keys"])
            for k in range(KT):
                if k:
                    pool.wait_ge(h_lo, 2 * KT + k)
                pool.wait_ge(h_hi, 2 * KT + k + 1)
                nc.gpsimd.tensor_tensor(peer_h[1][:, k, NM:L], real(h, k), peer_h[0][:, k, 0:T].bitcast(F32), ALU.subtract).then_inc(h_lo, 1)
            pool.wait_ge(h_lo, 3 * KT)
            lo(0, HI_EXPERTS + 1, None, 0, peer_w)
            pool.wait_ge(g_copied, T // 4)
            lo(1, HI_EXPERTS + 2, UP_EXPERTS + 1, 1, peer_w)
            with pool.Fori(0, (NK - 2) // 6) as i:
                for m in range(2, 8):
                    r = expert_u(0, m)
                    lo(r, i * 12 + (HI_EXPERTS + r + 1), i * 6 + (UP_EXPERTS + m), r % NX, peer_w)

        @block.scalar
        def _(act_e):
            steps = [0]

            def link(ins):
                steps[0] += 1
                ins.then_inc(act_step, 1)
                act_e.wait_ge(act_step, steps[0])

            A = nc.scalar.activation
            act_e.dma_start(cols[:], cols_d).then_inc(loaded_const, 16)
            act_e.dma_start(square[:], sq_d).then_inc(loaded_const, 16)
            act_e.dma_start(posi.bitcast(I32), pos_d).then_inc(loaded_const, 16)
            act_e.dma_start(x[:, :, 0:NM], meta_d).then_inc(loaded_const, 16)
            act_e.dma_start(zt[0:2 * HB + 1, :], zt_d).then_inc(loaded_const, 16)
            act_e.dma_start(w1[0:2 * HB + 1, :], w1_d).then_inc(loaded_const, 16)
            act_e.dma_start(w2[0:FW, :], w2_d).then_inc(loaded_const, 16)
            act_e.dma_start(w3[0:FW + 1, :], w3_d).then_inc(loaded_const, 16)
            act_e.dma_start(decay, decay_d).then_inc(loaded_const, 16)
            act_e.dma_start(dft, dft_d).then_inc(loaded_const, 16)
            act_e.dma_start(idft, idft_d).then_inc(loaded_const, 16)

            def squares(n, src, w):
                if n:
                    act_e.wait_ge(ssq_ready, n)
                for k in range(KT):
                    A(sq[:, k, 0:w], src(k), ACT.Square).then_inc(sq_ready, 1)

            def root(n, w):
                act_e.wait_ge(var_ready, n + 1)
                A(std[:, 0:w], var[:, 0:w], ACT.Sqrt).then_inc(std_ready, 1)

            def ffn_hi(f, base, r, i=None):
                c = base + r
                n = 16 * (c // NS + 1)
                act_e.wait_ge(landed[c % NS], n if i is None else i * 16 + n)
                if r >= NW:
                    act_e.wait_ge(chunk_done, c - NW + 1 if i is None else i * 6 + (c - NW + 1))
                A(ffn_w[r % NW][0], ring[:, c % NS, :], ACT.Copy).then_inc(hi_ready, 1)

            def input_hi(n, ready, dst):
                for k in range(KT):
                    act_e.wait_ge(h_ready, ready + k + 1)
                    A(dst[:, k, 0:T], real(h, k), ACT.Copy).then_inc(h_hi, 1)

            act_e.wait_ge(loaded_x, 16)
            squares(0, lambda k: real(x, k), T)
            root(0, T)
            for r in range(NW):
                ffn_hi(0, START["ffn1"], r)
            input_hi(0, 0, ffn_h[0])
            act_e.wait_ge(rope_arg, 2)
            A(rope_s, ang, ACT.Sin).then_inc(rope_sin, 1)
            A(rope_c, angq, ACT.Sin).then_inc(rope_sin, 1)
            for layer in range(2):
                act_e.wait_ge(flt_arg, layer + 1)
                A(hdn[0:FW, :], arg[0:FW, :], ACT.Sin).then_inc(flt_sin, 1)
            act_e.wait_ge(lam_sum, 1)
            A(small[:, 4:6], ps[:, 7, 0:2], ACT.Exp).then_inc(lam_exp, 1)
            act_e.wait_ge(lam_e, 1)
            A(small[:, 16:32], small[:, 32:48], ACT.Exp, scale=-1.0).then_inc(lam_exp, 1)

            def ffn(f, base):
                def one(done, buf):
                    act_e.wait_ge(chunk_done, done)
                    A(silu[:, buf, :], ps[:, 4 + buf, 0:T], ACT.Silu).then_inc(silu_ready, 1)

                ffn_hi(f, base, 3)
                if f:
                    act_e.wait_ge(act_ready, FT - 1)
                one(base + 2, 0)
                ffn_hi(f, base, 4)
                ffn_hi(f, base, 5)
                if f:
                    act_e.wait_ge(act_ready, FT)
                one(base + 4, 1)
                with act_e.Fori(0, (FT - 2) // 2) as i:
                    for m in (2, 3):
                        for r in range(3 * m, 3 * m + 3):
                            ffn_hi(f, base, r, i)
                        act_e.wait_ge(act_ready, i * 2 + (f * FT + m - 1))
                        one(i * 6 + (base + 3 * m + 1), m % 2)

            ffn(0, START["ffn1"])
            act_e.dma_start(mask, mask_d).then_inc(loaded_mask, 16)
            act_e.wait_ge(chunk_done, START["qk"])
            squares(1, acc, T)
            root(1, T)
            act_e.wait_ge(x_ready, 8)
            squares(2, lambda k: real(x, k), T)
            root(2, T)
            for n in range(28):
                act_e.wait_ge(chunk_done, START["qk"] + n + 1)
                if n >= 2:
                    act_e.wait_ge(qk_ready, n - 1)
                A(raw[:, n % 2, :], ps[:, 4 + n % 2, 0:T], ACT.Copy).then_inc(raw_copied, 1)
            act_e.wait_ge(chunk_done, START["vd"])
            for b in range(4):
                A(va[:, b // 2, (b % 2) * 512:(b % 2 + 1) * 512], ps[:, b, :], ACT.Copy).then_inc(v_copied, 1)

            def da_exps(hd):
                act_e.wait_ge(da_nbias, hd + 1)
                if hd >= 2:
                    act_e.wait_ge(da_mixed, 2 * (hd - 1))
                for c in range(2):
                    for q in range(2):
                        A(da_p[:, hd % 2, 2 * c + q, :], ps[:, 2 * (hd % 2) + c, q * T:(q + 1) * T], ACT.Exp,
                          bias=small[:, 64 + 8 * (hd % 2) + 2 * c + q:65 + 8 * (hd % 2) + 2 * c + q], scale=DH ** -0.5,
                          accum_out=small[:, 80 + 8 * (hd % 2) + 2 * c + q:81 + 8 * (hd % 2) + 2 * c + q]).then_inc(da_exp, 1)

            def gate_copy(n):
                act_e.wait_ge(chunk_done, START["gates"] + n + 1)
                A(sg[:, n, :], ps[:, 4 + n % 2, 0:T], ACT.Copy).then_inc(gate_copied, 1)

            da_exps(0)
            for hd in range(DA_H):
                if hd + 1 < DA_H:
                    da_exps(hd + 1)
                gate_copy(2 * hd)
                act_e.wait_ge(da_turned, hd + 1)
                if hd >= 2:
                    act_e.wait_ge(da_out, hd - 1)
                A(da_at[:, hd % 2, :], ps[:, 6, :], ACT.Copy).then_inc(da_tcopied, 1)
                gate_copy(2 * hd + 1)
            for j in range(DIL_H):
                act_e.wait_ge(dl_nbias, j + 1)
                for q in range(2):
                    A(dl_p[:, :, q, :], dl_p[:, :, q, :], ACT.Exp, bias=small[:, 100 + q:101 + q], scale=DH ** -0.5,
                      accum_out=small[:, 104 + q:105 + q]).then_inc(dl_exp, 1)
                act_e.wait_ge(dl_turned, j + 1)
                if j >= 1:
                    act_e.wait_ge(dl_out, j)
                A(dl_pt[:, :, :, :].rearrange("p a b c -> p a (b c)"), ps[:, 3:6, :], ACT.Copy).then_inc(dl_tcopied, 1)
            act_e.wait_ge(ssq_ready, 3)
            for hd in range(DA_H):
                act_e.wait_ge(ot_ready, hd + 1)
                A(sq[:, hd, 0:T], ot[:, hd, :], ACT.Square).then_inc(sub_sq, 1)
            A(sg[:, :, :], sg[:, :, :], ACT.Sigmoid).then_inc(sg_ready, 1)
            act_e.wait_ge(sub_var, 1)
            A(srstd[:, :, :], srstd[:, :, :], ACT.Sqrt).then_inc(sub_std, 1)
            act_e.wait_ge(sub_sum, 1)
            act_e.wait_ge(merged_ready, KT)
            for r in range(NW):
                ffn_hi(1, START["ffn2"], r)
            act_e.wait_ge(chunk_done, START["ffn2"])
            squares(3, acc, T)
            root(3, T)
            act_e.wait_ge(x_ready, 16)
            squares(4, lambda k: real(x, k), T)
            root(4, T)
            input_hi(1, 2 * KT, ffn_h[0])
            ffn(1, START["ffn2"])
            act_e.wait_ge(chunk_done, START["rgx"])
            squares(5, acc, T)
            root(5, T)
            act_e.wait_ge(x_ready, 24)
            act_e.wait_ge(loaded_const, 16 * N_CONST)
            squares(6, lambda k: x[:, k, :], L)
            root(6, L)

            for n in range(RT):
                act_e.wait_ge(chunk_done, START["rgx"] + n + 1)
                A(rgx[:, n, :], ps[:, 4 + n % 2, 0:L], ACT.Copy).then_inc(in2_copied, 1)
            for d in range(2):
                w = L if d == 0 else T
                for g, buf in ((0, r_g), (1, i_g)):
                    for t in range(RT):
                        n = (2 * d + g) * RT + t
                        act_e.wait_ge(rg_gated, n + 1)
                        A(buf[d][:, t, :], ps[:, 4 + n % 2, 0:w], ACT.Sigmoid, bias=col("rg_gate_b_2", n)).then_inc(in2_copied, 1)
            for n in range(3):
                act_e.wait_ge(vt_turned, n + 1)
                A(vt[0:LT[n][1], n, :], ps[0:LT[n][1], n, :], ACT.Copy).then_inc(vt_ready, 1)
            act_e.wait_ge(sp_ready, 2)
            act_e.wait_ge(in2_copied, RT + 4 * RT)
            for d in range(2):
                for t in range(RT):
                    A(m_g[d][:, t, :], r_g[d][:, t, :], ACT.Tanh, scale=small[:, 160 + 8 * d + t:161 + 8 * d + t]).then_inc(rg_tanh, 1)
            act_e.wait_ge(rg_tanh, 2 * RT)
            for d in range(2):
                for t in range(RT):
                    A(r_g[d][:, t, :], r_g[d][:, t, :], ACT.Exp, scale=small[:, 176 + 8 * d + t:177 + 8 * d + t]).then_inc(decay_ready, 1)
            for n in range(RT):
                act_e.wait_ge(chunk_done, START["rgg"] + n + 1)
                A(gg[:, n, :], ps[:, 4 + n % 2, 0:T], ACT.Gelu_apprx_tanh).then_inc(in2_copied, 1)
            for d in range(2):
                act_e.wait_ge(rg_den, d + 1)
                A(m_g[d][:, :, :], m_g[d][:, :, :], ACT.Sqrt).then_inc(rg_sqrt, 1)
            for n in range(16):
                act_e.wait_ge(chunk_done, START["gl"] + n + 1)
                A(sgl[:, n, :], ps[:, 4 + n % 2, 0:T], ACT.Sigmoid, bias=col("b_gate_2", n)).then_inc(in2_copied, 1)

            act_e.wait_ge(x_ready, 32)
            squares(7, lambda k: real(x, k), T)
            root(7, T)
            act_e.wait_ge(ssq_ready, 8)
            input_hi(2, 4 * KT, peer_h[0])
            for n in range(16):
                act_e.wait_ge(chunk_done, START["wq"] + n + 1)
                A(pq[:, n, :], ps[:, 4 + n % 2, 0:T], ACT.Copy).then_inc(pq_copied, 1)
            for b in range(8):
                act_e.wait_ge(sc_out, b + 1)
                A(sc[:, b // 4, 4 * (b % 4):4 * (b % 4) + 4, :].rearrange("p a b -> p (a b)"), ps[:, b, :], ACT.Copy).then_inc(sc_copied, 1)
            act_e.wait_ge(cv_ready, 2)
            A(ew[:, 2, :, :], ew[:, 2, :, :], ACT.Exp).then_inc(ce_ready, 1)

            base = START["experts"]

            def expert_hi(r, i=None):
                n = 16 * (r // NX + 1)
                act_e.wait_ge(expert_landed[r % NX], n if i is None else i * 64 + n)
                n = base + max(0, r - NW + 1)
                act_e.wait_ge(chunk_done, n if i is None else i * 12 + n)
                A(peer_w[r % NW][0], ring[:, r % NX, :], ACT.Copy).then_inc(hi_ready, 1)

            for r in range(NW):
                expert_hi(r)

            def gate_out(q, done, bank):
                act_e.wait_ge(g_token, done)
                A(gates_all[:, :, q], ps[:, bank, :].rearrange("p (t e) -> p e t", t=4), ACT.Copy).then_inc(g_copied, 1)

            act_e.wait_ge(ewt_ready, 3)
            with act_e.Fori(0, T // 8) as i:
                for m in range(2):
                    gate_out(bass.ds(i * 8 + 4 * m, 4), i * 8 + (4 * m + 4), 4 + m)

            def expert(done, buf):
                act_e.wait_ge(chunk_done, done)
                A(ge_p[:, buf, :], ps[:, 4 + buf, 0:T], ACT.Gelu_apprx_tanh).then_inc(gelu_ready, 1)

            expert(base + 1, 0)
            expert_hi(3)
            expert(base + 2, 1)
            with act_e.Fori(0, (NK - 2) // 6) as i:
                for m in range(2, 8):
                    expert_hi(2 * m, i)
                    expert_hi(2 * m + 1, i)
                    act_e.wait_ge(peer_act, i * 6 + (m - 1))
                    expert(i * 12 + (base + 2 * m), m % 2)
            act_e.wait_ge(x_ready, 40)
            squares(8, lambda k: real(x, k), T)
            root(8, T)

        @block.vector
        def _(dve):
            steps = [0]
            V = nc.vector

            def link(ins):
                steps[0] += 1
                ins.then_inc(dve_step, 1)
                dve.wait_ge(dve_step, steps[0])

            def mean_square(n, w, width=D, half=False):
                dve.wait_ge(ssq_ready, n + 1)
                f = 4.0 if half else 1.0
                V.tensor_scalar(var[:, 0:w], ps[:, 6, 0:w], f / width, f * EPS, ALU.mult, ALU.add).then_inc(var_ready, 1)
                dve.wait_ge(std_ready, n + 1)
                link(V.reciprocal(rstd[:, 0:w], std[:, 0:w]))

            def norm_in(n, name, src, dst, w):
                mean_square(n, w)
                for k in range(KT):
                    V.scalar_tensor_tensor(dst(k), src(k), col(name, k), rstd[:, 0:w], ALU.mult, ALU.mult).then_inc(h_ready, 1)

            def norm_out(n, name, half):
                mean_square(n, T, half=half)
                for k in range(KT):
                    link(V.scalar_tensor_tensor(h[:, k, 0:T], acc(k), col(name, k), rstd[:, 0:T], ALU.mult, ALU.mult))
                    V.tensor_tensor(real(x, k), real(x, k), h[:, k, 0:T], ALU.add).then_inc(x_ready, 1)

            def reduce_angle(a, q):
                link(V.tensor_scalar(q, a, 1.0 / TWO_PI, ROUND, ALU.mult, ALU.add))
                link(V.tensor_scalar(q, q, -ROUND, None, ALU.add))
                link(V.scalar_tensor_tensor(a, q, -PI1, a, ALU.mult, ALU.add))
                link(V.scalar_tensor_tensor(a, q, -PI2, a, ALU.mult, ALU.add))
                link(V.scalar_tensor_tensor(a, q, -PI3, a, ALU.mult, ALU.add))
                return V.tensor_scalar(a, a, PI_IN, -PI_IN, ALU.min, ALU.max)

            def split_gated(buf, src, split, n):
                dve.wait_ge(act_gated, n)
                V.tensor_copy(split[0][:, buf, :], src[:, buf, :]).then_inc(act_hi, 1)
                dve.wait_ge(act_hi, n)
                return V.tensor_tensor(split[1][:, buf, :], src[:, buf, :], split[0][:, buf, :].bitcast(F32), ALU.subtract)

            def input_lo(n, split):
                for k in range(KT):
                    dve.wait_ge(h_hi, n * KT + k + 1)
                    V.tensor_tensor(split[1][:, k, :], real(h, k), split[0][:, k, :].bitcast(F32), ALU.subtract).then_inc(h_lo, 1)

            def down_lo(r, done, slot, split):
                dve.wait_ge(hi_ready, done)
                V.tensor_tensor(split[r % NW][1], ring[:, slot, :], split[r % NW][0].bitcast(F32), ALU.subtract).then_inc(lo_down, 1)

            dve.wait_ge(loaded_const, 16 * N_CONST)
            dve.wait_ge(loaded_x, 16)
            norm_in(0, NORMS[0], lambda k: real(x, k), lambda k: real(h, k), T)
            input_lo(0, ffn_h)
            link(V.tensor_copy(ang, posi.bitcast(I32)))
            link(V.tensor_scalar(ang, ang, col("rope_inv"), None, ALU.mult))
            link(reduce_angle(ang, angq))
            link(V.scalar_tensor_tensor(angq, ang, -1.0, ang, ALU.mult, ALU.min))
            link(V.tensor_scalar(angq, angq, math.pi / 2, None, ALU.add))
            V.tensor_scalar(ang, ang, col("rope_sign"), None, ALU.mult).then_inc(rope_arg, 2)
            for layer, b in enumerate(("hy_b1_2", "hy_b2_2")):
                dve.wait_ge(flt_pe, layer + 1)
                at = COL["hy_freq_2"] + layer
                link(V.tensor_scalar(arg[0:FW, :], ps[0:FW, 5, 0:L], cols[0:FW, COL[b]:COL[b] + 1], cols[0:FW, at:at + 1], ALU.add, ALU.mult))
                reduce_angle(arg[0:FW, :], turn[0:FW, :]).then_inc(flt_arg, 1)
            for n, (t0, tn) in enumerate(LT):
                dve.wait_ge(flt_pe, 3 + n)
                for d in range(2):
                    link(V.tensor_tensor(kfb[0:tn, d, :], ps[0:tn, 4 + d, :], decay[0:tn, n, d, :], ALU.mult))
                V.tensor_tensor(ksum[0:tn, n, :], kfb[0:tn, 0, :], kfb[0:tn, 1, :], ALU.add).then_inc(flt_k, 1)
                V.tensor_tensor(kdif[0:tn, n, :], kfb[0:tn, 0, :], kfb[0:tn, 1, :], ALU.subtract).then_inc(flt_k, 1)
                dve.wait_ge(flt_k, 2 * n + 2)
            for n, (f0, fn) in enumerate(LT):
                dve.wait_ge(flt_pe, 6 + n)
                V.tensor_copy(kre[0:fn, n, :], ps[0:fn, 4, :]).then_inc(flt_k, 1)
                V.tensor_copy(kim[0:fn, n, :], ps[0:fn, 5, :]).then_inc(flt_k, 1)
            for n in (1, 2):
                V.tensor_tensor(small[:, n - 1:n], col(f"lambda_q{n}"), col(f"lambda_k{n}"), ALU.mult).then_inc(lam_prod, 1)
            lam = cols[:, COL["rg_lambda_2"]:COL["rg_lambda_2"] + 16]
            V.scalar_tensor_tensor(small[:, 32:48], lam, -1.0, lam, ALU.mult, ALU.max).then_inc(lam_e, 1)
            dve.wait_ge(lam_exp, 2)
            link(V.tensor_tensor(small[:, 6:7], small[:, 5:6], small[:, 4:5], ALU.subtract))
            link(V.tensor_scalar(small[:, 7:8], small[:, 6:7], -LAMBDA_INIT, None, ALU.add))
            e, w, w2s, pl = small[:, 16:32], small[:, 112:128], small[:, 128:144], small[:, 144:160]
            link(V.tensor_scalar(w, e, 2.0, None, ALU.add))
            link(V.reciprocal(w, w))
            link(V.tensor_tensor(w, w, e, ALU.mult))
            link(V.tensor_tensor(w2s, w, w, ALU.mult))
            link(V.tensor_scalar(pl, w2s, 1.0 / 17, 1.0 / 15, ALU.mult, ALU.add))
            for odd in (13, 11, 9, 7, 5, 3, 1):
                link(V.tensor_tensor(pl, pl, w2s, ALU.mult))
                link(V.tensor_scalar(pl, pl, 1.0 / odd, None, ALU.add))
            link(V.tensor_tensor(pl, pl, w, ALU.mult))
            link(V.tensor_scalar(w, lam, -1.0, 0.0, ALU.mult, ALU.max))
            link(V.scalar_tensor_tensor(pl, pl, 2.0, w, ALU.mult, ALU.add))
            V.tensor_scalar(small[:, 160:176], pl, RG_C, None, ALU.mult).then_inc(sp_ready, 1)
            V.tensor_scalar(small[:, 176:192], pl, -RG_C, None, ALU.mult).then_inc(sp_ready, 1)

            def ffn(f, base):
                hi = f * 3 * FT + 1

                def one(n, buf):
                    dve.wait_ge(silu_ready, n)
                    V.tensor_tensor(act[:, buf, :], silu[:, buf, :], ps[:, 4 + buf, T:2 * T], ALU.mult).then_inc(act_gated, 1)
                    split_gated(buf, act, ffn_act, n).then_inc(act_ready, 1)

                one(f * FT + 1, 0)
                down_lo(4, hi + 4, (base + 4) % NS, ffn_w)
                one(f * FT + 2, 1)
                with dve.Fori(0, (FT - 2) // 2) as i:
                    for m in (2, 3):
                        r = 3 * m + 1
                        down_lo(r, i * 6 + (hi + r), (base + r) % NS, ffn_w)
                        dve.wait_ge(chunk_done, i * 6 + (base + 3 * m - 1))
                        one(i * 2 + (f * FT + m + 1), m % 2)
                r = 3 * FT - 1
                down_lo(r, hi + r, (base + r) % NS, ffn_w)

            ffn(0, START["ffn1"])
            norm_out(1, NORMS[1], True)
            norm_in(2, NORMS[2], lambda k: real(x, k), lambda k: real(h, k), T)
            dve.wait_ge(rope_sin, 2)
            for n in range(28):
                dve.wait_ge(swapped, n + 1)
                link(V.tensor_tensor(rot[:, 0, :], ps[:, 6 + n % 2, 0:T], rope_s, ALU.mult))
                link(V.tensor_tensor(rot[:, 1, :], raw[:, n % 2, :], rope_c, ALU.mult))
                V.tensor_tensor(qk[:, n, :], rot[:, 0, :], rot[:, 1, :], ALU.add).then_inc(qk_ready, 1)
                dve.wait_ge(qk_ready, n + 1)
            dve.wait_ge(chunk_done, START["gates"])
            for b in range(4):
                c0, cn = (b % 2) * 512, (512, 256)[b % 2]
                V.tensor_copy(vd[:, b // 2, c0:c0 + cn], ps[:, 4 + b, 0:cn]).then_inc(v_copied, 1)

            def da_max(hd):
                dve.wait_ge(da_scores, hd + 1)
                o = 8 * (hd % 2)
                link(V.tensor_reduce(small[:, 48 + o:52 + o], ps[:, 2 * (hd % 2):2 * (hd % 2) + 2, :].rearrange("p c (q k) -> p c q k", q=2), AX.X, ALU.max, negate=True))
                V.tensor_scalar(small[:, 64 + o:68 + o], small[:, 48 + o:52 + o], DH ** -0.5, None, ALU.mult).then_inc(da_nbias, 1)

            def da_mix(hd):
                dve.wait_ge(da_exp, 4 * (hd + 1))
                o = 80 + 8 * (hd % 2)
                link(V.reciprocal(small[:, o:o + 4], small[:, o:o + 4]))
                link(V.tensor_scalar(small[:, o + 2:o + 4], small[:, o + 2:o + 4], small[:, 7:8], None, ALU.mult))
                if hd >= 2:
                    dve.wait_ge(da_turned, hd - 1)
                for q in range(2):
                    link(V.tensor_scalar(da_t[:, q, :], da_p[:, hd % 2, 2 + q, :], small[:, o + 2 + q:o + 3 + q], None, ALU.mult))
                    V.scalar_tensor_tensor(da_a[:, hd % 2, q, :], da_p[:, hd % 2, q, :], small[:, o + q:o + q + 1], da_t[:, q, :], ALU.mult, ALU.add).then_inc(da_mixed, 1)

            def da_take(hd):
                dve.wait_ge(da_out, hd + 1)
                V.tensor_copy(ot[:, hd, :], ps[:, 7, 0:T]).then_inc(ot_ready, 1)

            da_max(0)
            for hd in range(DA_H):
                if hd + 1 < DA_H:
                    da_max(hd + 1)
                da_mix(hd)
                if hd:
                    da_take(hd - 1)
            da_take(DA_H - 1)
            dve.wait_ge(da_mixed, 2 * DA_H)
            dve.wait_ge(loaded_mask, 16)
            for j in range(DIL_H):
                dve.wait_ge(dl_scores, j + 1)
                if j:
                    dve.wait_ge(dl_turned, j)
                for g in range(3):
                    link(V.tensor_tensor(dl_p[:, g, :, :], ps[:, g, :].rearrange("p (q k) -> p q k", q=2), mask[:, g, :, :], ALU.add))
                for q in range(2):
                    link(V.tensor_reduce(small[:, 98 + q:99 + q], dl_p[:, :, q, :], AX.XY, ALU.max, negate=True))
                V.tensor_scalar(small[:, 100:102], small[:, 98:100], DH ** -0.5, None, ALU.mult).then_inc(dl_nbias, 1)
                dve.wait_ge(dl_exp, 2 * (j + 1))
                link(V.reciprocal(small[:, 106:108], small[:, 104:106]))
                for q in range(2):
                    V.tensor_scalar(dl_p[:, :, q, :], dl_p[:, :, q, :], small[:, 106 + q:107 + q], None, ALU.mult).then_inc(dl_prob, 1)
                dve.wait_ge(dl_out, j + 1)
                r0 = DH * (j % 2)
                V.tensor_copy(odt[r0:r0 + DH, j // 2, :], ps[r0:r0 + DH, 7, 0:T]).then_inc(od_ready, 1)
            dve.wait_ge(sub_sum, 1)
            f = (1.0 - LAMBDA_INIT) ** -2
            V.tensor_scalar(srstd[:, :, :], ps[:, 0:4, :].rearrange("p b (n t) -> p (b n) t", t=T), f / P, f * EPS, ALU.mult, ALU.add).then_inc(sub_var, 1)
            dve.wait_ge(sub_std, 1)
            link(V.reciprocal(srstd[:, :, :], srstd[:, :, :]))
            for hd in range(DA_H):
                V.scalar_tensor_tensor(oa[:, hd, :], ot[:, hd, :], col("g_subln"), srstd[:, hd, :], ALU.mult, ALU.mult).then_inc(oa_ready, 1)
            dve.wait_ge(sg_ready, 1)
            dve.wait_ge(chunk_done, START["proj_a"])
            for n in range(KT):
                dve.wait_ge(chunk_done, START["proj_a"] + n + 1)
                link(V.tensor_tensor(rot[:, 0, :], acc(n), sg[:, 8 + n, :], ALU.mult))
                link(V.tensor_tensor(rot[:, 1, :], ps[:, 4 + n % 2, 0:T], sg[:, n, :], ALU.mult))
                V.tensor_tensor(merged[:, n, :], rot[:, 0, :], rot[:, 1, :], ALU.add).then_inc(merged_ready, 1)
                dve.wait_ge(merged_ready, n + 1)
            norm_out(3, NORMS[3], False)
            norm_in(4, NORMS[4], lambda k: real(x, k), lambda k: real(h, k), T)
            input_lo(1, ffn_h)
            ffn(1, START["ffn2"])
            norm_out(5, NORMS[5], True)
            norm_in(6, NORMS[6], lambda k: x[:, k, :], lambda k: h[:, k, :], L)

            for n in range(RT):
                dve.wait_ge(in2_copied, n + 1)
                for d in range(2):
                    w = [col("rg_conv_w_2", (4 * d + j) * RT + n) for j in range(4)]
                    dst = xc[d][:, n, :]
                    src = rgx[:, n, :] if d == 0 else rgx[:, n, NM:L]
                    link(V.tensor_scalar(dst, src, w[0], col("rg_conv_b_2", d * RT + n), ALU.mult, ALU.add))
                    for j in range(1, 4):
                        if d == 0:
                            link(V.scalar_tensor_tensor(dst[:, j:L], rgx[:, n, 0:L - j], w[j], dst[:, j:L], ALU.mult, ALU.add))
                        else:
                            ins = V.scalar_tensor_tensor(dst[:, 0:T - j], rgx[:, n, NM + j:L], w[j], dst[:, 0:T - j], ALU.mult, ALU.add)
                            if j < 3:
                                link(ins)
                ins.then_inc(rg_conv, 1)
            for n in range(12):
                dve.wait_ge(chunk_done, START["hyena"] + n + 1)
                src = ps[:, 4 + n % 2, :]
                part = (2, 1, 0)[n // 4] * HYT + n % 4
                w = [col("hy_conv_w_2", j * 12 + part) for j in range(3)]
                link(V.tensor_scalar(hu[:, n, :], src[:, 0:L], w[1], col("hy_conv_b_2", part), ALU.mult, ALU.add))
                link(V.scalar_tensor_tensor(hu[:, n, 1:L], src[:, 0:L - 1], w[0], hu[:, n, 1:L], ALU.mult, ALU.add))
                V.scalar_tensor_tensor(hu[:, n, 0:L - 1], src[:, 1:L], w[2], hu[:, n, 0:L - 1], ALU.mult, ALU.add).then_inc(hy_conv, 1)
            dve.wait_ge(hy_conv, 12)
            for c in range(HYT):
                V.tensor_tensor(hu[:, c, :], hu[:, c, :], hu[:, 4 + c, :], ALU.mult).then_inc(vx_ready, 1)
            for d in range(2):
                dve.wait_ge(rg_tanh, RT * (d + 1))
                den = i_tmp(d)
                link(V.tensor_scalar(den, m_g[d][:, :, :], 1.0, None, ALU.add))
                link(V.reciprocal(den, den))
                V.scalar_tensor_tensor(m_g[d][:, :, :], m_g[d][:, :, :], 2.0, den, ALU.mult, ALU.mult).then_inc(rg_den, 1)
                dve.wait_ge(rg_den, d + 1)
            dve.wait_ge(decay_ready, 2 * RT)
            for d in range(2):
                dve.wait_ge(rg_sqrt, d + 1)
                f0 = 0 if d == 0 else T - 1
                link(V.memset(m_g[d][:, :, f0:f0 + 1], 1.0))
                link(V.tensor_tensor(i_g[d][:, :, :], i_g[d][:, :, :], xc[d][:, :, :], ALU.mult))
                link(V.tensor_tensor(i_g[d][:, :, :], i_g[d][:, :, :], m_g[d][:, :, :], ALU.mult))
                for t in range(RT):
                    a, b, o = r_g[d][:, t, :], i_g[d][:, t, :], m_g[d][:, t, :]
                    if d:
                        a, b, o = a[:, ::-1], b[:, ::-1], o[:, ::-1]
                    link(V.tensor_tensor_scan(o, a, b, 0.0, ALU.mult, ALU.add))
            link(V.tensor_tensor(m_g[1][:, :, :], m_g[1][:, :, :], m_g[0][:, :, NM:L], ALU.add))
            dve.wait_ge(in2_copied, RT + 4 * RT + RT)
            V.tensor_tensor(gg[:, :, :], gg[:, :, :], m_g[1][:, :, :], ALU.mult).then_inc(rg_ready, 1)
            for n, (f0, fn) in enumerate(LT):
                dve.wait_ge(spec_ready, n + 1)
                ure, uim = ps[0:fn, 0, :], ps[0:fn, 1, :]
                link(V.tensor_tensor(ys[0:fn, n, 0, :], ure, kre[0:fn, n, :], ALU.mult))
                link(V.tensor_tensor(ys[0:fn, n, 1, :], ure, kim[0:fn, n, :], ALU.mult))
                link(V.tensor_tensor(tmp_spec(fn, 0), uim, kim[0:fn, n, :], ALU.mult))
                link(V.tensor_tensor(tmp_spec(fn, 1), uim, kre[0:fn, n, :], ALU.mult))
                V.tensor_tensor(ys[0:fn, n, 0, :], ys[0:fn, n, 0, :], tmp_spec(fn, 0), ALU.subtract).then_inc(ys_ready, 1)
                V.tensor_tensor(ys[0:fn, n, 1, :], ys[0:fn, n, 1, :], tmp_spec(fn, 1), ALU.add).then_inc(ys_ready, 1)
                dve.wait_ge(ys_ready, 2 * n + 2)
            for c in range(HYT):
                dve.wait_ge(conv_out, c + 1)
                link(V.scalar_tensor_tensor(hu[:, 4 + c, 0:T], hu[:, c, NM:L], col("hy_skip_2", c), ps[:, 2 + c % 2, 0:T], ALU.mult, ALU.add))
                V.tensor_tensor(hu[:, 4 + c, 0:T], hu[:, 4 + c, 0:T], hu[:, 8 + c, NM:L], ALU.mult).then_inc(hy_ready, 1)
            dve.wait_ge(in2_copied, RT + 4 * RT + RT + 16)
            for n in range(KT):
                dve.wait_ge(chunk_done, START["rgout"] + n + 1)
                link(V.tensor_tensor(tmp_mix(0), acc(n), sgl[:, n, :], ALU.mult))
                link(V.tensor_tensor(tmp_mix(1), ps[:, 4 + n % 2, 0:T], sgl[:, 8 + n, :], ALU.mult))
                V.tensor_tensor(merged2[:, n, :], tmp_mix(0), tmp_mix(1), ALU.add).then_inc(merged2_ready, 1)
                dve.wait_ge(merged2_ready, n + 1)
            for n in range(KT):
                dve.wait_ge(chunk_done, START["out2"] + n + 1)
                V.tensor_tensor(real(x, n), real(x, n), ps[:, 4 + n % 2, 0:T], ALU.add).then_inc(x_ready, 1)
            dve.wait_ge(x_ready, 32)

            norm_in(7, NORMS[7], lambda k: real(x, k), lambda k: real(h, k), T)
            tiu = ti.bitcast(U32)
            ciu = ci.bitcast(U32)

            def top16(vals, idx, src, scratch):
                link(V.max(vals[:, 0:8], src))
                V.max_index(idx[:, 0:8], vals[:, 0:8], src)
                link(V.match_replace(scratch, vals[:, 0:8], src, -3.0e38))
                link(V.max(vals[:, 8:16], scratch))
                link(V.max_index(idx[:, 8:16], vals[:, 8:16], scratch))

            for t in range(2):
                for n in range(16):
                    if n % 4 == 0:
                        dve.wait_ge(sc_copied, 4 * t + n // 4 + 1)
                    top16(tv[:, t, n, :], tiu[:, t, n, :], sc[:, t, n, :], scr[:, 0:NK])
                link(V.tensor_copy(tif[:, t, :, :], tiu[:, t, :, :]))
                pair = tv[:, t, :, :].rearrange("p (h c) k -> p h c k", c=2)
                link(V.tensor_tensor(cand[:, t, :, :].rearrange("p h (i j) -> p h i j", i=TOPK),
                                     pair[:, :, 0, :].unsqueeze(3).to_broadcast([P, PH, TOPK, TOPK]),
                                     pair[:, :, 1, :].unsqueeze(2).to_broadcast([P, PH, TOPK, TOPK]), ALU.add))
                for n in range(PH):
                    top16(cv[:, t, n, :], ciu[:, t, n, :], cand[:, t, n, :], scr)
                V.tensor_tensor(ew[:, 2, t, :].rearrange("p (h k) -> p h k", k=TOPK), cv[:, t, :, :],
                                cv[:, t, :, 0:1].to_broadcast([P, PH, TOPK]), ALU.subtract).then_inc(cv_ready, 1)
            dve.wait_ge(iota_ready, 3)
            cijb = cij.bitcast(U32)
            for t in range(2):
                flat = ciu[:, t, :, :].rearrange("p h k -> p (h k)")
                link(V.tensor_scalar(cijb[:, t, 0, :], flat, 4, None, ALU.logical_shift_right))
                link(V.tensor_scalar(cijb[:, t, 1, :], flat, 15, None, ALU.bitwise_and))
                link(V.tensor_copy(cijf[:, t, :, :], cijb[:, t, :, :]))
                for c in range(2):
                    link(V.tensor_tensor(hot, cijf[:, t, c, :].unsqueeze(2).to_broadcast([P, PH * TOPK, TOPK]),
                                         io16.unsqueeze(1).to_broadcast([P, PH * TOPK, TOPK]), ALU.is_equal))
                    keyf = tif[:, t, :, :].rearrange("p (h c) k -> p h c k", c=2)[:, :, c, :]
                    link(V.tensor_tensor(hot.rearrange("p (h k) i -> p h k i", k=TOPK), hot.rearrange("p (h k) i -> p h k i", k=TOPK),
                                         keyf.unsqueeze(2).to_broadcast([P, PH, TOPK, TOPK]), ALU.mult))
                    link(V.tensor_reduce(ew[:, c, t, :], hot, AX.X, ALU.add))
            dve.wait_ge(ce_ready, 1)
            wts = ew[:, 2, :, :].rearrange("p t (h k) -> p (t h) k", k=TOPK)
            link(V.tensor_reduce(small[:, 208:224], wts, AX.X, ALU.add))
            link(V.reciprocal(small[:, 208:224], small[:, 208:224]))
            V.tensor_tensor(wts, wts, small[:, 208:224].unsqueeze(2).to_broadcast([P, 2 * PH, TOPK]), ALU.mult).then_inc(ew_ready, 1)
            for n, dst in enumerate((e1t, e2t, gt)):
                dve.wait_ge(ew_turned, n + 1)
                V.tensor_copy(dst, ps[:, 4 + n, 0:T]).then_inc(ewt_ready, 1)
            dve.wait_ge(ewt_ready, 3)
            def rows(m, e1, e2, g):
                V.tensor_scalar(sel_b[:, m, :], iota, e2, None, ALU.is_equal)
                V.tensor_scalar(sel_a[:, m, :], iota, e1, g, ALU.is_equal, ALU.mult).then_inc(ab_ready, 1)

            for m in range(8):
                rows(m, e1t[:, m:m + 1], e2t[:, m:m + 1], gt[:, m:m + 1])
            with dve.Fori(1, T // 8) as i:
                for m in range(8):
                    dve.wait_ge(g_token, i * 8 + (m - 7))
                    t = bass.ds(i * 8 + m, 1)
                    rows(m, e1t[:, t], e2t[:, t], gt[:, t])
            base = START["experts"]
            dve.wait_ge(g_copied, T // 4)

            def expert(e, n, buf):
                dve.wait_ge(gelu_ready, n)
                V.tensor_tensor(act_p[:, buf, :], ge_p[:, buf, :], e, ALU.mult).then_inc(act_gated, 1)
                split_gated(buf, act_p, peer_part, n + 2 * FT).then_inc(peer_act, 1)

            def expert_lo(r, i=None):
                down_lo(r, HI_EXPERTS + r + 1 if i is None else i * 12 + (HI_EXPERTS + r + 1), r % NX, peer_w)

            expert(gates_all[:, 0, :], 1, 0)
            expert_lo(2)
            expert(gates_all[:, 1, :], 2, 1)
            with dve.Fori(0, (NK - 2) // 6) as i:
                for m in range(2, 8):
                    expert_lo(2 * m, i)
                    dve.wait_ge(chunk_done, i * 12 + (base + 2 * m - 1))
                    expert(gates_all[:, bass.ds(i * 6 + m, 1), :].rearrange("p a t -> p (a t)"), i * 6 + (m + 1), m % 2)
            expert_lo(2 * NK - 1)
            dve.wait_ge(chunk_done, N_CHUNKS)
            for n in range(KT):
                V.tensor_tensor(real(x, n), real(x, n), acc(n), ALU.add).then_inc(x_ready, 1)
            dve.wait_ge(x_ready, 40)
            norm_in(8, NORMS[8], lambda k: real(x, k), lambda k: real(h, k), T)

        @block.tensor
        def _(pe):
            M = nc.tensor.matmul

            def land(c):
                pe.wait_ge(landed[c % NS], 16 * (c // NS + 1))

            def tile(c, out, rhs, nk=KT, slot_cols=0):
                land(c)
                for k in range(nk):
                    ins = M(out, ring[:, c % NS, slot_cols + k * P:slot_cols + (k + 1) * P], rhs(k), start=(k == 0), stop=(k == nk - 1))
                return ins

            def product(out, w, cols_at, act_hl, start, stop):
                hi, lo = w[0][:, cols_at:cols_at + P], w[1][:, cols_at:cols_at + P]
                M(out, hi, act_hl[0], start=start, stop=False, skip_group_check=True)
                M(out, hi, act_hl[1], start=False, stop=False, skip_group_check=True)
                return M(out, lo, act_hl[0], start=False, stop=stop, skip_group_check=True)

            def sums(n, w):
                if n:
                    pe.wait_ge(var_ready, n)
                for k in range(KT):
                    pe.wait_ge(sq_ready, KT * n + k + 1)
                    ins = M(ps[:, 6, 0:w], ones, sq[:, k, 0:w], start=(k == 0), stop=(k == KT - 1))
                ins.then_inc(ssq_ready, 1)

            pe.wait_ge(loaded_const, 16 * N_CONST)
            sums(0, T)
            pe.wait_ge(iota_ready, 1)
            M(ps[0:FW, 5, 0:L], w1[0:2 * HB + 1, :], zt[0:2 * HB + 1, :], start=True, stop=True).then_inc(flt_pe, 1)
            pe.wait_ge(flt_sin, 1)
            M(ps[0:FW, 5, 0:L], w2[0:FW, :], hdn[0:FW, :], start=True, stop=True).then_inc(flt_pe, 1)
            pe.wait_ge(flt_sin, 2)
            for n, (t0, tn) in enumerate(LT):
                if n:
                    pe.wait_ge(flt_k, 2 * n)
                for d in range(2):
                    ins = M(ps[0:tn, 4 + d, :], hdn[0:FW + 1, t0:t0 + tn], w3[0:FW + 1, d * HY:(d + 1) * HY], start=True, stop=True)
                ins.then_inc(flt_pe, 1)
            pe.wait_ge(flt_k, 6)
            for n, (f0, fn) in enumerate(LT):
                if n:
                    pe.wait_ge(flt_k, 6 + 2 * n)
                for d, src in ((0, ksum), (1, kdif)):
                    for m, (t0, tn) in enumerate(LT):
                        ins = M(ps[0:fn, 4 + d, :], dft[0:tn, m, d, f0:f0 + fn], src[0:tn, m, :], start=(m == 0), stop=(m == 2))
                ins.then_inc(flt_pe, 1)
            pe.wait_ge(flt_k, 12)
            pe.wait_ge(lam_prod, 2)
            M(ps[:, 7, 0:2], ones, small[:, 0:2], start=True, stop=True).then_inc(lam_sum, 1)

            def ffn(f, base):
                def first(j, buf, i=None):
                    r = ffn_up(0, j) - 1
                    for half in range(2):
                        n = f * 2 * FT + 2 * j + half + 1
                        pe.wait_ge(lo_up, n if i is None else i * 4 + n)
                        for k in range(KT):
                            if j == 0 and half == 0:
                                pe.wait_ge(h_lo, f * KT + k + 1)
                            ins = product(ps[:, 4 + buf, half * T:(half + 1) * T], ffn_w[(r + half) % NW], k * P, (ffn_h[0][:, k, :], ffn_h[1][:, k, :]), k == 0, k == KT - 1)
                        ins.then_inc(chunk_done, 1)

                def second(j, buf, begin, end, i=None):
                    r = ffn_down(0, j)
                    n = f * FT + j + 1
                    pe.wait_ge(lo_down, n if i is None else i * 2 + n)
                    for t in range(KT):
                        ins = product(acc(t), ffn_w[r % NW], t * P, (ffn_act[0][:, buf, :], ffn_act[1][:, buf, :]), begin and t % 2 == 0, end)
                    ins.then_inc(chunk_done, 1)

                first(0, 0)
                first(1, 1)
                pe.wait_ge(act_ready, f * FT + 1)
                second(0, 0, True, False)
                with pe.Fori(0, (FT - 2) // 2) as i:
                    for m in (2, 3):
                        pe.wait_ge(act_ready, i * 2 + (f * FT + m - 1))
                        first(m, m % 2, i)
                        pe.wait_ge(act_ready, i * 2 + (f * FT + m))
                        second(m - 1, (m - 1) % 2, False, False, i)
                pe.wait_ge(act_ready, f * FT + FT)
                second(FT - 1, (FT - 1) % 2, False, True)

            ffn(0, START["ffn1"])
            sums(1, T)
            sums(2, T)
            pe.wait_ge(h_ready, 16)

            def swap_tile(n):
                pe.wait_ge(raw_copied, n + 1)
                if n >= 2:
                    pe.wait_ge(qk_ready, n - 1)
                if n == 0:
                    pe.wait_ge(var_ready, 3)
                M(ps[:, 6 + n % 2, 0:T], swap, raw[:, n % 2, :], start=True, stop=True).then_inc(swapped, 1)

            for n in range(28):
                if n >= 2:
                    pe.wait_ge(raw_copied, n - 1)
                tile(START["qk"] + n, ps[:, 4 + n % 2, 0:T], lambda k: real(h, k)).then_inc(chunk_done, 1)
                if n:
                    swap_tile(n - 1)
            swap_tile(27)
            for name, width, b0 in (("va", D, 0), ("vd", 3 * DIL_H * DH, 4)):
                if b0:
                    pe.wait_ge(qk_ready, 28)
                for k in range(KT):
                    c = START[name] + k
                    land(c)
                    for t in range(2):
                        for n in range(2):
                            w = min(512, width - 512 * n)
                            ins = M(ps[:, b0 + 2 * t + n, 0:w], h[:, k, NM + t * P:NM + (t + 1) * P], ring[:, c % NS, n * 512:n * 512 + w], start=(k == 0), stop=(k == KT - 1))
                    ins.then_inc(chunk_done, 1)
            pe.wait_ge(v_copied, 8)

            def da_score(hd):
                if hd >= 2:
                    pe.wait_ge(da_exp, 4 * (hd - 1))
                for c in range(2):
                    r0 = DH * c
                    for q in range(2):
                        ins = M(ps[:, 2 * (hd % 2) + c, q * T:(q + 1) * T], qk[r0:r0 + DH, hd, q * P:(q + 1) * P], qk[r0:r0 + DH, 8 + hd, :], start=True, stop=True)
                ins.then_inc(da_scores, 1)

            def gate_tile(n):
                if n >= 2:
                    pe.wait_ge(gate_copied, n - 1)
                tile(START["gates"] + n, ps[:, 4 + n % 2, 0:T], lambda k: real(h, k)).then_inc(chunk_done, 1)

            da_score(0)
            for hd in range(DA_H):
                if hd + 1 < DA_H:
                    da_score(hd + 1)
                gate_tile(2 * hd)
                pe.wait_ge(da_mixed, 2 * (hd + 1))
                if hd:
                    pe.wait_ge(da_tcopied, hd)
                for kt in range(2):
                    for q in range(2):
                        ins = nc.tensor.transpose(ps[:, 6, kt * T + q * P:kt * T + (q + 1) * P], da_a[:, hd % 2, q, kt * P:(kt + 1) * P], ident)
                ins.then_inc(da_turned, 1)
                gate_tile(2 * hd + 1)
                pe.wait_ge(da_tcopied, hd + 1)
                if hd:
                    pe.wait_ge(ot_ready, hd)
                for kt in range(2):
                    ins = M(ps[:, 7, 0:T], va[:, kt, hd * P:(hd + 1) * P], da_at[:, hd % 2, kt * T:(kt + 1) * T], start=(kt == 0), stop=(kt == 1))
                ins.then_inc(da_out, 1)
            pe.wait_ge(gate_copied, 16)
            pe.wait_ge(ot_ready, DA_H)
            for j in range(DIL_H):
                r0 = DH * (j % 2)
                if j:
                    pe.wait_ge(dl_nbias, j)
                for g in range(3):
                    n = (DIL_H * g + j) // 2
                    for q in range(2):
                        ins = M(ps[:, g, q * T:(q + 1) * T], qk[r0:r0 + DH, 16 + n, q * P:(q + 1) * P], qk[r0:r0 + DH, 22 + n, :], start=True, stop=True)
                ins.then_inc(dl_scores, 1)
                pe.wait_ge(dl_prob, 2 * (j + 1))
                if j:
                    pe.wait_ge(dl_tcopied, j)
                for g in range(3):
                    for kt in range(2):
                        for q in range(2):
                            ins = nc.tensor.transpose(ps[:, 3 + g, kt * T + q * P:kt * T + (q + 1) * P], dl_p[:, g, q, kt * P:(kt + 1) * P], ident)
                ins.then_inc(dl_turned, 1)
                pe.wait_ge(dl_tcopied, j + 1)
                if j:
                    pe.wait_ge(od_ready, j)
                for n in range(6):
                    g, kt = n // 2, n % 2
                    at = (DIL_H * g + j) * DH
                    ins = M(ps[r0:r0 + DH, 7, 0:T], vd[:, kt, at:at + DH], dl_pt[:, g, kt, :], start=(n == 0), stop=(n == 5))
                ins.then_inc(dl_out, 1)
            for hd in range(DA_H):
                pe.wait_ge(sub_sq, hd + 1)
                ins = M(acc(hd), ones, sq[:, hd, 0:T], start=True, stop=True)
            ins.then_inc(sub_sum, 1)
            pe.wait_ge(od_ready, DIL_H)
            pe.wait_ge(sub_var, 1)
            for n in range(KT):
                c = START["proj_b"] + n // 4
                ins = tile(c, acc(n), lambda k: odt[:, k, :], nk=2, slot_cols=(n % 4) * 2 * P)
                if n % 4 == 3:
                    ins.then_inc(chunk_done, 1)
            pe.wait_ge(oa_ready, DA_H)
            for n in range(KT):
                if n >= 2:
                    pe.wait_ge(merged_ready, n - 1)
                tile(START["proj_a"] + n, ps[:, 4 + n % 2, 0:T], lambda k: oa[:, k, :]).then_inc(chunk_done, 1)
            pe.wait_ge(merged_ready, KT)
            for n in range(KT):
                tile(START["out1"] + n, acc(n), lambda k: merged[:, k, :]).then_inc(chunk_done, 1)
            sums(3, T)
            sums(4, T)
            ffn(1, START["ffn2"])
            sums(5, T)
            sums(6, L)

            pe.wait_ge(h_ready, 32)
            for n in range(RT):
                if n >= 2:
                    pe.wait_ge(in2_copied, n - 1)
                tile(START["rgx"] + n, ps[:, 4 + n % 2, 0:L], lambda k: h[:, k, :]).then_inc(chunk_done, 1)
            pe.wait_ge(in2_copied, RT)
            for n in range(12):
                if n >= 2:
                    pe.wait_ge(hy_conv, n - 1)
                tile(START["hyena"] + n, ps[:, 4 + n % 2, 0:L], lambda k: h[:, k, :]).then_inc(chunk_done, 1)
            pe.wait_ge(rg_conv, RT)
            pe.wait_ge(hy_conv, 12)
            for d in range(2):
                w = L if d == 0 else T
                for g in range(2):
                    c = START["rggate"] + 2 * d + g
                    land(c)
                    for t in range(RT):
                        n = (2 * d + g) * RT + t
                        if n >= 2:
                            pe.wait_ge(in2_copied, RT + n - 1)
                        M(ps[:, 4 + n % 2, 0:w], ring[:, c % NS, t * P:(t + 1) * P], xc[d][:, t, :], start=True, stop=True).then_inc(rg_gated, 1)
                    pe.wait_ge(rg_gated, (2 * d + g + 1) * RT)
                    pe.sem_inc(chunk_done, 1)
            pe.wait_ge(vx_ready, HYT)
            for n, (t0, tn) in enumerate(LT):
                for c in range(HYT):
                    ins = nc.tensor.transpose(ps[0:tn, n, c * P:(c + 1) * P], hu[:, c, t0:t0 + tn], ident)
                ins.then_inc(vt_turned, 1)
            pe.wait_ge(in2_copied, 5 * RT)
            for n in range(RT):
                if n >= 2:
                    pe.wait_ge(in2_copied, 5 * RT + n - 1)
                tile(START["rgg"] + n, ps[:, 4 + n % 2, 0:T], lambda k: real(h, k)).then_inc(chunk_done, 1)
            pe.wait_ge(vt_ready, 3)
            for n, (f0, fn) in enumerate(LT):
                if n:
                    pe.wait_ge(ys_ready, 2 * n)
                for d in range(2):
                    for m, (t0, tn) in enumerate(LT):
                        ins = M(ps[0:fn, d, :], dft[0:tn, m, d, f0:f0 + fn], vt[0:tn, m, :], start=(m == 0), stop=(m == 2))
                ins.then_inc(spec_ready, 1)
                if n == 0:
                    for m in range(8):
                        gl_tile(pe, tile, m)
                else:
                    for m in range(8 + 4 * (n - 1), 8 + 4 * n):
                        gl_tile(pe, tile, m)
            pe.wait_ge(ys_ready, 6)
            for c in range(HYT):
                if c >= 2:
                    pe.wait_ge(hy_ready, c - 1)
                for n, (f0, fn) in enumerate(LT):
                    for d in range(2):
                        ins = M(ps[:, 2 + c % 2, 0:T], ys[0:fn, n, d, c * P:(c + 1) * P], idft[0:fn, n, d, :], start=(n == 0 and d == 0), stop=(n == 2 and d == 1))
                ins.then_inc(conv_out, 1)
            pe.wait_ge(hy_ready, HYT)
            for n in range(KT):
                ins = tile(START["hyout"] + n // 2, acc(n), lambda k: hu[:, 4 + k, 0:T], nk=4, slot_cols=(n % 2) * 4 * P)
                if n % 2:
                    ins.then_inc(chunk_done, 1)
            pe.wait_ge(rg_ready, 1)
            pe.wait_ge(in2_copied, 6 * RT + 16)
            for n in range(KT):
                if n >= 2:
                    pe.wait_ge(merged2_ready, n - 1)
                tile(START["rgout"] + n, ps[:, 4 + n % 2, 0:T], lambda k: gg[:, k, :]).then_inc(chunk_done, 1)
            pe.wait_ge(merged2_ready, KT)
            for n in range(KT):
                if n >= 2:
                    pe.wait_ge(x_ready, 24 + n - 1)
                tile(START["out2"] + n, ps[:, 4 + n % 2, 0:T], lambda k: merged2[:, k, :]).then_inc(chunk_done, 1)

            sums(7, T)
            pe.wait_ge(x_ready, 32)
            pe.wait_ge(h_ready, 40)
            for n in range(16):
                if n >= 2:
                    pe.wait_ge(pq_copied, n - 1)
                tile(START["wq"] + n, ps[:, 4 + n % 2, 0:T], lambda k: real(h, k)).then_inc(chunk_done, 1)
            pe.wait_ge(pq_copied, 16)
            pe.wait_ge(var_ready, 8)
            for t in range(2):
                for n in range(16):
                    c = START["keys"] + n // 8
                    land(c)
                    ins = M(ps[:, 4 * t + n // 4, (n % 4) * P:(n % 4 + 1) * P], pq[:, n, t * P:(t + 1) * P], ring[:, c % NS, (n % 8) * P:(n % 8 + 1) * P], start=True, stop=True)
                    if n % 4 == 3:
                        ins.then_inc(sc_out, 1)
            pe.wait_ge(sc_out, 8)
            pe.sem_inc(chunk_done, 2)
            pe.wait_ge(ew_ready, 1)
            pe.wait_ge(sc_copied, 8)
            for n in range(3):
                for t in range(2):
                    ins = nc.tensor.transpose(ps[:, 4 + n, t * P:(t + 1) * P], ew[:, n, t, :], ident)
                ins.then_inc(ew_turned, 1)
            pe.wait_ge(ewt_ready, 3)

            def token(ready, m):
                pe.wait_ge(ab_ready, ready)
                M(ps[:, 4 + m // 4, (m % 4) * P:(m % 4 + 1) * P], sel_b[:, m, :], sel_a[:, m, :], start=True, stop=True).then_inc(g_token, 1)

            for m in range(8):
                token(m + 1, m)
            with pe.Fori(1, T // 8) as i:
                for m in range(8):
                    if m % 4 == 0:
                        pe.wait_ge(g_copied, i * 2 + (m // 4 - 1))
                    token(i * 8 + (m + 1), m)
            pe.wait_ge(g_copied, T // 4)
            base = START["experts"]

            def first(e, buf, i=None):
                r = expert_u(0, e)
                n = UP_EXPERTS + e + 1
                pe.wait_ge(lo_up, n if i is None else i * 6 + n)
                for k in range(KT):
                    ins = product(ps[:, 4 + buf, 0:T], peer_w[r % NW], k * P, (peer_h[0][:, k, 0:T], peer_h[1][:, k, NM:L]), k == 0, k == KT - 1)
                ins.then_inc(chunk_done, 1)

            def second(e, buf, begin, end, i=None):
                r = expert_v(0, e)
                n = DOWN_EXPERTS + e + 1
                pe.wait_ge(lo_down, n if i is None else i * 6 + n)
                for t in range(KT):
                    ins = product(acc(t), peer_w[r % NW], t * P, (peer_part[0][:, buf, :], peer_part[1][:, buf, :]), begin and t % 2 == 0, end)
                ins.then_inc(chunk_done, 1)

            pe.wait_ge(h_lo, 3 * KT)
            first(0, 0)
            first(1, 1)
            pe.wait_ge(peer_act, 1)
            second(0, 0, True, False)
            with pe.Fori(0, (NK - 2) // 6) as i:
                for m in range(2, 8):
                    pe.wait_ge(gelu_ready, i * 6 + (m - 1))
                    first(m, m % 2, i)
                    pe.wait_ge(peer_act, i * 6 + m)
                    second(m - 1, (m - 1) % 2, False, False, i)
            pe.wait_ge(peer_act, NK)
            second(NK - 1, (NK - 1) % 2, False, True)
            sums(8, T)


def _by_tile(w, t=P):
    k, n = w.shape
    return w.reshape(k // P, P, n // t, t).transpose(2, 1, 0, 3).reshape(n // t, P, -1)


def _by_row(w):
    return w.reshape(w.shape[0] // P, P, w.shape[1])


def _stream(i):
    def lagged(first, second):
        out = [first[0]]
        for j in range(1, len(second)):
            out += [first[j], second[j - 1][None]]
        return out + [second[-1][None]]

    def mlp(gu, down):
        up = _by_tile(gu)
        return lagged([np.stack([up[j], up[FT + j]]) for j in range(FT)], _by_row(down))

    w = i["w_in"][0]
    cuts = np.cumsum([0, D, D, D, 768, 768, 768, D, D])
    qa, ka, va, qd, kd, vd, ga, gb = (w[:, a:b] for a, b in zip(cuts[:-1], cuts[1:]))
    w2 = i["w_in_2"][0]
    cuts = np.cumsum([0, HY, HY, HY, D, D, 2 * D])
    x0, x1, v, rx, rg, gl = (w2[:, a:b] for a, b in zip(cuts[:-1], cuts[1:]))
    pad = np.zeros((D, D - 768), np.float32)
    u = i["peer_u_2"][0].reshape(NK, NK, KT, P).transpose(0, 3, 2, 1).reshape(NK, P, D)
    vv = i["peer_v_2"][0].reshape(NK, NK, D)
    parts = (
        mlp(i["w_gu1"][0], i["w_down1"][0])
        + [_by_tile(m) for m in (qa, ka, qd, kd)]
        + [_by_row(va), _by_row(np.concatenate([vd, pad], 1)), _by_tile(ga), _by_tile(gb)]
        + [_by_tile(i["w_proj_b"][0]).reshape(2, 4, P, 2 * P).transpose(0, 2, 1, 3).reshape(2, P, CW)]
        + [_by_tile(i["w_proj_a"][0]), _by_tile(i["w_out"][0])]
        + mlp(i["w_gu2"][0], i["w_down2"][0])
        + [_by_tile(m) for m in (rx, v, x1, x0)]
        + [i["rg_gate_w_2"][0].transpose(0, 1, 3, 2, 4).reshape(4, P, CW)]
        + [_by_tile(rg), _by_tile(gl)]
        + [_by_tile(i["hy_out_2"][0]).reshape(4, 2, P, 4 * P).transpose(0, 2, 1, 3).reshape(4, P, CW)]
        + [_by_tile(i["rg_out_2"][0]), _by_tile(i["w_out_2"][0]), _by_tile(i["peer_wq_2"][0])]
        + [i["peer_keys_2"][0].reshape(2, 8, NK, P).transpose(0, 3, 1, 2).reshape(2, P, CW)]
        + lagged(list(u[:, None]), vv)
    )
    out = np.concatenate(parts, 0)
    assert out.shape == (N_CHUNKS, P, CW), out.shape
    return out


def _columns(i):
    d = np.arange(P) % DH
    inv = (np.float32(THETA) ** (-(np.arange(0, ROT, 2, dtype=np.float32) / np.float32(ROT)))).astype(np.float32)
    table = {
        "rope_inv": np.where(d < ROT, inv[d % (ROT // 2)], 0).astype(np.float32),
        "rope_sign": np.where(d < ROT // 2, -1, 1).astype(np.float32),
    }
    out = []
    for name, n in COLUMNS:
        a = table[name] if name in table else np.asarray(i[name])
        width = min(P, a.size // n)
        c = a.reshape(n, width).T
        if width < P:
            c = np.concatenate([c, np.zeros((P - width, n), np.float32)], 0)
        out.append(c)
    return np.ascontiguousarray(np.concatenate(out, 1))


def _tiled(a):
    out = np.zeros((3 * P,) + a.shape[1:], np.float32)
    out[:L] = a
    return np.ascontiguousarray(np.moveaxis(out.reshape((3, P) + a.shape[1:]), 0, 1))


def _constants():
    f32 = np.float32
    t = np.linspace(0.0, 1.0, L, dtype=f32)[:, None]
    w = (f32(2.0 * math.pi / L) * np.arange(L, dtype=f32))[:, None]
    bands = np.linspace(1e-4, HB - 1, HB, dtype=f32)[None, :]
    z = np.concatenate([t, np.cos(bands * w), -np.sin(bands * w)], 1).astype(f32)
    deltas = np.abs(np.linspace(math.log(1e-2) / 0.3, math.log(1e-2) / 1.5, HY, dtype=f32))
    decay = np.exp(-t * deltas).astype(f32)
    back = decay.copy()
    back[0] = 0.0
    s, f = np.arange(L, dtype=np.float64), np.arange(L, dtype=np.float64) + 0.5
    a = 2.0 * math.pi * np.outer(s, f) / (2 * L)
    dft = np.stack([np.cos(a), -np.sin(a)], 1).astype(f32)
    a = 2.0 * math.pi * np.outer(f, np.arange(NM, L)) / (2 * L)
    idft = (np.stack([np.cos(a), -np.sin(a)], 1) / L).astype(f32)
    q, k = np.arange(T)[:, None], np.arange(T)[None, :]
    mask = []
    for dil, half in DIL:
        seen = ((q - k) % dil == 0) & (abs(q - k) <= half * dil)
        mask.append(np.where(seen, 0.0, NEG * math.sqrt(DH)).astype(f32).reshape(2, P, T).transpose(1, 0, 2))
    swap = np.zeros((P, P), f32)
    d = np.arange(P)
    r = d % DH
    swap[np.where(r < 8, d + 8, np.where(r < ROT, d - 8, d)), d] = 1.0
    sq = np.stack([np.eye(P, dtype=f32), swap, np.ones((P, P), f32)], 1)
    return {"zt": np.ascontiguousarray(z.T), "decay": _tiled(np.stack([decay, back], 1)), "dft": _tiled(dft), "idft": _tiled(idft),
            "mask": np.ascontiguousarray(np.stack(mask, 1)), "squares": np.ascontiguousarray(sq)}


def kernel(**inputs):
    import concourse.bacc as bacc
    from concourse.bass_utils import run_bass_kernel_spmd

    i = {k: np.asarray(v) for k, v in inputs.items()}
    c = _constants()

    def features(a):
        return np.ascontiguousarray(a.T.reshape(KT, P, -1).transpose(1, 0, 2))

    arrays = {
        "x": features(i["x"][0]), "meta": features(i["meta_2"]),
        "positions": np.ascontiguousarray(np.broadcast_to(i["positions"][0], (P, T))),
        "stream": _stream(i), "columns": _columns(i),
        "filter_w1": i["hy_w1_2"][0], "filter_w2": i["hy_w2_2"][0],
        "filter_w3": np.concatenate([i["hy_w3_2"][0], i["hy_b3_2"]], 0),
        "zt": c["zt"], "decay": c["decay"], "dft": c["dft"], "idft": c["idft"], "mask": c["mask"], "squares": c["squares"],
    }
    nc = bacc.Bacc("TRN2", target_bir_lowering=False, num_devices=1)
    args = [nc.dram_tensor(f"in_{n}", a.shape, mybir.dt.from_np(a.dtype), kind="ExternalInput").ap() for n, a in arrays.items()]
    out = nc.dram_tensor("out", (P, KT, T), F32, kind="ExternalOutput").ap()
    build(nc, *args, out)
    r = run_bass_kernel_spmd(nc, [{f"in_{n}": a for n, a in arrays.items()}], core_ids=[0])
    got = r.results[0]["out"]
    return got.transpose(2, 1, 0).reshape(1, T, D)
```

```python
import math
from contextlib import ExitStack

import numpy as np

import concourse.bass as bass
from concourse import mybir

F32 = mybir.dt.float32
F32R = mybir.dt.float32r
I32 = mybir.dt.int32
U32 = mybir.dt.uint32
ALU = mybir.AluOpType
ACT = mybir.ActivationFunctionType
AX = mybir.AxisListType

P = 128
D = 1024
KT = D // P
T = 256
NM = 16
L = T + NM
FF = 2816
FT = FF // P
EPS = 1e-6

DA_H = 8
DH = 64
DIL = ((1, 64), (4, 64), (16, 64))
DIL_H = 4
NEG = -1e30
ROT = 16
THETA = 500000.0
LAMBDA_INIT = 0.8 - 0.6 * math.exp(0.0)

HY = 512
HYT = HY // P
HB = 16
FW = 64
RT = D // P
RG_C = 8.0

PH = 8
NK = 128
NA = 42
TOPK = 16

NS = 6
NX = 3
NW = 3
CW = 1024
STAGES = [
    ("ffn1", 3 * FT), ("qk", 28), ("va", KT), ("vd", KT), ("gates", 16), ("proj_b", 2), ("proj_a", 8),
    ("out1", 8), ("ffn2", 3 * FT), ("rgx", 8), ("hyena", 12), ("rggate", 4), ("rgg", 8), ("gl", 16),
    ("hyout", 4), ("rgout", 8), ("out2", 8), ("wq", 16), ("keys", 2), ("experts", 2 * NK),
]
START, N_CHUNKS = {}, 0
for _name, _n in STAGES:
    START[_name] = N_CHUNKS
    N_CHUNKS += _n

COLUMNS = [
    ("g_pre_ffn1", 8), ("g_post_ffn1", 8), ("g_pre_mix", 8), ("g_post_mix", 8), ("g_pre_ffn2", 8),
    ("g_post_ffn2", 8), ("g_mix_2", 8), ("g_ffn_2", 8), ("g_final_2", 8), ("g_subln", 1),
    ("b_gate_2", 16), ("hy_conv_w_2", 36), ("hy_conv_b_2", 12), ("hy_skip_2", 4), ("rg_conv_w_2", 64),
    ("rg_conv_b_2", 16), ("rg_gate_b_2", 32), ("rg_lambda_2", 16), ("hy_b1_2", 1), ("hy_b2_2", 1),
    ("hy_freq_2", 2), ("lambda_q1", 1), ("lambda_k1", 1), ("lambda_q2", 1), ("lambda_k2", 1),
    ("rope_inv", 1), ("rope_sign", 1),
]
COL, N_COLS = {}, 0
for _name, _n in COLUMNS:
    COL[_name] = N_COLS
    N_COLS += _n

LT = [(0, P), (P, P), (2 * P, NM)]

NORMS = ["g_pre_ffn1", "g_post_ffn1", "g_pre_mix", "g_post_mix", "g_pre_ffn2", "g_post_ffn2", "g_mix_2",
         "g_ffn_2", "g_final_2"]
TWO_PI = 2.0 * math.pi
ROUND = 1.5 * 2.0 ** 23
PI1 = 6.28125
PI2 = float(np.float32(np.round((TWO_PI - PI1) * 2 ** 21) / 2 ** 21))
PI3 = float(np.float32(TWO_PI - PI1 - PI2))
PI_IN = 3.1415925


def build(nc, x_d, meta_d, pos_d, stream_d, cols_d, w1_d, w2_d, w3_d, zt_d, decay_d, dft_d, idft_d, mask_d, sq_d, out_d):
    with ExitStack() as ctx:
        place = {}

        def sb(name, shape, dt=F32):
            place[name] = -(-nc.sbuf_base // 32) * 32
            return ctx.enter_context(nc.sbuf_tensor(name, shape, dt))

        def over(name, under, at, shape):
            return nc.alloc_sbuf_tensor_at(name, shape, dtype=F32R, offset=place[under] + 4 * at)

        def sem(name):
            return ctx.enter_context(nc.semaphore(name))

        ring = sb("ring", [P, NS, CW])
        x = sb("x", [P, KT, L])
        h = sb("h", [P, KT, L])
        sq = sb("sq", [P, KT, L])
        cols = sb("cols", [P, N_COLS])
        square = sb("square", [P, 3, P])
        ident, swap, ones = square[:, 0, :], square[:, 1, :], square[:, 2, :]
        stat = sb("stat", [P, 2, L])
        var, std, rstd = stat[:, 0, :], stat[:, 0, :], stat[:, 1, :]
        small = sb("small", [P, 256])
        arena = sb("arena", [P, NK * T])
        aux = sb("aux", [P, 6240])
        FFN_AT, FFN_N = 9984, NW * 2 * CW + 2 * KT * T + 4 * T
        ffn_split = over("ffn_split", "arena", FFN_AT, [P, FFN_N])
        peer_hi = over("peer_hi", "ring", NX * CW, [P, NW, CW])
        peer_split = over("peer_split", "aux", 0, [P, NW * CW + 4 * T])
        peer_h = over("peer_h_hi", "sq", 0, [P, KT, L]), over("peer_h_lo", "h", 0, [P, KT, L])
        ps = ctx.enter_context(nc.psum_tensor("ps", [P, 8, 512], F32))

        class Space:

            def __init__(self, base, at=0):
                self.base, self.at = base, at

            def take(self, *shape):
                n = int(np.prod(shape))
                piece = self.base[:, self.at:self.at + n]
                self.at += n
                assert self.at <= self.base.shape[1], (self.at, self.base.shape)
                if len(shape) == 2:
                    piece = piece.rearrange("p (a b) -> p a b", a=shape[0])
                if len(shape) == 3:
                    piece = piece.rearrange("p (a b c) -> p a b c", a=shape[0], b=shape[1])
                return piece

        def col(name, n=0):
            at = COL[name] + n
            return cols[:, at:at + 1]

        def split_pair(s, *shape):
            return s.take(*shape), s.take(*shape)

        s = Space(aux)
        kre, kim = s.take(3, HY), s.take(3, HY)
        dft = s.take(3, 2, L)
        idft = s.take(3, 2, T)
        s = Space(aux)
        s.take(CW)
        sel_b, sel_a = s.take(4, 4, NK), s.take(4, 4, NK)
        e1t, e2t, gt = s.take(T), s.take(T), s.take(T)
        iota, io16 = s.take(NK), s.take(TOPK)
        s = Space(aux, NW * CW + 4 * T)
        ge_p, act_p = s.take(2, T), s.take(2, T)
        s = Space(peer_split)
        peer_lo = s.take(NW, CW)
        peer_w = [(peer_hi[:, n, :], peer_lo[:, n, :]) for n in range(NW)]
        peer_part = split_pair(s, 2, T)

        s = Space(arena, 23360)
        assert FFN_AT + FFN_N <= s.at
        zt, w1, w2, w3 = s.take(L), s.take(FW), s.take(FW), s.take(2 * HY)
        arg, turn, hdn = s.take(L), s.take(L), s.take(L)
        decay = s.take(3, 2, HY)
        kfb, ksum, kdif = s.take(2, HY), s.take(3, HY), s.take(3, HY)
        s = Space(arena)
        rope_c, rope_s = s.take(T), s.take(T)
        posi = s.take(T)
        ang, angq = s.take(T), s.take(T)
        silu, act = s.take(2, T), s.take(2, T)
        first = s.at
        raw, rot = s.take(2, T), s.take(2, T)
        qk = s.take(28, T)
        va, vd = s.take(2, D), s.take(2, 3 * DIL_H * DH)
        sg = s.take(16, T)
        mask = s.take(3, 2, T)
        da_p, da_a, da_t = s.take(2, 4, T), s.take(2, 2, T), s.take(2, T)
        da_at, ot = s.take(2, 2 * T), s.take(DA_H, T)
        dl_p, dl_pt = s.take(3, 2, T), s.take(3, 2, T)
        odt = s.take(2, T)
        s = Space(ffn_split)
        ffn_w = [split_pair(s, CW) for _ in range(NW)]
        ffn_h, ffn_act = split_pair(s, KT, T), split_pair(s, 2, T)
        s = Space(arena, first + 4 * T)
        oa, srstd, merged = s.take(DA_H, T), s.take(DA_H, T), s.take(KT, T)
        s = Space(arena)
        rgx = s.take(RT, L)
        xc = [s.take(RT, L), s.take(RT, T)]
        r_g = [s.take(RT, L), s.take(RT, T)]
        i_g = [s.take(RT, L), s.take(RT, T)]
        m_g = [s.take(RT, L), s.take(RT, T)]
        hu = s.take(12, L)
        ys = s.take(3, 2, HY)
        gg = s.take(RT, T)
        sgl = s.take(16, T)
        s = Space(arena, 0)
        merged2 = s.take(KT, T)
        vt = sq[:, :, :].rearrange("p a b -> p (a b)")[:, 0:3 * HY].rearrange("p (a b) -> p a b", a=3)
        s = Space(arena)
        pq = s.take(16, T)
        s = Space(arena, 100 * T)
        assert NA <= 100 and NA % 6 == 0 and (NK - 2 - NA) % 6 == 0
        sc = s.take(2, 16, NK)
        scr = s.take(2 * NK)
        tv, ti, tif = s.take(2, 16, TOPK), s.take(2, 16, TOPK), s.take(2, 16, TOPK)
        cv, ci = s.take(2, PH, TOPK), s.take(2, PH, TOPK)
        ew = s.take(3, 2, PH * TOPK)
        s = Space(arena, 100 * T)
        cand = s.take(2, PH, TOPK * TOPK)
        s = Space(arena, 100 * T)
        hot = s.take(PH * TOPK, TOPK)
        cij, cijf = s.take(2, 2, PH * TOPK), s.take(2, 2, PH * TOPK)
        gates_all = arena[:, :].rearrange("p (e t) -> p e t", t=T)

        landed = [sem(f"landed{i}") for i in range(NS)]
        chunk_done = sem("chunk_done")
        expert_landed = [sem(f"expert_landed{i}") for i in range(NX)]
        hi_ready = sem("hi_ready")
        lo_up, lo_down = sem("lo_up"), sem("lo_down")
        h_hi, h_lo = sem("h_hi"), sem("h_lo")
        loaded_mask = sem("loaded_mask")
        loaded_vec = sem("loaded_vec")
        loaded_const = sem("loaded_const")
        loaded_x = sem("loaded_x")
        iota_ready = sem("iota_ready")
        dve_step = sem("dve_step")
        act_step = sem("act_step")
        sq_ready, ssq_ready, var_ready, std_ready = sem("sq_ready"), sem("ssq_ready"), sem("var_ready"), sem("std_ready")
        h_ready, x_ready = sem("h_ready"), sem("x_ready")
        flt_pe, flt_arg, flt_sin, flt_k = sem("flt_pe"), sem("flt_arg"), sem("flt_sin"), sem("flt_k")
        lam_prod, lam_sum, lam_exp = sem("lam_prod"), sem("lam_sum"), sem("lam_exp")
        rope_arg, rope_sin = sem("rope_arg"), sem("rope_sin")
        silu_ready, act_ready = sem("silu_ready"), sem("act_ready")
        act_gated, act_hi = sem("act_gated"), sem("act_hi")
        raw_copied, swapped, qk_ready = sem("raw_copied"), sem("swapped"), sem("qk_ready")
        v_copied, gate_copied = sem("v_copied"), sem("gate_copied")
        da_scores, da_nbias, da_exp, da_mixed = sem("da_scores"), sem("da_nbias"), sem("da_exp"), sem("da_mixed")
        da_turned, da_tcopied, da_out, ot_ready = sem("da_turned"), sem("da_tcopied"), sem("da_out"), sem("ot_ready")
        dl_scores, dl_nbias, dl_exp, dl_prob = sem("dl_scores"), sem("dl_nbias"), sem("dl_exp"), sem("dl_prob")
        dl_turned, dl_tcopied, dl_out, od_ready = sem("dl_turned"), sem("dl_tcopied"), sem("dl_out"), sem("od_ready")
        sub_sq, sub_sum, sub_var, sub_std, oa_ready = sem("sub_sq"), sem("sub_sum"), sem("sub_var"), sem("sub_std"), sem("oa_ready")
        sg_ready, merged_ready = sem("sg_ready"), sem("merged_ready")
        in2_copied, hy_conv, rg_conv, vx_ready = sem("in2_copied"), sem("hy_conv"), sem("rg_conv"), sem("vx_ready")
        vt_turned, vt_ready, spec_ready, ys_ready = sem("vt_turned"), sem("vt_ready"), sem("spec_ready"), sem("ys_ready")
        conv_out, hy_ready = sem("conv_out"), sem("hy_ready")
        rg_gated, rg_tanh, rg_den, rg_sqrt, rg_ready, decay_ready = (
            sem("rg_gated"), sem("rg_tanh"), sem("rg_den"), sem("rg_sqrt"), sem("rg_ready"), sem("decay_ready"))
        merged2_ready = sem("merged2_ready")
        lam_e, sp_ready = sem("lam_e"), sem("sp_ready")
        pq_copied, sc_out, sc_copied = sem("pq_copied"), sem("sc_out"), sem("sc_copied")
        cv_ready, ce_ready, ew_ready, ew_turned, ewt_ready = (
            sem("cv_ready"), sem("ce_ready"), sem("ew_ready"), sem("ew_turned"), sem("ewt_ready"))
        ab_raw, ab_ready, g_token, g_copied, g_gated = sem("ab_raw"), sem("ab_ready"), sem("g_token"), sem("g_copied"), sem("g_gated")
        gelu_ready, peer_act = sem("gelu_ready"), sem("peer_act")
        stored = sem("stored")
        N_CONST = 8

        def acc(n):
            return ps[:, n // 2, (n % 2) * T:(n % 2 + 1) * T]

        def real(buf, k):
            return buf[:, k, NM:L]

        def ffn_up(base, j):
            return base + (1 if j == 0 else 3 * j)

        def ffn_down(base, j):
            return base + (3 * FT - 1 if j == FT - 1 else 3 * j + 4)

        HI_EXPERTS, UP_EXPERTS, DOWN_EXPERTS = 2 * 3 * FT, 2 * 2 * FT, 2 * FT

        def expert_u(e):
            return e if e < NA else 2 * NA + (0 if e == NA else 2 * (e - NA) - 1)

        def expert_v(e):
            return NA + e if e < NA else 2 * NK - 1 if e == NK - 1 else 2 * NA + 2 * (e - NA) + 2

        N_PAIRS = (NK - 2 - NA) // 6
        QUADS = T // 4

        def tmp_spec(fn, n):
            return rgx[0:fn, :, :].rearrange("p a b -> p (a b)")[:, n * HY:(n + 1) * HY]

        def tmp_mix(n):
            return ys[:, 0, 0, n * T:(n + 1) * T]

        def i_tmp(d):
            return rgx[:, :, 0:(L if d == 0 else T)]

        def gl_tile(pe, tile, m):
            pe.wait_ge(in2_copied, 5 * RT + RT + m - 1)
            tile(START["gl"] + m, ps[:, 4 + m % 2, 0:T], lambda k: real(h, k)).then_inc(chunk_done, 1)

        block = ctx.enter_context(nc.Block())

        @block.sync
        def _(sp):
            sp.dma_start(x[:, :, NM:L], x_d).then_inc(loaded_x, 16)
            for c in range(NS):
                sp.dma_start(ring[:, c, :], stream_d[c]).then_inc(landed[c], 16)
            base = START["experts"]
            whole = (base - NS) // NS
            with sp.Fori(0, whole) as i:
                for m in range(NS):
                    sp.wait_ge(chunk_done, i * NS + (m + 1))
                    sp.dma_start(ring[:, m, :], stream_d[bass.ds(i * NS + (NS + m), 1), :, :].rearrange("a p n -> p (a n)")).then_inc(landed[m], 16)
            for c in range(NS + whole * NS, base):
                sp.wait_ge(chunk_done, c - NS + 1)
                sp.dma_start(ring[:, c % NS, :], stream_d[c]).then_inc(landed[c % NS], 16)
            for c in range(NX):
                sp.wait_ge(chunk_done, max(n for n in range(base) if n % NS == c) + 1)
                sp.dma_start(ring[:, c, :], stream_d[base + c]).then_inc(expert_landed[c], 16)

            def refill(r, i=0, step=0):
                u = {expert_u(e): e for e in range(NK)}
                v = {expert_v(e): e for e in range(NK)}
                keys = step if r - NX < 2 * NA else step // 2
                if r - NX in u:
                    sp.wait_ge(lo_up, i * keys + (UP_EXPERTS + u[r - NX] + 1))
                else:
                    sp.wait_ge(lo_down, i * keys + (DOWN_EXPERTS + v[r - NX] + 1))
                c = stream_d[bass.ds(i * step + (base + r), 1), :, :].rearrange("a p n -> p (a n)") if step else stream_d[base + r]
                sp.dma_start(ring[:, r % NX, :], c).then_inc(expert_landed[r % NX], 16)

            for part in range(2):
                with sp.Fori(0, NA // 6) as i:
                    for m in range(6):
                        refill(part * NA + NX + m, i, 6)
            first = 2 * NA + NX
            refill(first)
            with sp.Fori(0, (2 * NK - first - 1) // 6) as i:
                for m in range(6):
                    refill(first + 1 + m, i, 6)
            for r in range(2 * NK - (2 * NK - first - 1) % 6, 2 * NK):
                refill(r)
            sp.wait_ge(h_ready, 8 * 6)
            sp.dma_start(out_d, h[:, :, NM:L]).then_inc(stored, 16)
            sp.wait_ge(stored, 16)

        @block.gpsimd
        def _(pool):
            def lo(r, done, made, slot, split):
                if made is not None:
                    pool.wait_ge(lo_up, made)
                pool.wait_ge(hi_ready, done)
                nc.gpsimd.tensor_tensor(split[r % NW][1], ring[:, slot, :], split[r % NW][0].bitcast(F32), ALU.subtract).then_inc(lo_up, 1)

            def ffn(f, base):
                for r in range(4):
                    lo(r, f * 3 * FT + r + 1, f * 2 * FT + r if f or r else None, (base + r) % NS, ffn_w)
                with pool.Fori(0, (FT - 2) // 2) as i:
                    for m in (2, 3):
                        for half, r in enumerate((3 * m - 1, 3 * m)):
                            lo(r, i * 6 + (f * 3 * FT + r + 1), i * 4 + (f * 2 * FT + 2 * m + half), (base + r) % NS, ffn_w)

            nc.gpsimd.memset(hdn[64:65, :], 1.0).then_inc(iota_ready, 1)
            pool.wait_ge(iota_ready, 1)
            ffn(0, START["ffn1"])
            ffn(1, START["ffn2"])
            pool.wait_ge(lo_up, UP_EXPERTS)
            pool.wait_ge(x_ready, 8 * 4)
            nc.gpsimd.iota(iota, pattern=[[1, NK]], base=0, channel_multiplier=0, allow_small_or_imprecise_dtypes=True).then_inc(iota_ready, 1)
            pool.wait_ge(iota_ready, 2)
            nc.gpsimd.iota(io16, pattern=[[1, TOPK]], base=0, channel_multiplier=0, allow_small_or_imprecise_dtypes=True).then_inc(iota_ready, 1)
            pool.wait_ge(iota_ready, 3)

            def up_lo(e, i=0, step=0):
                n = UP_EXPERTS + e
                lo(expert_u(e), i * (step if e < NA else 2 * step) + (HI_EXPERTS + expert_u(e) + 1), i * step + n, expert_u(e) % NX, peer_w)

            with pool.Fori(0, NA // 6) as i:
                for m in range(6):
                    up_lo(m, i, 6)
            pool.wait_ge(lo_up, UP_EXPERTS + NA)
            def down(e, i=0, step=0):
                r = expert_v(e)
                n, done = DOWN_EXPERTS + e, HI_EXPERTS + r + 1
                pool.wait_ge(lo_down, i * step + n if step else n)
                pool.wait_ge(hi_ready, i * step + done if step else done)
                nc.gpsimd.tensor_tensor(peer_w[r % NW][1], ring[:, r % NX, :], peer_w[r % NW][0].bitcast(F32), ALU.subtract).then_inc(lo_down, 1)

            down(0)
            pool.wait_ge(g_token, QUADS)
            for e in range(1, 6):
                down(e)
            with pool.Fori(0, NA // 6 - 1) as i:
                for m in range(6, 12):
                    down(m, i, 6)
            pool.wait_ge(lo_down, DOWN_EXPERTS + NA)
            up_lo(NA)
            up_lo(NA + 1)
            with pool.Fori(0, N_PAIRS) as i:
                for m in range(2, 8):
                    up_lo(NA + m, i, 6)

        @block.scalar
        def _(act_e):
            steps = [0]

            def link(ins):
                steps[0] += 1
                ins.then_inc(act_step, 1)
                act_e.wait_ge(act_step, steps[0])

            A = nc.scalar.activation
            act_e.dma_start(cols[:], cols_d).then_inc(loaded_vec, 16)
            act_e.dma_start(square[:], sq_d).then_inc(loaded_vec, 16)
            act_e.dma_start(posi.bitcast(I32), pos_d).then_inc(loaded_vec, 16)

            def squares(n, src, w):
                if n:
                    act_e.wait_ge(ssq_ready, n)
                for k in range(KT):
                    A(sq[:, k, 0:w], src(k), ACT.Square).then_inc(sq_ready, 1)

            def root(n, w):
                act_e.wait_ge(var_ready, n + 1)
                A(std[:, 0:w], var[:, 0:w], ACT.Sqrt).then_inc(std_ready, 1)

            def ffn_hi(f, base, r, i=None):
                c = base + r
                n = 16 * (c // NS + 1)
                act_e.wait_ge(landed[c % NS], n if i is None else i * 16 + n)
                if r >= NW:
                    act_e.wait_ge(chunk_done, c - NW + 1 if i is None else i * 6 + (c - NW + 1))
                A(ffn_w[r % NW][0], ring[:, c % NS, :], ACT.Copy).then_inc(hi_ready, 1)

            def input_hi(n, ready, dst):
                for k in range(KT):
                    act_e.wait_ge(h_ready, ready + k + 1)
                    A(dst[:, k, 0:T], real(h, k), ACT.Copy).then_inc(h_hi, 1)

            act_e.wait_ge(loaded_x, 16)
            squares(0, lambda k: real(x, k), T)
            root(0, T)
            for r in range(NW):
                ffn_hi(0, START["ffn1"], r)
            input_hi(0, 0, ffn_h[0])
            act_e.dma_start(x[:, :, 0:NM], meta_d).then_inc(loaded_const, 16)
            act_e.dma_start(zt[0:2 * HB + 1, :], zt_d).then_inc(loaded_const, 16)
            act_e.dma_start(w1[0:2 * HB + 1, :], w1_d).then_inc(loaded_const, 16)
            act_e.dma_start(w2[0:FW, :], w2_d).then_inc(loaded_const, 16)
            act_e.dma_start(w3[0:FW + 1, :], w3_d).then_inc(loaded_const, 16)
            act_e.dma_start(decay, decay_d).then_inc(loaded_const, 16)
            act_e.dma_start(dft, dft_d).then_inc(loaded_const, 16)
            act_e.dma_start(idft, idft_d).then_inc(loaded_const, 16)
            act_e.wait_ge(rope_arg, 2)
            A(rope_s, ang, ACT.Sin).then_inc(rope_sin, 1)
            A(rope_c, angq, ACT.Sin).then_inc(rope_sin, 1)
            def ffn(f, base):
                def one(done, buf):
                    act_e.wait_ge(chunk_done, done)
                    A(silu[:, buf, :], ps[:, 4 + buf, 0:T], ACT.Silu).then_inc(silu_ready, 1)

                ffn_hi(f, base, 3)
                if f:
                    act_e.wait_ge(act_ready, FT - 1)
                one(base + 2, 0)
                ffn_hi(f, base, 4)
                ffn_hi(f, base, 5)
                if f:
                    act_e.wait_ge(act_ready, FT)
                one(base + 4, 1)
                with act_e.Fori(0, (FT - 2) // 2) as i:
                    for m in (2, 3):
                        for r in range(3 * m, 3 * m + 3):
                            ffn_hi(f, base, r, i)
                        act_e.wait_ge(act_ready, i * 2 + (f * FT + m - 1))
                        one(i * 6 + (base + 3 * m + 1), m % 2)

            ffn(0, START["ffn1"])
            act_e.dma_start(mask, mask_d).then_inc(loaded_mask, 16)
            act_e.wait_ge(chunk_done, START["qk"])
            squares(1, acc, T)
            root(1, T)
            act_e.wait_ge(x_ready, 8)
            squares(2, lambda k: real(x, k), T)
            root(2, T)

            def between(n):
                if n == 0:
                    act_e.wait_ge(lam_sum, 1)
                    A(small[:, 4:6], ps[:, 0, 0:2], ACT.Exp).then_inc(lam_exp, 1)
                    act_e.wait_ge(lam_e, 1)
                    A(small[:, 16:32], small[:, 32:48], ACT.Exp, scale=-1.0).then_inc(lam_exp, 1)
                if n in (3, 6):
                    act_e.wait_ge(flt_arg, n // 3)
                    A(hdn[0:FW, :], arg[0:FW, :], ACT.Sin).then_inc(flt_sin, 1)

            for n in range(28):
                act_e.wait_ge(chunk_done, START["qk"] + n + 1)
                if n >= 2:
                    act_e.wait_ge(qk_ready, n - 1)
                A(raw[:, n % 2, :], ps[:, 4 + n % 2, 0:T], ACT.Copy).then_inc(raw_copied, 1)
                between(n)
            act_e.wait_ge(chunk_done, START["vd"])
            for b in range(4):
                A(va[:, b // 2, (b % 2) * 512:(b % 2 + 1) * 512], ps[:, b, :], ACT.Copy).then_inc(v_copied, 1)

            def da_exps(hd):
                act_e.wait_ge(da_nbias, hd + 1)
                if hd >= 2:
                    act_e.wait_ge(da_mixed, 2 * (hd - 1))
                for c in range(2):
                    for q in range(2):
                        A(da_p[:, hd % 2, 2 * c + q, :], ps[:, 2 * (hd % 2) + c, q * T:(q + 1) * T], ACT.Exp,
                          bias=small[:, 64 + 8 * (hd % 2) + 2 * c + q:65 + 8 * (hd % 2) + 2 * c + q], scale=DH ** -0.5,
                          accum_out=small[:, 80 + 8 * (hd % 2) + 2 * c + q:81 + 8 * (hd % 2) + 2 * c + q]).then_inc(da_exp, 1)

            def gate_copy(n):
                act_e.wait_ge(chunk_done, START["gates"] + n + 1)
                A(sg[:, n, :], ps[:, 4 + n % 2 if n < DA_H else 6, 0:T], ACT.Copy).then_inc(gate_copied, 1)

            da_exps(0)
            for hd in range(DA_H):
                if hd + 1 < DA_H:
                    da_exps(hd + 1)
                gate_copy(hd)
                act_e.wait_ge(da_turned, hd + 1)
                if hd >= 2:
                    act_e.wait_ge(da_out, hd - 1)
                A(da_at[:, hd % 2, :], ps[:, 6, :], ACT.Copy).then_inc(da_tcopied, 1)
            for j in range(DIL_H):
                act_e.wait_ge(dl_nbias, j + 1)
                for q in range(2):
                    A(dl_p[:, :, q, :], dl_p[:, :, q, :], ACT.Exp, bias=small[:, 100 + q:101 + q], scale=DH ** -0.5,
                      accum_out=small[:, 104 + q:105 + q]).then_inc(dl_exp, 1)
                gate_copy(DA_H + 2 * j)
                act_e.wait_ge(dl_turned, j + 1)
                if j >= 1:
                    act_e.wait_ge(dl_out, j)
                A(dl_pt[:, :, :, :].rearrange("p a b c -> p a (b c)"), ps[:, 3:6, :], ACT.Copy).then_inc(dl_tcopied, 1)
                gate_copy(DA_H + 2 * j + 1)
            act_e.wait_ge(ssq_ready, 3)
            for hd in range(DA_H):
                act_e.wait_ge(ot_ready, hd + 1)
                A(sq[:, hd, 0:T], ot[:, hd, :], ACT.Square).then_inc(sub_sq, 1)
            act_e.wait_ge(gate_copied, 2 * KT)
            A(sg[:, :, :], sg[:, :, :], ACT.Sigmoid).then_inc(sg_ready, 1)
            act_e.wait_ge(sub_var, 1)
            A(srstd[:, :, :], srstd[:, :, :], ACT.Sqrt).then_inc(sub_std, 1)
            act_e.wait_ge(sub_sum, 1)
            act_e.wait_ge(merged_ready, KT)
            for r in range(NW):
                ffn_hi(1, START["ffn2"], r)
            act_e.wait_ge(chunk_done, START["ffn2"])
            squares(3, acc, T)
            root(3, T)
            act_e.wait_ge(x_ready, 16)
            squares(4, lambda k: real(x, k), T)
            root(4, T)
            input_hi(1, 2 * KT, ffn_h[0])
            ffn(1, START["ffn2"])
            act_e.wait_ge(chunk_done, START["rgx"])
            squares(5, acc, T)
            root(5, T)
            act_e.wait_ge(x_ready, 24)
            act_e.wait_ge(loaded_const, 16 * N_CONST)
            squares(6, lambda k: x[:, k, :], L)
            root(6, L)

            for n in range(RT):
                act_e.wait_ge(chunk_done, START["rgx"] + n + 1)
                A(rgx[:, n, :], ps[:, 4 + n % 2, 0:L], ACT.Copy).then_inc(in2_copied, 1)
            for d in range(2):
                w = L if d == 0 else T
                for g, buf in ((0, r_g), (1, i_g)):
                    for t in range(RT):
                        n = (2 * d + g) * RT + t
                        act_e.wait_ge(rg_gated, n + 1)
                        A(buf[d][:, t, :], ps[:, 4 + n % 2, 0:w], ACT.Sigmoid, bias=col("rg_gate_b_2", n)).then_inc(in2_copied, 1)
            for n in range(3):
                act_e.wait_ge(vt_turned, n + 1)
                A(vt[0:LT[n][1], n, :], ps[0:LT[n][1], n, :], ACT.Copy).then_inc(vt_ready, 1)
            act_e.wait_ge(sp_ready, 2)
            act_e.wait_ge(in2_copied, RT + 4 * RT)
            for d in range(2):
                for t in range(RT):
                    A(m_g[d][:, t, :], r_g[d][:, t, :], ACT.Tanh, scale=small[:, 160 + 8 * d + t:161 + 8 * d + t]).then_inc(rg_tanh, 1)
            act_e.wait_ge(rg_tanh, 2 * RT)
            for d in range(2):
                for t in range(RT):
                    A(r_g[d][:, t, :], r_g[d][:, t, :], ACT.Exp, scale=small[:, 176 + 8 * d + t:177 + 8 * d + t]).then_inc(decay_ready, 1)
            for n in range(RT):
                act_e.wait_ge(chunk_done, START["rgg"] + n + 1)
                A(gg[:, n, :], ps[:, 4 + n % 2, 0:T], ACT.Gelu_apprx_tanh).then_inc(in2_copied, 1)
            for d in range(2):
                act_e.wait_ge(rg_den, d + 1)
                A(m_g[d][:, :, :], m_g[d][:, :, :], ACT.Sqrt).then_inc(rg_sqrt, 1)
            for n in range(16):
                act_e.wait_ge(chunk_done, START["gl"] + n + 1)
                A(sgl[:, n, :], ps[:, 4 + n % 2, 0:T], ACT.Sigmoid, bias=col("b_gate_2", n)).then_inc(in2_copied, 1)

            act_e.wait_ge(x_ready, 32)
            squares(7, lambda k: real(x, k), T)
            root(7, T)
            act_e.wait_ge(ssq_ready, 8)
            input_hi(2, 4 * KT, peer_h[0])
            for n in range(16):
                act_e.wait_ge(chunk_done, START["wq"] + n + 1)
                A(pq[:, n, :], ps[:, 4 + n % 2, 0:T], ACT.Copy).then_inc(pq_copied, 1)
            for b in range(8):
                act_e.wait_ge(sc_out, b + 1)
                A(sc[:, b // 4, 4 * (b % 4):4 * (b % 4) + 4, :].rearrange("p a b -> p (a b)"), ps[:, b, :], ACT.Copy).then_inc(sc_copied, 1)
            base = START["experts"]

            def expert_hi(r, i=0, step=0):
                n = 16 * (r // NX + 1)
                act_e.wait_ge(expert_landed[r % NX], i * (step // NX * 16) + n if step else n)
                n = base + max(0, r - NW + 1)
                act_e.wait_ge(chunk_done, i * step + n if step else n)
                A(peer_w[r % NW][0], ring[:, r % NX, :], ACT.Copy).then_inc(hi_ready, 1)

            def ahead(e, dst, i=0, step=0):
                n = base + e + 1
                act_e.wait_ge(chunk_done, i * step + n if step else n)
                A(dst, ps[:, 4 + e % 2, 0:T], ACT.Gelu_apprx_tanh).then_inc(gelu_ready, 1)
                expert_hi(e + NW, i, step)

            for r in range(NW):
                expert_hi(r)
            with act_e.Fori(0, NA // 6 - 1) as i:
                for m in range(6):
                    ahead(m, gates_all[:, bass.ds(i * 6 + m, 1), :].rearrange("p a t -> p (a t)"), i, 6)
            act_e.wait_ge(cv_ready, 2)
            A(ew[:, 2, :, :], ew[:, 2, :, :], ACT.Exp).then_inc(ce_ready, 1)
            for e in range(NA - 6, NA):
                ahead(e, gates_all[:, e, :])

            def weigh(q, i=0, step=0):
                act_e.wait_ge(ab_raw, i * step + (q + 1) if step else q + 1)
                for m in range(4):
                    t = 4 * q + m
                    g = gt[:, bass.ds(i * (4 * step) + t, 1)] if step else gt[:, t:t + 1]
                    ins = A(sel_a[:, q % 4, m, :], sel_a[:, q % 4, m, :], ACT.Copy, scale=g)
                ins.then_inc(ab_ready, 1)

            def gates_out(q, i=0, step=0):
                act_e.wait_ge(g_token, i * step + (q + 1) if step else q + 1)
                t = bass.ds(i * (4 * step) + 4 * q, 4) if step else slice(4 * q, 4 * q + 4)
                A(gates_all[:, NA:NK, t], ps[:, 4 + q % 4, :].rearrange("p (t e) -> p e t", t=4)[:, NA:NK, :], ACT.Copy).then_inc(g_copied, 1)

            act_e.wait_ge(ewt_ready, 3)
            weigh(0)
            weigh(1)
            with act_e.Fori(0, QUADS // 4 - 1) as i:
                for m in range(4):
                    weigh(m + 2, i, 4)
                    gates_out(m, i, 4)
            for q in range(QUADS - 4, QUADS):
                if q + 2 < QUADS:
                    weigh(q + 2)
                gates_out(q)
            with act_e.Fori(0, NA // 6) as i:
                for m in range(6):
                    expert_hi(NA + NW + m, i, 6)

            def expert(done, buf):
                act_e.wait_ge(chunk_done, done)
                A(ge_p[:, buf, :], ps[:, 4 + buf, 0:T], ACT.Gelu_apprx_tanh).then_inc(gelu_ready, 1)

            act_e.wait_ge(peer_act, NA)
            expert(base + expert_u(NA) + 1, 0)
            expert_hi(2 * NA + 3)
            expert(base + expert_u(NA + 1) + 1, 1)
            with act_e.Fori(0, N_PAIRS) as i:
                for m in range(2, 8):
                    expert_hi(2 * NA + 2 * m, i, 12)
                    expert_hi(2 * NA + 2 * m + 1, i, 12)
                    act_e.wait_ge(peer_act, i * 6 + (NA + m - 1))
                    expert(i * 12 + (base + expert_u(NA + m) + 1), m % 2)
            act_e.wait_ge(x_ready, 40)
            squares(8, lambda k: real(x, k), T)
            root(8, T)

        @block.vector
        def _(dve):
            steps = [0]
            V = nc.vector

            def link(ins):
                steps[0] += 1
                ins.then_inc(dve_step, 1)
                dve.wait_ge(dve_step, steps[0])

            def mean_square(n, w, width=D, half=False):
                dve.wait_ge(ssq_ready, n + 1)
                f = 4.0 if half else 1.0
                V.tensor_scalar(var[:, 0:w], ps[:, 6, 0:w], f / width, f * EPS, ALU.mult, ALU.add).then_inc(var_ready, 1)
                dve.wait_ge(std_ready, n + 1)
                link(V.reciprocal(rstd[:, 0:w], std[:, 0:w]))

            def norm_in(n, name, src, dst, w):
                mean_square(n, w)
                for k in range(KT):
                    V.scalar_tensor_tensor(dst(k), src(k), col(name, k), rstd[:, 0:w], ALU.mult, ALU.mult).then_inc(h_ready, 1)

            def norm_out(n, name, half):
                mean_square(n, T, half=half)
                for k in range(KT):
                    link(V.scalar_tensor_tensor(h[:, k, 0:T], acc(k), col(name, k), rstd[:, 0:T], ALU.mult, ALU.mult))
                    V.tensor_tensor(real(x, k), real(x, k), h[:, k, 0:T], ALU.add).then_inc(x_ready, 1)

            def reduce_angle(a, q):
                link(V.tensor_scalar(q, a, 1.0 / TWO_PI, ROUND, ALU.mult, ALU.add))
                link(V.tensor_scalar(q, q, -ROUND, None, ALU.add))
                link(V.scalar_tensor_tensor(a, q, -PI1, a, ALU.mult, ALU.add))
                link(V.scalar_tensor_tensor(a, q, -PI2, a, ALU.mult, ALU.add))
                link(V.scalar_tensor_tensor(a, q, -PI3, a, ALU.mult, ALU.add))
                return V.tensor_scalar(a, a, PI_IN, -PI_IN, ALU.min, ALU.max)

            def split_gated(buf, src, split, n):
                dve.wait_ge(act_gated, n)
                V.tensor_copy(split[0][:, buf, :], src[:, buf, :]).then_inc(act_hi, 1)
                dve.wait_ge(act_hi, n)
                return V.tensor_tensor(split[1][:, buf, :], src[:, buf, :], split[0][:, buf, :].bitcast(F32), ALU.subtract)

            def input_lo(n, split):
                for k in range(KT):
                    dve.wait_ge(h_hi, n * KT + k + 1)
                    V.tensor_tensor(split[1][:, k, :], real(h, k), split[0][:, k, :].bitcast(F32), ALU.subtract).then_inc(h_lo, 1)

            def down_lo(r, done, slot, split):
                dve.wait_ge(hi_ready, done)
                V.tensor_tensor(split[r % NW][1], ring[:, slot, :], split[r % NW][0].bitcast(F32), ALU.subtract).then_inc(lo_down, 1)

            dve.wait_ge(loaded_vec, 16 * 3)
            dve.wait_ge(loaded_x, 16)
            norm_in(0, NORMS[0], lambda k: real(x, k), lambda k: real(h, k), T)
            input_lo(0, ffn_h)
            link(V.tensor_copy(ang, posi.bitcast(I32)))
            link(V.tensor_scalar(ang, ang, col("rope_inv"), None, ALU.mult))
            link(reduce_angle(ang, angq))
            link(V.scalar_tensor_tensor(angq, ang, -1.0, ang, ALU.mult, ALU.min))
            link(V.tensor_scalar(angq, angq, math.pi / 2, None, ALU.add))
            V.tensor_scalar(ang, ang, col("rope_sign"), None, ALU.mult).then_inc(rope_arg, 2)
            for n in (1, 2):
                V.tensor_tensor(small[:, n - 1:n], col(f"lambda_q{n}"), col(f"lambda_k{n}"), ALU.mult).then_inc(lam_prod, 1)
            lam = cols[:, COL["rg_lambda_2"]:COL["rg_lambda_2"] + 16]
            V.scalar_tensor_tensor(small[:, 32:48], lam, -1.0, lam, ALU.mult, ALU.max).then_inc(lam_e, 1)
            def ffn(f, base):
                hi = f * 3 * FT + 1

                def one(n, buf):
                    dve.wait_ge(silu_ready, n)
                    V.tensor_tensor(act[:, buf, :], silu[:, buf, :], ps[:, 4 + buf, T:2 * T], ALU.mult).then_inc(act_gated, 1)
                    split_gated(buf, act, ffn_act, n).then_inc(act_ready, 1)

                one(f * FT + 1, 0)
                down_lo(4, hi + 4, (base + 4) % NS, ffn_w)
                one(f * FT + 2, 1)
                with dve.Fori(0, (FT - 2) // 2) as i:
                    for m in (2, 3):
                        r = 3 * m + 1
                        down_lo(r, i * 6 + (hi + r), (base + r) % NS, ffn_w)
                        dve.wait_ge(chunk_done, i * 6 + (base + 3 * m - 1))
                        one(i * 2 + (f * FT + m + 1), m % 2)
                r = 3 * FT - 1
                down_lo(r, hi + r, (base + r) % NS, ffn_w)

            ffn(0, START["ffn1"])
            norm_out(1, NORMS[1], True)
            norm_in(2, NORMS[2], lambda k: real(x, k), lambda k: real(h, k), T)

            def between(n):
                if n in (1, 4):
                    layer = n // 3
                    if n == 1:
                        dve.wait_ge(loaded_const, 16 * N_CONST)
                    dve.wait_ge(flt_pe, layer + 1)
                    b, at = COL[("hy_b1_2", "hy_b2_2")[layer]], COL["hy_freq_2"] + layer
                    link(V.tensor_scalar(arg[0:FW, :], ps[0:FW, 1, 0:L], cols[0:FW, b:b + 1], cols[0:FW, at:at + 1], ALU.add, ALU.mult))
                    reduce_angle(arg[0:FW, :], turn[0:FW, :]).then_inc(flt_arg, 1)
                if n in (7, 10, 13):
                    m = (n - 7) // 3
                    tn = LT[m][1]
                    dve.wait_ge(flt_pe, 3 + m)
                    for d in range(2):
                        link(V.tensor_tensor(kfb[0:tn, d, :], ps[0:tn, 1 + d, :], decay[0:tn, m, d, :], ALU.mult))
                    V.tensor_tensor(ksum[0:tn, m, :], kfb[0:tn, 0, :], kfb[0:tn, 1, :], ALU.add).then_inc(flt_k, 1)
                    V.tensor_tensor(kdif[0:tn, m, :], kfb[0:tn, 0, :], kfb[0:tn, 1, :], ALU.subtract).then_inc(flt_k, 1)
                    dve.wait_ge(flt_k, 2 * m + 2)
                if n in (16, 19, 22):
                    m = (n - 16) // 3
                    fn = LT[m][1]
                    dve.wait_ge(flt_pe, 6 + m)
                    V.tensor_copy(kre[0:fn, m, :], ps[0:fn, 1, :]).then_inc(flt_k, 1)
                    V.tensor_copy(kim[0:fn, m, :], ps[0:fn, 2, :]).then_inc(flt_k, 1)
                if n == 25:
                    dve.wait_ge(lam_exp, 2)
                    link(V.tensor_tensor(small[:, 6:7], small[:, 5:6], small[:, 4:5], ALU.subtract))
                    link(V.tensor_scalar(small[:, 7:8], small[:, 6:7], -LAMBDA_INIT, None, ALU.add))
                    e, w, w2s, pl = small[:, 16:32], small[:, 112:128], small[:, 128:144], small[:, 144:160]
                    link(V.tensor_scalar(w, e, 2.0, None, ALU.add))
                    link(V.reciprocal(w, w))
                    link(V.tensor_tensor(w, w, e, ALU.mult))
                    link(V.tensor_tensor(w2s, w, w, ALU.mult))
                    link(V.tensor_scalar(pl, w2s, 1.0 / 17, 1.0 / 15, ALU.mult, ALU.add))
                    for odd in (13, 11, 9, 7, 5, 3, 1):
                        link(V.tensor_tensor(pl, pl, w2s, ALU.mult))
                        link(V.tensor_scalar(pl, pl, 1.0 / odd, None, ALU.add))
                    link(V.tensor_tensor(pl, pl, w, ALU.mult))
                    link(V.tensor_scalar(w, lam, -1.0, 0.0, ALU.mult, ALU.max))
                    link(V.scalar_tensor_tensor(pl, pl, 2.0, w, ALU.mult, ALU.add))
                    V.tensor_scalar(small[:, 160:176], pl, RG_C, None, ALU.mult).then_inc(sp_ready, 1)
                    V.tensor_scalar(small[:, 176:192], pl, -RG_C, None, ALU.mult).then_inc(sp_ready, 1)

            dve.wait_ge(rope_sin, 2)
            for n in range(28):
                dve.wait_ge(swapped, n + 1)
                link(V.tensor_tensor(rot[:, 0, :], ps[:, 6 + n % 2, 0:T], rope_s, ALU.mult))
                link(V.tensor_tensor(rot[:, 1, :], raw[:, n % 2, :], rope_c, ALU.mult))
                V.tensor_tensor(qk[:, n, :], rot[:, 0, :], rot[:, 1, :], ALU.add).then_inc(qk_ready, 1)
                dve.wait_ge(qk_ready, n + 1)
                between(n)
            dve.wait_ge(chunk_done, START["gates"])
            for b in range(4):
                c0, cn = (b % 2) * 512, (512, 256)[b % 2]
                V.tensor_copy(vd[:, b // 2, c0:c0 + cn], ps[:, 4 + b, 0:cn]).then_inc(v_copied, 1)

            def da_max(hd):
                dve.wait_ge(da_scores, hd + 1)
                o = 8 * (hd % 2)
                link(V.tensor_reduce(small[:, 48 + o:52 + o], ps[:, 2 * (hd % 2):2 * (hd % 2) + 2, :].rearrange("p c (q k) -> p c q k", q=2), AX.X, ALU.max, negate=True))
                V.tensor_scalar(small[:, 64 + o:68 + o], small[:, 48 + o:52 + o], DH ** -0.5, None, ALU.mult).then_inc(da_nbias, 1)

            def da_mix(hd):
                dve.wait_ge(da_exp, 4 * (hd + 1))
                o = 80 + 8 * (hd % 2)
                link(V.reciprocal(small[:, o:o + 4], small[:, o:o + 4]))
                link(V.tensor_scalar(small[:, o + 2:o + 4], small[:, o + 2:o + 4], small[:, 7:8], None, ALU.mult))
                if hd >= 2:
                    dve.wait_ge(da_turned, hd - 1)
                for q in range(2):
                    link(V.tensor_scalar(da_t[:, q, :], da_p[:, hd % 2, 2 + q, :], small[:, o + 2 + q:o + 3 + q], None, ALU.mult))
                    V.scalar_tensor_tensor(da_a[:, hd % 2, q, :], da_p[:, hd % 2, q, :], small[:, o + q:o + q + 1], da_t[:, q, :], ALU.mult, ALU.add).then_inc(da_mixed, 1)

            def da_take(hd):
                dve.wait_ge(da_out, hd + 1)
                V.tensor_copy(ot[:, hd, :], ps[:, 7, 0:T]).then_inc(ot_ready, 1)

            da_max(0)
            for hd in range(DA_H):
                if hd + 1 < DA_H:
                    da_max(hd + 1)
                da_mix(hd)
                if hd:
                    da_take(hd - 1)
            da_take(DA_H - 1)
            dve.wait_ge(da_mixed, 2 * DA_H)
            dve.wait_ge(loaded_mask, 16)
            for j in range(DIL_H):
                dve.wait_ge(dl_scores, j + 1)
                if j:
                    dve.wait_ge(dl_turned, j)
                for g in range(3):
                    link(V.tensor_tensor(dl_p[:, g, :, :], ps[:, g, :].rearrange("p (q k) -> p q k", q=2), mask[:, g, :, :], ALU.add))
                for q in range(2):
                    link(V.tensor_reduce(small[:, 98 + q:99 + q], dl_p[:, :, q, :], AX.XY, ALU.max, negate=True))
                V.tensor_scalar(small[:, 100:102], small[:, 98:100], DH ** -0.5, None, ALU.mult).then_inc(dl_nbias, 1)
                dve.wait_ge(dl_exp, 2 * (j + 1))
                link(V.reciprocal(small[:, 106:108], small[:, 104:106]))
                for q in range(2):
                    V.tensor_scalar(dl_p[:, :, q, :], dl_p[:, :, q, :], small[:, 106 + q:107 + q], None, ALU.mult).then_inc(dl_prob, 1)
                dve.wait_ge(dl_out, j + 1)
                r0 = DH * (j % 2)
                V.tensor_copy(odt[r0:r0 + DH, j // 2, :], ps[r0:r0 + DH, 7, 0:T]).then_inc(od_ready, 1)
            dve.wait_ge(sub_sum, 1)
            f = (1.0 - LAMBDA_INIT) ** -2
            V.tensor_scalar(srstd[:, :, :], ps[:, 0:4, :].rearrange("p b (n t) -> p (b n) t", t=T), f / P, f * EPS, ALU.mult, ALU.add).then_inc(sub_var, 1)
            dve.wait_ge(sub_std, 1)
            link(V.reciprocal(srstd[:, :, :], srstd[:, :, :]))
            for hd in range(DA_H):
                V.scalar_tensor_tensor(oa[:, hd, :], ot[:, hd, :], col("g_subln"), srstd[:, hd, :], ALU.mult, ALU.mult).then_inc(oa_ready, 1)
            dve.wait_ge(sg_ready, 1)
            dve.wait_ge(chunk_done, START["proj_a"])
            for n in range(KT):
                dve.wait_ge(chunk_done, START["proj_a"] + n + 1)
                link(V.tensor_tensor(rot[:, 0, :], acc(n), sg[:, 8 + n, :], ALU.mult))
                link(V.tensor_tensor(rot[:, 1, :], ps[:, 4 + n % 2, 0:T], sg[:, n, :], ALU.mult))
                V.tensor_tensor(merged[:, n, :], rot[:, 0, :], rot[:, 1, :], ALU.add).then_inc(merged_ready, 1)
                dve.wait_ge(merged_ready, n + 1)
            norm_out(3, NORMS[3], False)
            norm_in(4, NORMS[4], lambda k: real(x, k), lambda k: real(h, k), T)
            input_lo(1, ffn_h)
            ffn(1, START["ffn2"])
            norm_out(5, NORMS[5], True)
            norm_in(6, NORMS[6], lambda k: x[:, k, :], lambda k: h[:, k, :], L)

            for n in range(RT):
                dve.wait_ge(in2_copied, n + 1)
                for d in range(2):
                    w = [col("rg_conv_w_2", (4 * d + j) * RT + n) for j in range(4)]
                    dst = xc[d][:, n, :]
                    src = rgx[:, n, :] if d == 0 else rgx[:, n, NM:L]
                    link(V.tensor_scalar(dst, src, w[0], col("rg_conv_b_2", d * RT + n), ALU.mult, ALU.add))
                    for j in range(1, 4):
                        if d == 0:
                            link(V.scalar_tensor_tensor(dst[:, j:L], rgx[:, n, 0:L - j], w[j], dst[:, j:L], ALU.mult, ALU.add))
                        else:
                            ins = V.scalar_tensor_tensor(dst[:, 0:T - j], rgx[:, n, NM + j:L], w[j], dst[:, 0:T - j], ALU.mult, ALU.add)
                            if j < 3:
                                link(ins)
                ins.then_inc(rg_conv, 1)
            for n in range(12):
                dve.wait_ge(chunk_done, START["hyena"] + n + 1)
                src = ps[:, 4 + n % 2, :]
                part = (2, 1, 0)[n // 4] * HYT + n % 4
                w = [col("hy_conv_w_2", j * 12 + part) for j in range(3)]
                link(V.tensor_scalar(hu[:, n, :], src[:, 0:L], w[1], col("hy_conv_b_2", part), ALU.mult, ALU.add))
                link(V.scalar_tensor_tensor(hu[:, n, 1:L], src[:, 0:L - 1], w[0], hu[:, n, 1:L], ALU.mult, ALU.add))
                V.scalar_tensor_tensor(hu[:, n, 0:L - 1], src[:, 1:L], w[2], hu[:, n, 0:L - 1], ALU.mult, ALU.add).then_inc(hy_conv, 1)
            dve.wait_ge(hy_conv, 12)
            for c in range(HYT):
                V.tensor_tensor(hu[:, c, :], hu[:, c, :], hu[:, 4 + c, :], ALU.mult).then_inc(vx_ready, 1)
            for d in range(2):
                dve.wait_ge(rg_tanh, RT * (d + 1))
                den = i_tmp(d)
                link(V.tensor_scalar(den, m_g[d][:, :, :], 1.0, None, ALU.add))
                link(V.reciprocal(den, den))
                V.scalar_tensor_tensor(m_g[d][:, :, :], m_g[d][:, :, :], 2.0, den, ALU.mult, ALU.mult).then_inc(rg_den, 1)
                dve.wait_ge(rg_den, d + 1)
            dve.wait_ge(decay_ready, 2 * RT)
            for d in range(2):
                dve.wait_ge(rg_sqrt, d + 1)
                f0 = 0 if d == 0 else T - 1
                link(V.memset(m_g[d][:, :, f0:f0 + 1], 1.0))
                link(V.tensor_tensor(i_g[d][:, :, :], i_g[d][:, :, :], xc[d][:, :, :], ALU.mult))
                link(V.tensor_tensor(i_g[d][:, :, :], i_g[d][:, :, :], m_g[d][:, :, :], ALU.mult))
                for t in range(RT):
                    a, b, o = r_g[d][:, t, :], i_g[d][:, t, :], m_g[d][:, t, :]
                    if d:
                        a, b, o = a[:, ::-1], b[:, ::-1], o[:, ::-1]
                    link(V.tensor_tensor_scan(o, a, b, 0.0, ALU.mult, ALU.add))
            link(V.tensor_tensor(m_g[1][:, :, :], m_g[1][:, :, :], m_g[0][:, :, NM:L], ALU.add))
            dve.wait_ge(in2_copied, RT + 4 * RT + RT)
            V.tensor_tensor(gg[:, :, :], gg[:, :, :], m_g[1][:, :, :], ALU.mult).then_inc(rg_ready, 1)
            for n, (f0, fn) in enumerate(LT):
                dve.wait_ge(spec_ready, n + 1)
                ure, uim = ps[0:fn, 0, :], ps[0:fn, 1, :]
                link(V.tensor_tensor(ys[0:fn, n, 0, :], ure, kre[0:fn, n, :], ALU.mult))
                link(V.tensor_tensor(ys[0:fn, n, 1, :], ure, kim[0:fn, n, :], ALU.mult))
                link(V.tensor_tensor(tmp_spec(fn, 0), uim, kim[0:fn, n, :], ALU.mult))
                link(V.tensor_tensor(tmp_spec(fn, 1), uim, kre[0:fn, n, :], ALU.mult))
                V.tensor_tensor(ys[0:fn, n, 0, :], ys[0:fn, n, 0, :], tmp_spec(fn, 0), ALU.subtract).then_inc(ys_ready, 1)
                V.tensor_tensor(ys[0:fn, n, 1, :], ys[0:fn, n, 1, :], tmp_spec(fn, 1), ALU.add).then_inc(ys_ready, 1)
                dve.wait_ge(ys_ready, 2 * n + 2)
            for c in range(HYT):
                dve.wait_ge(conv_out, c + 1)
                link(V.scalar_tensor_tensor(hu[:, 4 + c, 0:T], hu[:, c, NM:L], col("hy_skip_2", c), ps[:, 2 + c % 2, 0:T], ALU.mult, ALU.add))
                V.tensor_tensor(hu[:, 4 + c, 0:T], hu[:, 4 + c, 0:T], hu[:, 8 + c, NM:L], ALU.mult).then_inc(hy_ready, 1)
            dve.wait_ge(in2_copied, RT + 4 * RT + RT + 16)
            for n in range(KT):
                dve.wait_ge(chunk_done, START["rgout"] + n + 1)
                link(V.tensor_tensor(tmp_mix(0), acc(n), sgl[:, n, :], ALU.mult))
                link(V.tensor_tensor(tmp_mix(1), ps[:, 4 + n % 2, 0:T], sgl[:, 8 + n, :], ALU.mult))
                V.tensor_tensor(merged2[:, n, :], tmp_mix(0), tmp_mix(1), ALU.add).then_inc(merged2_ready, 1)
                dve.wait_ge(merged2_ready, n + 1)
            for n in range(KT):
                dve.wait_ge(chunk_done, START["out2"] + n + 1)
                V.tensor_tensor(real(x, n), real(x, n), ps[:, 4 + n % 2, 0:T], ALU.add).then_inc(x_ready, 1)
            dve.wait_ge(x_ready, 32)

            norm_in(7, NORMS[7], lambda k: real(x, k), lambda k: real(h, k), T)
            dve.wait_ge(chunk_done, START["keys"])
            for k in range(KT):
                dve.wait_ge(h_hi, 2 * KT + k + 1)
                V.tensor_tensor(peer_h[1][:, k, NM:L], real(h, k), peer_h[0][:, k, 0:T].bitcast(F32), ALU.subtract).then_inc(h_lo, 1)
            tiu = ti.bitcast(U32)
            ciu = ci.bitcast(U32)

            def top16(vals, idx, src, scratch):
                link(V.max(vals[:, 0:8], src))
                V.max_index(idx[:, 0:8], vals[:, 0:8], src)
                link(V.match_replace(scratch, vals[:, 0:8], src, -3.0e38))
                link(V.max(vals[:, 8:16], scratch))
                link(V.max_index(idx[:, 8:16], vals[:, 8:16], scratch))

            for t in range(2):
                for n in range(16):
                    if n % 4 == 0:
                        dve.wait_ge(sc_copied, 4 * t + n // 4 + 1)
                    top16(tv[:, t, n, :], tiu[:, t, n, :], sc[:, t, n, :], scr[:, 0:NK])
                link(V.tensor_copy(tif[:, t, :, :], tiu[:, t, :, :]))
                pair = tv[:, t, :, :].rearrange("p (h c) k -> p h c k", c=2)
                link(V.tensor_tensor(cand[:, t, :, :].rearrange("p h (i j) -> p h i j", i=TOPK),
                                     pair[:, :, 0, :].unsqueeze(3).to_broadcast([P, PH, TOPK, TOPK]),
                                     pair[:, :, 1, :].unsqueeze(2).to_broadcast([P, PH, TOPK, TOPK]), ALU.add))
                for n in range(PH):
                    top16(cv[:, t, n, :], ciu[:, t, n, :], cand[:, t, n, :], scr)
                V.tensor_tensor(ew[:, 2, t, :].rearrange("p (h k) -> p h k", k=TOPK), cv[:, t, :, :],
                                cv[:, t, :, 0:1].to_broadcast([P, PH, TOPK]), ALU.subtract).then_inc(cv_ready, 1)
            dve.wait_ge(iota_ready, 3)
            cijb = cij.bitcast(U32)
            for t in range(2):
                flat = ciu[:, t, :, :].rearrange("p h k -> p (h k)")
                link(V.tensor_scalar(cijb[:, t, 0, :], flat, 4, None, ALU.logical_shift_right))
                link(V.tensor_scalar(cijb[:, t, 1, :], flat, 15, None, ALU.bitwise_and))
                link(V.tensor_copy(cijf[:, t, :, :], cijb[:, t, :, :]))
                for c in range(2):
                    link(V.tensor_tensor(hot, cijf[:, t, c, :].unsqueeze(2).to_broadcast([P, PH * TOPK, TOPK]),
                                         io16.unsqueeze(1).to_broadcast([P, PH * TOPK, TOPK]), ALU.is_equal))
                    keyf = tif[:, t, :, :].rearrange("p (h c) k -> p h c k", c=2)[:, :, c, :]
                    link(V.tensor_tensor(hot.rearrange("p (h k) i -> p h k i", k=TOPK), hot.rearrange("p (h k) i -> p h k i", k=TOPK),
                                         keyf.unsqueeze(2).to_broadcast([P, PH, TOPK, TOPK]), ALU.mult))
                    link(V.tensor_reduce(ew[:, c, t, :], hot, AX.X, ALU.add))
            dve.wait_ge(ce_ready, 1)
            wts = ew[:, 2, :, :].rearrange("p t (h k) -> p (t h) k", k=TOPK)
            link(V.tensor_reduce(small[:, 208:224], wts, AX.X, ALU.add))
            link(V.reciprocal(small[:, 208:224], small[:, 208:224]))
            V.tensor_tensor(wts, wts, small[:, 208:224].unsqueeze(2).to_broadcast([P, 2 * PH, TOPK]), ALU.mult).then_inc(ew_ready, 1)
            for n, dst in enumerate((e1t, e2t, gt)):
                dve.wait_ge(ew_turned, n + 1)
                V.tensor_copy(dst, ps[:, 1 + n, 0:T]).then_inc(ewt_ready, 1)
            dve.wait_ge(ewt_ready, 3)

            def rows(q, i=0, step=0):
                if q >= 4:
                    dve.wait_ge(g_token, i * step + (q - 3) if step else q - 3)
                t = bass.ds(i * (4 * step) + 4 * q, 4) if step else slice(4 * q, 4 * q + 4)
                row = iota.unsqueeze(1).to_broadcast([P, 4, NK])
                V.tensor_tensor(sel_b[:, q % 4, :, :], row, e2t[:, t].unsqueeze(2).to_broadcast([P, 4, NK]), ALU.is_equal)
                V.tensor_tensor(sel_a[:, q % 4, :, :], row, e1t[:, t].unsqueeze(2).to_broadcast([P, 4, NK]), ALU.is_equal).then_inc(ab_raw, 1)

            def gate_first(q, i=0, step=0):
                dve.wait_ge(g_copied, i * step + (q + 1) if step else q + 1)
                t = bass.ds(i * (4 * step) + 4 * q, 4) if step else slice(4 * q, 4 * q + 4)
                V.tensor_tensor(gates_all[:, 0:NA, t], ps[:, 4 + q % 4, :].rearrange("p (t e) -> p e t", t=4)[:, 0:NA, :], gates_all[:, 0:NA, t], ALU.mult).then_inc(g_gated, 1)

            for q in range(4):
                rows(q)
            dve.wait_ge(gelu_ready, NA)
            with dve.Fori(0, QUADS // 4 - 1) as i:
                for m in range(4):
                    rows(m + 4, i, 4)
                    gate_first(m, i, 4)
            for q in range(QUADS - 4, QUADS):
                gate_first(q)
            base = START["experts"]
            dve.wait_ge(g_gated, QUADS)

            def first_key(e, buf, i=0):
                n = base + NA + e - 1
                if e >= 2:
                    dve.wait_ge(chunk_done, i * 6 + n)
                tile = gates_all[:, bass.ds(i * 6 + e, 1), :].rearrange("p a t -> p (a t)") if e >= 2 else gates_all[:, e, :]
                n = 2 * FT + e + 1
                V.tensor_copy(peer_part[0][:, buf, :], tile).then_inc(act_hi, 1)
                dve.wait_ge(act_hi, i * 6 + n if e >= 2 else n)
                V.tensor_tensor(peer_part[1][:, buf, :], tile, peer_part[0][:, buf, :].bitcast(F32), ALU.subtract).then_inc(peer_act, 1)

            def last_first_key(e):
                dve.wait_ge(chunk_done, base + NA + e - 1)
                V.tensor_copy(peer_part[0][:, e % 2, :], gates_all[:, e, :]).then_inc(act_hi, 1)
                dve.wait_ge(act_hi, 2 * FT + e + 1)
                V.tensor_tensor(peer_part[1][:, e % 2, :], gates_all[:, e, :], peer_part[0][:, e % 2, :].bitcast(F32), ALU.subtract).then_inc(peer_act, 1)

            first_key(0, 0)
            first_key(1, 1)
            with dve.Fori(0, NA // 6 - 1) as i:
                for m in range(2, 8):
                    first_key(m, m % 2, i)
            for e in range(NA - 4, NA):
                last_first_key(e)

            def expert(tile, n, buf):
                dve.wait_ge(gelu_ready, n)
                V.tensor_tensor(act_p[:, buf, :], ge_p[:, buf, :], tile, ALU.mult).then_inc(act_gated, 1)
                dve.wait_ge(act_gated, n + (2 * FT - NA))
                V.tensor_copy(peer_part[0][:, buf, :], act_p[:, buf, :]).then_inc(act_hi, 1)
                dve.wait_ge(act_hi, n + 2 * FT)
                V.tensor_tensor(peer_part[1][:, buf, :], act_p[:, buf, :], peer_part[0][:, buf, :].bitcast(F32), ALU.subtract).then_inc(peer_act, 1)

            def expert_lo(r, i=None):
                down_lo(r, HI_EXPERTS + r + 1 if i is None else i * 12 + (HI_EXPERTS + r + 1), r % NX, peer_w)

            for e in (NA, NA + 1):
                dve.wait_ge(chunk_done, base + NA + e - 1)
                expert(gates_all[:, e, :], e + 1, e % 2)
                if e == NA:
                    dve.wait_ge(lo_down, DOWN_EXPERTS + NA)
                    expert_lo(expert_v(NA))
            with dve.Fori(0, N_PAIRS) as i:
                for m in range(2, 8):
                    expert_lo(expert_v(NA + m - 1), i)
                    dve.wait_ge(chunk_done, i * 12 + (base + expert_v(NA + m - 2) + 1))
                    expert(gates_all[:, bass.ds(i * 6 + (NA + m), 1), :].rearrange("p a t -> p (a t)"), i * 6 + (NA + m + 1), m % 2)
            expert_lo(2 * NK - 1)
            dve.wait_ge(chunk_done, N_CHUNKS)
            for n in range(KT):
                V.tensor_tensor(real(x, n), real(x, n), acc(n), ALU.add).then_inc(x_ready, 1)
            dve.wait_ge(x_ready, 40)
            norm_in(8, NORMS[8], lambda k: real(x, k), lambda k: real(h, k), T)

        @block.tensor
        def _(pe):
            M = nc.tensor.matmul

            def land(c):
                pe.wait_ge(landed[c % NS], 16 * (c // NS + 1))

            def tile(c, out, rhs, nk=KT, slot_cols=0):
                land(c)
                for k in range(nk):
                    ins = M(out, ring[:, c % NS, slot_cols + k * P:slot_cols + (k + 1) * P], rhs(k), start=(k == 0), stop=(k == nk - 1))
                return ins

            def product(out, w, cols_at, act_hl, start, stop):
                hi, lo = w[0][:, cols_at:cols_at + P], w[1][:, cols_at:cols_at + P]
                M(out, hi, act_hl[0], start=start, stop=False, skip_group_check=True)
                M(out, hi, act_hl[1], start=False, stop=False, skip_group_check=True)
                return M(out, lo, act_hl[0], start=False, stop=stop, skip_group_check=True)

            def sums(n, w):
                if n:
                    pe.wait_ge(var_ready, n)
                for k in range(KT):
                    pe.wait_ge(sq_ready, KT * n + k + 1)
                    ins = M(ps[:, 6, 0:w], ones, sq[:, k, 0:w], start=(k == 0), stop=(k == KT - 1))
                ins.then_inc(ssq_ready, 1)

            pe.wait_ge(loaded_vec, 16 * 3)
            sums(0, T)

            def ffn(f, base):
                def first(j, buf, i=None):
                    r = ffn_up(0, j) - 1
                    for half in range(2):
                        n = f * 2 * FT + 2 * j + half + 1
                        pe.wait_ge(lo_up, n if i is None else i * 4 + n)
                        for k in range(KT):
                            if j == 0 and half == 0:
                                pe.wait_ge(h_lo, f * KT + k + 1)
                            ins = product(ps[:, 4 + buf, half * T:(half + 1) * T], ffn_w[(r + half) % NW], k * P, (ffn_h[0][:, k, :], ffn_h[1][:, k, :]), k == 0, k == KT - 1)
                        ins.then_inc(chunk_done, 1)

                def second(j, buf, begin, end, i=None):
                    r = ffn_down(0, j)
                    n = f * FT + j + 1
                    pe.wait_ge(lo_down, n if i is None else i * 2 + n)
                    for t in range(KT):
                        ins = product(acc(t), ffn_w[r % NW], t * P, (ffn_act[0][:, buf, :], ffn_act[1][:, buf, :]), begin and t % 2 == 0, end)
                    ins.then_inc(chunk_done, 1)

                first(0, 0)
                first(1, 1)
                pe.wait_ge(act_ready, f * FT + 1)
                second(0, 0, True, False)
                with pe.Fori(0, (FT - 2) // 2) as i:
                    for m in (2, 3):
                        pe.wait_ge(act_ready, i * 2 + (f * FT + m - 1))
                        first(m, m % 2, i)
                        pe.wait_ge(act_ready, i * 2 + (f * FT + m))
                        second(m - 1, (m - 1) % 2, False, False, i)
                pe.wait_ge(act_ready, f * FT + FT)
                second(FT - 1, (FT - 1) % 2, False, True)

            ffn(0, START["ffn1"])
            sums(1, T)
            sums(2, T)
            pe.wait_ge(h_ready, 16)

            def swap_tile(n):
                pe.wait_ge(raw_copied, n + 1)
                if n >= 2:
                    pe.wait_ge(qk_ready, n - 1)
                if n == 0:
                    pe.wait_ge(var_ready, 3)
                M(ps[:, 6 + n % 2, 0:T], swap, raw[:, n % 2, :], start=True, stop=True).then_inc(swapped, 1)

            def between(n):
                if n == 2:
                    pe.wait_ge(loaded_const, 16 * N_CONST)
                    pe.wait_ge(iota_ready, 1)
                    M(ps[0:FW, 1, 0:L], w1[0:2 * HB + 1, :], zt[0:2 * HB + 1, :], start=True, stop=True).then_inc(flt_pe, 1)
                if n == 5:
                    pe.wait_ge(flt_sin, 1)
                    M(ps[0:FW, 1, 0:L], w2[0:FW, :], hdn[0:FW, :], start=True, stop=True).then_inc(flt_pe, 1)
                if n in (8, 11, 14):
                    m = (n - 8) // 3
                    t0, tn = LT[m]
                    if m:
                        pe.wait_ge(flt_k, 2 * m)
                    else:
                        pe.wait_ge(flt_sin, 2)
                    for d in range(2):
                        ins = M(ps[0:tn, 1 + d, :], hdn[0:FW + 1, t0:t0 + tn], w3[0:FW + 1, d * HY:(d + 1) * HY], start=True, stop=True)
                    ins.then_inc(flt_pe, 1)
                if n in (17, 20, 23):
                    m = (n - 17) // 3
                    f0, fn = LT[m]
                    pe.wait_ge(flt_k, 6 + 2 * m)
                    for d, src in ((0, ksum), (1, kdif)):
                        for k, (t0, tn) in enumerate(LT):
                            ins = M(ps[0:fn, 1 + d, :], dft[0:tn, k, d, f0:f0 + fn], src[0:tn, k, :], start=(k == 0), stop=(k == 2))
                    ins.then_inc(flt_pe, 1)

            pe.wait_ge(lam_prod, 2)
            M(ps[:, 0, 0:2], ones, small[:, 0:2], start=True, stop=True).then_inc(lam_sum, 1)
            for n in range(28):
                if n >= 2:
                    pe.wait_ge(raw_copied, n - 1)
                tile(START["qk"] + n, ps[:, 4 + n % 2, 0:T], lambda k: real(h, k)).then_inc(chunk_done, 1)
                if n:
                    swap_tile(n - 1)
                between(n)
            swap_tile(27)
            pe.wait_ge(flt_k, 12)
            pe.wait_ge(lam_exp, 1)
            for name, width, b0 in (("va", D, 0), ("vd", 3 * DIL_H * DH, 4)):
                if b0:
                    pe.wait_ge(qk_ready, 28)
                for k in range(KT):
                    c = START[name] + k
                    land(c)
                    for t in range(2):
                        for n in range(2):
                            w = min(512, width - 512 * n)
                            ins = M(ps[:, b0 + 2 * t + n, 0:w], h[:, k, NM + t * P:NM + (t + 1) * P], ring[:, c % NS, n * 512:n * 512 + w], start=(k == 0), stop=(k == KT - 1))
                    ins.then_inc(chunk_done, 1)
            pe.wait_ge(v_copied, 8)

            def da_score(hd):
                if hd >= 2:
                    pe.wait_ge(da_exp, 4 * (hd - 1))
                for c in range(2):
                    r0 = DH * c
                    for q in range(2):
                        ins = M(ps[:, 2 * (hd % 2) + c, q * T:(q + 1) * T], qk[r0:r0 + DH, hd, q * P:(q + 1) * P], qk[r0:r0 + DH, 8 + hd, :], start=True, stop=True)
                ins.then_inc(da_scores, 1)

            def gate_tile(n):
                if n >= 2:
                    pe.wait_ge(gate_copied, n - 1 if n < DA_H else n)
                tile(START["gates"] + n, ps[:, 4 + n % 2 if n < DA_H else 6, 0:T], lambda k: real(h, k)).then_inc(chunk_done, 1)

            da_score(0)
            for hd in range(DA_H):
                if hd + 1 < DA_H:
                    da_score(hd + 1)
                gate_tile(hd)
                pe.wait_ge(da_mixed, 2 * (hd + 1))
                if hd:
                    pe.wait_ge(da_tcopied, hd)
                for kt in range(2):
                    for q in range(2):
                        ins = nc.tensor.transpose(ps[:, 6, kt * T + q * P:kt * T + (q + 1) * P], da_a[:, hd % 2, q, kt * P:(kt + 1) * P], ident)
                ins.then_inc(da_turned, 1)
                pe.wait_ge(da_tcopied, hd + 1)
                if hd:
                    pe.wait_ge(ot_ready, hd)
                for kt in range(2):
                    ins = M(ps[:, 7, 0:T], va[:, kt, hd * P:(hd + 1) * P], da_at[:, hd % 2, kt * T:(kt + 1) * T], start=(kt == 0), stop=(kt == 1))
                ins.then_inc(da_out, 1)
            pe.wait_ge(gate_copied, DA_H)
            pe.wait_ge(ot_ready, DA_H)
            for j in range(DIL_H):
                r0 = DH * (j % 2)
                if j:
                    pe.wait_ge(dl_nbias, j)
                for g in range(3):
                    n = (DIL_H * g + j) // 2
                    for q in range(2):
                        ins = M(ps[:, g, q * T:(q + 1) * T], qk[r0:r0 + DH, 16 + n, q * P:(q + 1) * P], qk[r0:r0 + DH, 22 + n, :], start=True, stop=True)
                ins.then_inc(dl_scores, 1)
                gate_tile(DA_H + 2 * j)
                pe.wait_ge(dl_prob, 2 * (j + 1))
                if j:
                    pe.wait_ge(dl_tcopied, j)
                for g in range(3):
                    for kt in range(2):
                        for q in range(2):
                            ins = nc.tensor.transpose(ps[:, 3 + g, kt * T + q * P:kt * T + (q + 1) * P], dl_p[:, g, q, kt * P:(kt + 1) * P], ident)
                ins.then_inc(dl_turned, 1)
                gate_tile(DA_H + 2 * j + 1)
                pe.wait_ge(dl_tcopied, j + 1)
                if j:
                    pe.wait_ge(od_ready, j)
                for n in range(6):
                    g, kt = n // 2, n % 2
                    at = (DIL_H * g + j) * DH
                    ins = M(ps[r0:r0 + DH, 7, 0:T], vd[:, kt, at:at + DH], dl_pt[:, g, kt, :], start=(n == 0), stop=(n == 5))
                ins.then_inc(dl_out, 1)
            for hd in range(DA_H):
                pe.wait_ge(sub_sq, hd + 1)
                ins = M(acc(hd), ones, sq[:, hd, 0:T], start=True, stop=True)
            ins.then_inc(sub_sum, 1)
            pe.wait_ge(od_ready, DIL_H)
            pe.wait_ge(sub_var, 1)
            for n in range(KT):
                c = START["proj_b"] + n // 4
                ins = tile(c, acc(n), lambda k: odt[:, k, :], nk=2, slot_cols=(n % 4) * 2 * P)
                if n % 4 == 3:
                    ins.then_inc(chunk_done, 1)
            pe.wait_ge(oa_ready, DA_H)
            for n in range(KT):
                if n >= 2:
                    pe.wait_ge(merged_ready, n - 1)
                tile(START["proj_a"] + n, ps[:, 4 + n % 2, 0:T], lambda k: oa[:, k, :]).then_inc(chunk_done, 1)
            pe.wait_ge(merged_ready, KT)
            for n in range(KT):
                tile(START["out1"] + n, acc(n), lambda k: merged[:, k, :]).then_inc(chunk_done, 1)
            sums(3, T)
            sums(4, T)
            ffn(1, START["ffn2"])
            sums(5, T)
            sums(6, L)

            pe.wait_ge(h_ready, 32)
            for n in range(RT):
                if n >= 2:
                    pe.wait_ge(in2_copied, n - 1)
                tile(START["rgx"] + n, ps[:, 4 + n % 2, 0:L], lambda k: h[:, k, :]).then_inc(chunk_done, 1)
            pe.wait_ge(in2_copied, RT)
            for n in range(12):
                if n >= 2:
                    pe.wait_ge(hy_conv, n - 1)
                tile(START["hyena"] + n, ps[:, 4 + n % 2, 0:L], lambda k: h[:, k, :]).then_inc(chunk_done, 1)
            pe.wait_ge(rg_conv, RT)
            pe.wait_ge(hy_conv, 12)
            for d in range(2):
                w = L if d == 0 else T
                for g in range(2):
                    c = START["rggate"] + 2 * d + g
                    land(c)
                    for t in range(RT):
                        n = (2 * d + g) * RT + t
                        if n >= 2:
                            pe.wait_ge(in2_copied, RT + n - 1)
                        M(ps[:, 4 + n % 2, 0:w], ring[:, c % NS, t * P:(t + 1) * P], xc[d][:, t, :], start=True, stop=True).then_inc(rg_gated, 1)
                    pe.wait_ge(rg_gated, (2 * d + g + 1) * RT)
                    pe.sem_inc(chunk_done, 1)
            pe.wait_ge(vx_ready, HYT)
            for n, (t0, tn) in enumerate(LT):
                for c in range(HYT):
                    ins = nc.tensor.transpose(ps[0:tn, n, c * P:(c + 1) * P], hu[:, c, t0:t0 + tn], ident)
                ins.then_inc(vt_turned, 1)
            pe.wait_ge(in2_copied, 5 * RT)
            for n in range(RT):
                if n >= 2:
                    pe.wait_ge(in2_copied, 5 * RT + n - 1)
                tile(START["rgg"] + n, ps[:, 4 + n % 2, 0:T], lambda k: real(h, k)).then_inc(chunk_done, 1)
            pe.wait_ge(vt_ready, 3)
            for n, (f0, fn) in enumerate(LT):
                if n:
                    pe.wait_ge(ys_ready, 2 * n)
                for d in range(2):
                    for m, (t0, tn) in enumerate(LT):
                        ins = M(ps[0:fn, d, :], dft[0:tn, m, d, f0:f0 + fn], vt[0:tn, m, :], start=(m == 0), stop=(m == 2))
                ins.then_inc(spec_ready, 1)
                if n == 0:
                    for m in range(8):
                        gl_tile(pe, tile, m)
                else:
                    for m in range(8 + 4 * (n - 1), 8 + 4 * n):
                        gl_tile(pe, tile, m)
            pe.wait_ge(ys_ready, 6)
            for c in range(HYT):
                if c >= 2:
                    pe.wait_ge(hy_ready, c - 1)
                for n, (f0, fn) in enumerate(LT):
                    for d in range(2):
                        ins = M(ps[:, 2 + c % 2, 0:T], ys[0:fn, n, d, c * P:(c + 1) * P], idft[0:fn, n, d, :], start=(n == 0 and d == 0), stop=(n == 2 and d == 1))
                ins.then_inc(conv_out, 1)
            pe.wait_ge(hy_ready, HYT)
            for n in range(KT):
                ins = tile(START["hyout"] + n // 2, acc(n), lambda k: hu[:, 4 + k, 0:T], nk=4, slot_cols=(n % 2) * 4 * P)
                if n % 2:
                    ins.then_inc(chunk_done, 1)
            pe.wait_ge(rg_ready, 1)
            pe.wait_ge(in2_copied, 6 * RT + 16)
            for n in range(KT):
                if n >= 2:
                    pe.wait_ge(merged2_ready, n - 1)
                tile(START["rgout"] + n, ps[:, 4 + n % 2, 0:T], lambda k: gg[:, k, :]).then_inc(chunk_done, 1)
            pe.wait_ge(merged2_ready, KT)
            for n in range(KT):
                if n >= 2:
                    pe.wait_ge(x_ready, 24 + n - 1)
                tile(START["out2"] + n, ps[:, 4 + n % 2, 0:T], lambda k: merged2[:, k, :]).then_inc(chunk_done, 1)

            sums(7, T)
            pe.wait_ge(x_ready, 32)
            pe.wait_ge(h_ready, 40)
            for n in range(16):
                if n >= 2:
                    pe.wait_ge(pq_copied, n - 1)
                tile(START["wq"] + n, ps[:, 4 + n % 2, 0:T], lambda k: real(h, k)).then_inc(chunk_done, 1)
            pe.wait_ge(pq_copied, 16)
            pe.wait_ge(var_ready, 8)
            for t in range(2):
                for n in range(16):
                    c = START["keys"] + n // 8
                    land(c)
                    ins = M(ps[:, 4 * t + n // 4, (n % 4) * P:(n % 4 + 1) * P], pq[:, n, t * P:(t + 1) * P], ring[:, c % NS, (n % 8) * P:(n % 8 + 1) * P], start=True, stop=True)
                    if n % 4 == 3:
                        ins.then_inc(sc_out, 1)
            pe.wait_ge(sc_out, 8)
            pe.sem_inc(chunk_done, 2)
            base = START["experts"]

            def first(e, i=0, step=0):
                r = expert_u(e)
                n = UP_EXPERTS + e + 1
                pe.wait_ge(lo_up, i * step + n if step else n)
                for k in range(KT):
                    ins = product(ps[:, 4 + e % 2, 0:T], peer_w[r % NW], k * P, (peer_h[0][:, k, 0:T], peer_h[1][:, k, NM:L]), k == 0, k == KT - 1)
                ins.then_inc(chunk_done, 1)

            def second(e, begin=False, end=False, i=0, step=0):
                r = expert_v(e)
                n = DOWN_EXPERTS + e + 1
                pe.wait_ge(lo_down, i * step + n if step else n)
                pe.wait_ge(peer_act, i * step + (e + 1) if step else e + 1)
                for t in range(KT):
                    ins = product(acc(t), peer_w[r % NW], t * P, (peer_part[0][:, e % 2, :], peer_part[1][:, e % 2, :]), begin and t % 2 == 0, end)
                ins.then_inc(chunk_done, 1)

            pe.wait_ge(sc_copied, 8)
            pe.wait_ge(h_lo, 3 * KT)
            first(0)
            first(1)
            with pe.Fori(0, NA // 6 - 1) as i:
                for m in range(2, 8):
                    pe.wait_ge(gelu_ready, i * 6 + (m - 1))
                    first(m, i, 6)
            for e in range(NA - 4, NA):
                pe.wait_ge(gelu_ready, e - 1)
                first(e)
            pe.wait_ge(ew_ready, 1)
            for n in range(3):
                for t in range(2):
                    ins = nc.tensor.transpose(ps[:, 1 + n, t * P:(t + 1) * P], ew[:, n, t, :], ident)
                ins.then_inc(ew_turned, 1)
            pe.wait_ge(gelu_ready, NA)

            def four(q, i=0, step=0):
                pe.wait_ge(ab_ready, i * step + (q + 1) if step else q + 1)
                for m in range(4):
                    ins = M(ps[:, 4 + q % 4, m * P:(m + 1) * P], sel_b[:, q % 4, m, :], sel_a[:, q % 4, m, :], start=True, stop=True)
                ins.then_inc(g_token, 1)

            for q in range(4):
                four(q)
            with pe.Fori(0, QUADS // 4 - 1) as i:
                for m in range(4, 8):
                    pe.wait_ge(g_gated, i * 4 + (m - 3))
                    four(m, i, 4)
            pe.wait_ge(g_gated, QUADS)
            second(0, begin=True)
            for e in range(1, 6):
                second(e)
            with pe.Fori(0, NA // 6 - 1) as i:
                for m in range(6, 12):
                    second(m, i=i, step=6)
            first(NA)
            first(NA + 1)
            second(NA)
            with pe.Fori(0, N_PAIRS) as i:
                for m in range(2, 8):
                    pe.wait_ge(gelu_ready, i * 6 + (NA + m - 1))
                    first(NA + m, i, 6)
                    second(NA + m - 1, i=i, step=6)
            second(NK - 1, end=True)
            sums(8, T)


def _by_tile(w, t=P):
    k, n = w.shape
    return w.reshape(k // P, P, n // t, t).transpose(2, 1, 0, 3).reshape(n // t, P, -1)


def _by_row(w):
    return w.reshape(w.shape[0] // P, P, w.shape[1])


def _stream(i):
    def lagged(first, second):
        out = [first[0]]
        for j in range(1, len(second)):
            out += [first[j], second[j - 1][None]]
        return out + [second[-1][None]]

    def mlp(gu, down):
        up = _by_tile(gu)
        return lagged([np.stack([up[j], up[FT + j]]) for j in range(FT)], _by_row(down))

    w = i["w_in"][0]
    cuts = np.cumsum([0, D, D, D, 768, 768, 768, D, D])
    qa, ka, va, qd, kd, vd, ga, gb = (w[:, a:b] for a, b in zip(cuts[:-1], cuts[1:]))
    w2 = i["w_in_2"][0]
    cuts = np.cumsum([0, HY, HY, HY, D, D, 2 * D])
    x0, x1, v, rx, rg, gl = (w2[:, a:b] for a, b in zip(cuts[:-1], cuts[1:]))
    pad = np.zeros((D, D - 768), np.float32)
    u = i["peer_u_2"][0].reshape(NK, NK, KT, P).transpose(0, 3, 2, 1).reshape(NK, P, D)
    vv = i["peer_v_2"][0].reshape(NK, NK, D)
    parts = (
        mlp(i["w_gu1"][0], i["w_down1"][0])
        + [_by_tile(m) for m in (qa, ka, qd, kd)]
        + [_by_row(va), _by_row(np.concatenate([vd, pad], 1)), _by_tile(ga), _by_tile(gb)]
        + [_by_tile(i["w_proj_b"][0]).reshape(2, 4, P, 2 * P).transpose(0, 2, 1, 3).reshape(2, P, CW)]
        + [_by_tile(i["w_proj_a"][0]), _by_tile(i["w_out"][0])]
        + mlp(i["w_gu2"][0], i["w_down2"][0])
        + [_by_tile(m) for m in (rx, v, x1, x0)]
        + [i["rg_gate_w_2"][0].transpose(0, 1, 3, 2, 4).reshape(4, P, CW)]
        + [_by_tile(rg), _by_tile(gl)]
        + [_by_tile(i["hy_out_2"][0]).reshape(4, 2, P, 4 * P).transpose(0, 2, 1, 3).reshape(4, P, CW)]
        + [_by_tile(i["rg_out_2"][0]), _by_tile(i["w_out_2"][0]), _by_tile(i["peer_wq_2"][0])]
        + [i["peer_keys_2"][0].reshape(2, 8, NK, P).transpose(0, 3, 1, 2).reshape(2, P, CW)]
        + [u[:NA], vv[:NA]] + lagged(list(u[NA:, None]), vv[NA:])
    )
    out = np.concatenate(parts, 0)
    assert out.shape == (N_CHUNKS, P, CW), out.shape
    return out


def _columns(i):
    d = np.arange(P) % DH
    inv = (np.float32(THETA) ** (-(np.arange(0, ROT, 2, dtype=np.float32) / np.float32(ROT)))).astype(np.float32)
    table = {
        "rope_inv": np.where(d < ROT, inv[d % (ROT // 2)], 0).astype(np.float32),
        "rope_sign": np.where(d < ROT // 2, -1, 1).astype(np.float32),
    }
    out = []
    for name, n in COLUMNS:
        a = table[name] if name in table else np.asarray(i[name])
        width = min(P, a.size // n)
        c = a.reshape(n, width).T
        if width < P:
            c = np.concatenate([c, np.zeros((P - width, n), np.float32)], 0)
        out.append(c)
    return np.ascontiguousarray(np.concatenate(out, 1))


def _tiled(a):
    out = np.zeros((3 * P,) + a.shape[1:], np.float32)
    out[:L] = a
    return np.ascontiguousarray(np.moveaxis(out.reshape((3, P) + a.shape[1:]), 0, 1))


def _constants():
    f32 = np.float32
    t = np.linspace(0.0, 1.0, L, dtype=f32)[:, None]
    w = (f32(2.0 * math.pi / L) * np.arange(L, dtype=f32))[:, None]
    bands = np.linspace(1e-4, HB - 1, HB, dtype=f32)[None, :]
    z = np.concatenate([t, np.cos(bands * w), -np.sin(bands * w)], 1).astype(f32)
    deltas = np.abs(np.linspace(math.log(1e-2) / 0.3, math.log(1e-2) / 1.5, HY, dtype=f32))
    decay = np.exp(-t * deltas).astype(f32)
    back = decay.copy()
    back[0] = 0.0
    s, f = np.arange(L, dtype=np.float64), np.arange(L, dtype=np.float64) + 0.5
    a = 2.0 * math.pi * np.outer(s, f) / (2 * L)
    dft = np.stack([np.cos(a), -np.sin(a)], 1).astype(f32)
    a = 2.0 * math.pi * np.outer(f, np.arange(NM, L)) / (2 * L)
    idft = (np.stack([np.cos(a), -np.sin(a)], 1) / L).astype(f32)
    q, k = np.arange(T)[:, None], np.arange(T)[None, :]
    mask = []
    for dil, half in DIL:
        seen = ((q - k) % dil == 0) & (abs(q - k) <= half * dil)
        mask.append(np.where(seen, 0.0, NEG * math.sqrt(DH)).astype(f32).reshape(2, P, T).transpose(1, 0, 2))
    swap = np.zeros((P, P), f32)
    d = np.arange(P)
    r = d % DH
    swap[np.where(r < 8, d + 8, np.where(r < ROT, d - 8, d)), d] = 1.0
    sq = np.stack([np.eye(P, dtype=f32), swap, np.ones((P, P), f32)], 1)
    return {"zt": np.ascontiguousarray(z.T), "decay": _tiled(np.stack([decay, back], 1)), "dft": _tiled(dft), "idft": _tiled(idft),
            "mask": np.ascontiguousarray(np.stack(mask, 1)), "squares": np.ascontiguousarray(sq)}


def kernel(**inputs):
    import concourse.bacc as bacc
    from concourse.bass_utils import run_bass_kernel_spmd

    i = {k: np.asarray(v) for k, v in inputs.items()}
    c = _constants()

    def features(a):
        return np.ascontiguousarray(a.T.reshape(KT, P, -1).transpose(1, 0, 2))

    arrays = {
        "x": features(i["x"][0]), "meta": features(i["meta_2"]),
        "positions": np.ascontiguousarray(np.broadcast_to(i["positions"][0], (P, T))),
        "stream": _stream(i), "columns": _columns(i),
        "filter_w1": i["hy_w1_2"][0], "filter_w2": i["hy_w2_2"][0],
        "filter_w3": np.concatenate([i["hy_w3_2"][0], i["hy_b3_2"]], 0),
        "zt": c["zt"], "decay": c["decay"], "dft": c["dft"], "idft": c["idft"], "mask": c["mask"], "squares": c["squares"],
    }
    nc = bacc.Bacc("TRN2", target_bir_lowering=False, num_devices=1)
    args = [nc.dram_tensor(f"in_{n}", a.shape, mybir.dt.from_np(a.dtype), kind="ExternalInput").ap() for n, a in arrays.items()]
    out = nc.dram_tensor("out", (P, KT, T), F32, kind="ExternalOutput").ap()
    build(nc, *args, out)
    r = run_bass_kernel_spmd(nc, [{f"in_{n}": a for n, a in arrays.items()}], core_ids=[0])
    got = r.results[0]["out"]
    return got.transpose(2, 1, 0).reshape(1, T, D)
```

```python
import math
from contextlib import ExitStack

import numpy as np

import concourse.bass as bass
from concourse import mybir

F32 = mybir.dt.float32
F32R = mybir.dt.float32r
I32 = mybir.dt.int32
U32 = mybir.dt.uint32
ALU = mybir.AluOpType
ACT = mybir.ActivationFunctionType
AX = mybir.AxisListType

P = 128
D = 1024
KT = D // P
T = 256
NM = 16
L = T + NM
FF = 2816
FT = FF // P
EPS = 1e-6

DA_H = 8
DH = 64
DIL = ((1, 64), (4, 64), (16, 64))
DIL_H = 4
NEG = -1e30
ROT = 16
THETA = 500000.0
LAMBDA_INIT = 0.8 - 0.6 * math.exp(0.0)

HY = 512
HYT = HY // P
HB = 16
FW = 64
RT = D // P
RG_C = 8.0

PH = 8
NK = 128
NA = 42
TOPK = 16

NS = 6
NW = 3
CW = 1024
STAGES = [
    ("ffn1", 3 * FT), ("qk", 28), ("va", KT), ("vd", KT), ("gates", 16), ("proj_b", 2), ("proj_a", 8),
    ("out1", 8), ("ffn2", 3 * FT), ("rgx", 8), ("hyena", 12), ("rggate", 4), ("rgg", 8), ("gl", 16),
    ("hyout", 4), ("rgout", 8), ("out2", 8), ("wq", 16), ("experts", 2 * NK),
]
START, N_CHUNKS = {}, 0
for _name, _n in STAGES:
    START[_name] = N_CHUNKS
    N_CHUNKS += _n


def _split_plan():
    by, hi, lo, before = [], [], [], []
    made = {"hi": 0, "pool": 0, "dve": 0}
    for name, n in STAGES:
        for r in range(n):
            c = START[name] + r
            who = "pool"
            if name in ("proj_b", "rggate", "hyout"):
                who = None
            elif name in ("ffn1", "ffn2") and (r == n - 1 or r >= 4 and r % 3 == 1):
                who = "dve"
            elif name == "experts" and r >= 2 * NA and (r == n - 1 or r > 2 * NA and r % 2 == 0):
                who = "dve"
            if who:
                made["hi"] += 1
                made[who] += 1
            by.append(who)
            hi.append(made["hi"])
            lo.append(made[who] if who else None)
            same = [b for b in range(c) if by[b] and b % NW == c % NW and (b >= START["experts"]) == (name == "experts")]
            before.append(same[-1] if same else None)
    return by, hi, lo, before


BY, HI, LO, BEFORE = _split_plan()

COLUMNS = [
    ("g_pre_ffn1", 8), ("g_post_ffn1", 8), ("g_pre_mix", 8), ("g_post_mix", 8), ("g_pre_ffn2", 8),
    ("g_post_ffn2", 8), ("g_mix_2", 8), ("g_ffn_2", 8), ("g_final_2", 8), ("g_subln", 1),
    ("b_gate_2", 16), ("hy_conv_w_2", 36), ("hy_conv_b_2", 12), ("hy_skip_2", 4), ("rg_conv_w_2", 64),
    ("rg_conv_b_2", 16), ("rg_gate_b_2", 32), ("rg_lambda_2", 16), ("hy_b1_2", 1), ("hy_b2_2", 1),
    ("hy_freq_2", 2), ("lambda_q1", 1), ("lambda_k1", 1), ("lambda_q2", 1), ("lambda_k2", 1),
    ("rope_inv", 1), ("rope_sign", 1),
]
COL, N_COLS = {}, 0
for _name, _n in COLUMNS:
    COL[_name] = N_COLS
    N_COLS += _n

LT = [(0, P), (P, P), (2 * P, NM)]

NORMS = ["g_pre_ffn1", "g_post_ffn1", "g_pre_mix", "g_post_mix", "g_pre_ffn2", "g_post_ffn2", "g_mix_2",
         "g_ffn_2", "g_final_2"]
TWO_PI = 2.0 * math.pi
ROUND = 1.5 * 2.0 ** 23
PI1 = 6.28125
PI2 = float(np.float32(np.round((TWO_PI - PI1) * 2 ** 21) / 2 ** 21))
PI3 = float(np.float32(TWO_PI - PI1 - PI2))
PI_IN = 3.1415925


def build(nc, x_d, meta_d, pos_d, stream_d, cols_d, w1_d, w2_d, w3_d, zt_d, decay_d, dft_d, idft_d, mask_d, sq_d, keys_d, out_d):
    with ExitStack() as ctx:
        place = {}

        def sb(name, shape, dt=F32):
            place[name] = -(-nc.sbuf_base // 32) * 32
            return ctx.enter_context(nc.sbuf_tensor(name, shape, dt))

        def over(name, under, at, shape):
            return nc.alloc_sbuf_tensor_at(name, shape, dtype=F32R, offset=place[under] + 4 * at)

        def sem(name):
            return ctx.enter_context(nc.semaphore(name))

        ring = sb("ring", [P, NS, CW])
        x = sb("x", [P, KT, L])
        h = sb("h", [P, KT, L])
        sq = sb("sq", [P, KT, L])
        cols = sb("cols", [P, N_COLS])
        square = sb("square", [P, 3, P])
        ident, swap, ones = square[:, 0, :], square[:, 1, :], square[:, 2, :]
        stat = sb("stat", [P, 2, 32])
        rstd_out = sb("rstd_out", [P, T])
        root_t, rstd_t = stat[:, 0, 0:3], stat[:, 1, 0:3]
        sub_root_t, sub_rstd_t = stat[:, 0, 16:32], stat[:, 1, 16:32]
        small = sb("small", [P, 256])
        arena = sb("arena", [P, NK * T])
        aux = sb("aux", [P, 6240])
        HI_AT = NK * T - NW * CW
        main_hi = over("main_hi", "arena", HI_AT, [P, NW, CW])
        ring_lo = over("ring_lo", "ring", 0, [P, NS, CW])
        h_parts = over("h_hi", "sq", 0, [P, KT, L]), over("h_lo", "h", 0, [P, KT, L])
        VALUES_AT, MAPS_AT = 9472, 19712
        oa_parts = over("oa_parts", "arena", VALUES_AT, [P, 2, DA_H, T])
        ffn_part = over("ffn_part", "arena", VALUES_AT + 2 * DA_H * T, [P, 2, 2, T])
        merged_parts = over("merged_parts", "arena", MAPS_AT, [P, 2, KT, T])
        merged2_parts = over("merged2_parts", "arena", RT * (2 * L + T), [P, 2, KT, T])
        gg_parts = over("gg_parts", "arena", RT * (3 * L + 2 * T), [P, 2, RT, T])
        peer_split = over("peer_split", "aux", 0, [P, NW * CW + 4 * T])
        ps = ctx.enter_context(nc.psum_tensor("ps", [P, 8, 512], F32))

        class Space:

            def __init__(self, base, at=0):
                self.base, self.at = base, at

            def take(self, *shape):
                n = int(np.prod(shape))
                piece = self.base[:, self.at:self.at + n]
                self.at += n
                assert self.at <= self.base.shape[1], (self.at, self.base.shape)
                if len(shape) == 2:
                    piece = piece.rearrange("p (a b) -> p a b", a=shape[0])
                if len(shape) == 3:
                    piece = piece.rearrange("p (a b c) -> p a b c", a=shape[0], b=shape[1])
                return piece

        def col(name, n=0):
            at = COL[name] + n
            return cols[:, at:at + 1]

        def split_pair(s, *shape):
            return s.take(*shape), s.take(*shape)

        s = Space(aux)
        kre, kim = s.take(3, HY), s.take(3, HY)
        dft = s.take(3, 2, L)
        idft = s.take(3, 2, T)
        s = Space(aux)
        s.take(CW)
        sel_b, sel_a = s.take(4, 4, NK), s.take(4, 4, NK)
        e1t, e2t, gt = s.take(T), s.take(T), s.take(T)
        iota, io16 = s.take(NK), s.take(TOPK)
        s = Space(aux, NW * CW + 4 * T)
        ge_p, act_p = s.take(2, T), s.take(2, T)
        s = Space(peer_split)
        peer_hi = s.take(NW, CW)
        peer_part = split_pair(s, 2, T)

        s = Space(arena, 20288)
        zt, w1, w2, w3 = s.take(L), s.take(FW), s.take(FW), s.take(2 * HY)
        arg, turn, hdn = s.take(L), s.take(L), s.take(L)
        decay = s.take(3, 2, HY)
        kfb, ksum, kdif = s.take(2, HY), s.take(3, HY), s.take(3, HY)
        assert s.at <= HI_AT
        s = Space(arena)
        rope_c, rope_s = s.take(T), s.take(T)
        posi = s.take(T)
        ang, angq = s.take(T), s.take(T)
        silu, act = s.take(2, T), s.take(2, T)
        first = s.at
        raw, rot = s.take(2, T), s.take(2, T)
        qk = s.take(28, T)
        va, vd = s.take(2, D), s.take(2, 3 * DIL_H * DH)
        sg = s.take(16, T)
        mask = s.take(3, 2, T)
        da_p, da_a, da_t = s.take(2, 4, T), s.take(2, 2, T), s.take(2, T)
        da_at, ot = s.take(2, 2 * T), s.take(DA_H, T)
        dl_p, dl_pt = [s.take(3, 2, T)], s.take(3, 2, T)
        dl_p.append(Space(da_p.rearrange("p a b c -> p (a b c)")).take(3, 2, T))
        assert s.at <= HI_AT
        odt = arena[:, 2 * T:4 * T].rearrange("p (a b) -> p a b", a=2)
        ffn_act = ffn_part[:, 0, :, :], ffn_part[:, 1, :, :]
        s = Space(arena, first + 4 * T)
        oa = s.take(DA_H, T)
        s.take(DA_H, T)
        merged = s.take(KT, T)
        s = Space(arena)
        rgx = s.take(RT, L)
        xc = [s.take(RT, L), s.take(RT, T)]
        r_g = [s.take(RT, L), s.take(RT, T)]
        i_g = [s.take(RT, L), s.take(RT, T)]
        m_g = [s.take(RT, L), s.take(RT, T)]
        hu = s.take(12, L)
        gg = s.take(RT, T)
        sgl = s.take(16, T)
        vt01 = s.take(2, HY)
        assert s.at <= HI_AT
        s = Space(arena, RT * L)
        ys = s.take(3, 2, HY)
        s = Space(arena, 0)
        merged2 = s.take(KT, T)

        def vt(n):
            return vt01[:, n, :] if n < 2 else hu[:, 4:6, :].rearrange("p a b -> p (a b)")[:, 0:HY]

        s = Space(arena)
        pq = s.take(16, T)
        keys = s.take(2 * PH, NK)
        TOP_AT = 88 * T
        s = Space(arena, TOP_AT)
        assert NA <= 88 and NA % 6 == 0 and (NK - 2 - NA) % 6 == 0
        sc = s.take(2, 16, NK)
        scr = s.take(2 * NK)
        tv, ti, tif = s.take(2, 16, TOPK), s.take(2, 16, TOPK), s.take(2, 16, TOPK)
        cv, ci = s.take(2, PH, TOPK), s.take(2, PH, TOPK)
        ew = s.take(3, 2, PH * TOPK)
        assert s.at <= HI_AT
        s = Space(arena, TOP_AT)
        cand = s.take(2, PH, TOPK * TOPK)
        s = Space(arena, TOP_AT)
        hot = s.take(PH * TOPK, TOPK)
        cij, cijf = s.take(2, 2, PH * TOPK), s.take(2, 2, PH * TOPK)
        gates_all = arena[:, :].rearrange("p (e t) -> p e t", t=T)

        landed = [sem(f"landed{i}") for i in range(NS)]
        chunk_done = sem("chunk_done")
        hi_ready = sem("hi_ready")
        lo_pool, lo_dve = sem("lo_pool"), sem("lo_dve")
        h_hi, h_lo = sem("h_hi"), sem("h_lo")
        oa_hi, oa_lo, merged_hi, merged_lo = sem("oa_hi"), sem("oa_lo"), sem("merged_hi"), sem("merged_lo")
        gg_hi, gg_lo, merged2_hi, merged2_lo = sem("gg_hi"), sem("gg_lo"), sem("merged2_hi"), sem("merged2_lo")
        loaded_mask, loaded_keys = sem("loaded_mask"), sem("loaded_keys")
        loaded_vec = sem("loaded_vec")
        loaded_const = sem("loaded_const")
        loaded_x = sem("loaded_x")
        iota_ready = sem("iota_ready")
        dve_step = sem("dve_step")
        act_step = sem("act_step")
        sq_ready, ssq_ready, var_ready, std_ready = sem("sq_ready"), sem("ssq_ready"), sem("var_ready"), sem("std_ready")
        rstd_ready, rstd_spread = sem("rstd_ready"), sem("rstd_spread")
        sub_rstd, sub_spread = sem("sub_rstd"), sem("sub_spread")
        h_ready, x_ready = sem("h_ready"), sem("x_ready")
        flt_pe, flt_arg, flt_sin, flt_k = sem("flt_pe"), sem("flt_arg"), sem("flt_sin"), sem("flt_k")
        lam_prod, lam_sum, lam_exp = sem("lam_prod"), sem("lam_sum"), sem("lam_exp")
        rope_arg, rope_sin = sem("rope_arg"), sem("rope_sin")
        silu_ready, act_ready = sem("silu_ready"), sem("act_ready")
        act_gated, act_hi = sem("act_gated"), sem("act_hi")
        raw_copied, swapped, qk_ready = sem("raw_copied"), sem("swapped"), sem("qk_ready")
        v_copied, gate_copied = sem("v_copied"), sem("gate_copied")
        da_scores, da_nbias, da_exp, da_mixed = sem("da_scores"), sem("da_nbias"), sem("da_exp"), sem("da_mixed")
        da_turned, da_tcopied, da_out, ot_ready = sem("da_turned"), sem("da_tcopied"), sem("da_out"), sem("ot_ready")
        dl_scores, dl_nbias, dl_exp, dl_prob = sem("dl_scores"), sem("dl_nbias"), sem("dl_exp"), sem("dl_prob")
        dl_turned, dl_tcopied, dl_out, od_ready = sem("dl_turned"), sem("dl_tcopied"), sem("dl_out"), sem("od_ready")
        sub_sq, sub_sum, sub_var, sub_std, oa_ready = sem("sub_sq"), sem("sub_sum"), sem("sub_var"), sem("sub_std"), sem("oa_ready")
        sg_ready, merged_ready = sem("sg_ready"), sem("merged_ready")
        in2_copied, hy_conv, rg_conv, vx_ready = sem("in2_copied"), sem("hy_conv"), sem("rg_conv"), sem("vx_ready")
        vt_turned, vt_ready, spec_ready, ys_ready = sem("vt_turned"), sem("vt_ready"), sem("spec_ready"), sem("ys_ready")
        conv_out, hy_ready = sem("conv_out"), sem("hy_ready")
        rg_gated, rg_tanh, rg_den, rg_sqrt, rg_ready, decay_ready = (
            sem("rg_gated"), sem("rg_tanh"), sem("rg_den"), sem("rg_sqrt"), sem("rg_ready"), sem("decay_ready"))
        merged2_ready = sem("merged2_ready")
        lam_e, sp_ready = sem("lam_e"), sem("sp_ready")
        pq_copied, sc_out, sc_copied = sem("pq_copied"), sem("sc_out"), sem("sc_copied")
        cv_ready, ce_ready, ew_ready, ew_turned, ewt_ready = (
            sem("cv_ready"), sem("ce_ready"), sem("ew_ready"), sem("ew_turned"), sem("ewt_ready"))
        ab_raw, ab_ready, g_token, g_copied, g_gated = sem("ab_raw"), sem("ab_ready"), sem("g_token"), sem("g_copied"), sem("g_gated")
        gelu_ready, peer_act = sem("gelu_ready"), sem("peer_act")
        stored = sem("stored")
        N_CONST = 8

        def acc(n):
            return ps[:, n // 2, (n % 2) * T:(n % 2 + 1) * T]

        def token_tiles(w):
            return ((P, slice(0, 2)), (NM, slice(2, 3)))[:1 if w == T else 2]

        def rstd(w):
            return ps[:, 7, 0:w]

        def gate_bank(n):
            return ps[:, 4 + n % 2 if n < DA_H else 7 if n == 14 else 6, 0:T]

        def hyena_bank(n):
            return ps[:, (4, 5, 0, 1, 2, 3)[n % 6], :]

        def real(buf, k):
            return buf[:, k, NM:L]

        def ffn_up(base, j):
            return base + (1 if j == 0 else 3 * j)

        def ffn_down(base, j):
            return base + (3 * FT - 1 if j == FT - 1 else 3 * j + 4)

        def hi_part(c):
            return peer_hi[:, (c - START["experts"]) % NW, :] if c >= START["experts"] else main_hi[:, c % NW, :]

        def later(n, i, step):
            return i * step + n if step else n

        def expert_u(e):
            return e if e < NA else 2 * NA + (0 if e == NA else 2 * (e - NA) - 1)

        def expert_v(e):
            return NA + e if e < NA else 2 * NK - 1 if e == NK - 1 else 2 * NA + 2 * (e - NA) + 2

        N_PAIRS = (NK - 2 - NA) // 6
        QUADS = T // 4

        def tmp_spec(fn, n):
            return rgx[0:fn, :, :].rearrange("p a b -> p (a b)")[:, n * HY:(n + 1) * HY]

        def tmp_mix(n):
            return ys[:, 0, 0, n * T:(n + 1) * T]

        def i_tmp(d):
            return rgx[:, :, 0:(L if d == 0 else T)]

        def gl_tile(pe, tile, m):
            pe.wait_ge(in2_copied, 5 * RT + RT + m - 1)
            tile(START["gl"] + m, ps[:, 4 + m % 2, 0:T], lambda k: (h_parts[0][:, k, NM:L], h_parts[1][:, k, NM:L])).then_inc(chunk_done, 1)

        block = ctx.enter_context(nc.Block())

        @block.sync
        def _(sp):
            sp.dma_start(x[:, :, NM:L], x_d).then_inc(loaded_x, 16)
            for c in range(NS):
                sp.dma_start(ring[:, c, :], stream_d[c]).then_inc(landed[c], 16)
            whole = (N_CHUNKS - NS) // NS
            with sp.Fori(0, whole) as i:
                for m in range(NS):
                    sp.wait_ge(chunk_done, i * NS + (m + 1))
                    sp.dma_start(ring[:, m, :], stream_d[bass.ds(i * NS + (NS + m), 1), :, :].rearrange("a p n -> p (a n)")).then_inc(landed[m], 16)
            for c in range(NS + whole * NS, N_CHUNKS):
                sp.wait_ge(chunk_done, c - NS + 1)
                sp.dma_start(ring[:, c % NS, :], stream_d[c]).then_inc(landed[c % NS], 16)
            sp.wait_ge(h_ready, 8 * 6)
            sp.dma_start(out_d, h[:, :, NM:L]).then_inc(stored, 16)
            sp.wait_ge(stored, 16)

        @block.gpsimd
        def _(pool):
            def lo(c, i=0, his=0, los=0):
                if LO[c] > 1:
                    pool.wait_ge(lo_pool, later(LO[c] - 1, i, los))
                pool.wait_ge(hi_ready, later(HI[c], i, his))
                nc.gpsimd.tensor_tensor(ring_lo[:, c % NS, :], ring[:, c % NS, :], hi_part(c).bitcast(F32), ALU.subtract).then_inc(lo_pool, 1)

            def run(c, n):
                with pool.Fori(0, n // NS) as i:
                    for m in range(NS):
                        lo(c + m, i, NS, NS)
                for m in range(n - n % NS, n):
                    lo(c + m)

            def ffn(base):
                for r in range(4):
                    lo(base + r)
                with pool.Fori(0, (FT - 2) // 2) as i:
                    for m in (2, 3):
                        lo(base + 3 * m - 1, i, 6, 4)
                        lo(base + 3 * m, i, 6, 4)

            nc.gpsimd.memset(hdn[64:65, :], 1.0).then_inc(iota_ready, 1)
            pool.wait_ge(iota_ready, 1)
            ffn(START["ffn1"])
            run(START["qk"], START["proj_b"] - START["qk"])
            run(START["proj_a"], START["ffn2"] - START["proj_a"])
            ffn(START["ffn2"])
            run(START["rgx"], START["rggate"] - START["rgx"])
            run(START["rgg"], START["hyout"] - START["rgg"])
            run(START["rgout"], START["experts"] - START["rgout"])
            pool.wait_ge(lo_pool, LO[START["experts"] - 1])
            pool.wait_ge(x_ready, 8 * 4)
            nc.gpsimd.iota(iota, pattern=[[1, NK]], base=0, channel_multiplier=0, allow_small_or_imprecise_dtypes=True).then_inc(iota_ready, 1)
            pool.wait_ge(iota_ready, 2)
            nc.gpsimd.iota(io16, pattern=[[1, TOPK]], base=0, channel_multiplier=0, allow_small_or_imprecise_dtypes=True).then_inc(iota_ready, 1)
            pool.wait_ge(iota_ready, 3)
            base = START["experts"]
            run(base, 2 * NA)
            lo(base + expert_u(NA))
            lo(base + expert_u(NA + 1))
            with pool.Fori(0, N_PAIRS) as i:
                for m in range(2, 8):
                    lo(base + expert_u(NA + m), i, 12, 6)

        @block.scalar
        def _(act_e):
            steps = [0]

            def link(ins):
                steps[0] += 1
                ins.then_inc(act_step, 1)
                act_e.wait_ge(act_step, steps[0])

            A = nc.scalar.activation
            act_e.dma_start(cols[:], cols_d).then_inc(loaded_vec, 16)
            act_e.dma_start(square[:], sq_d).then_inc(loaded_vec, 16)
            act_e.dma_start(posi.bitcast(I32), pos_d).then_inc(loaded_vec, 16)

            def squares(n, src, w, ready=None):
                if n:
                    act_e.wait_ge(ssq_ready, n)
                for k in range(KT):
                    if ready is not None:
                        act_e.wait_ge(x_ready, ready + k + 1)
                    A(sq[:, k, 0:w], src(k), ACT.Square).then_inc(sq_ready, 1)

            def root(n, w):
                act_e.wait_ge(var_ready, n + 1)
                for p, c in token_tiles(w):
                    ins = A(root_t[0:p, c], root_t[0:p, c], ACT.Sqrt)
                ins.then_inc(std_ready, 1)

            def hi(c, i=0, step=0):
                act_e.wait_ge(landed[c % NS], later(16 * (c // NS + 1), i, step // NS * 16))
                if BEFORE[c] is not None:
                    act_e.wait_ge(chunk_done, later(BEFORE[c] + 1, i, step))
                A(hi_part(c), ring[:, c % NS, :], ACT.Copy).then_inc(hi_ready, 1)

            todo = [0]

            def hi_to(c):
                for n in range(todo[0], c + 1):
                    if BY[n]:
                        hi(n)
                todo[0] = c + 1

            def input_hi(ready, w=T):
                for k in range(KT):
                    act_e.wait_ge(h_ready, ready + k + 1)
                    A(h_parts[0][:, k, L - w:L], h[:, k, L - w:L], ACT.Copy).then_inc(h_hi, 1)

            act_e.wait_ge(loaded_x, 16)
            squares(0, lambda k: real(x, k), T)
            root(0, T)
            hi_to(NW - 1)
            act_e.wait_ge(ssq_ready, 1)
            input_hi(0)
            act_e.dma_start(x[:, :, 0:NM], meta_d).then_inc(loaded_const, 16)
            act_e.dma_start(zt[0:2 * HB + 1, :], zt_d).then_inc(loaded_const, 16)
            act_e.dma_start(w1[0:2 * HB + 1, :], w1_d).then_inc(loaded_const, 16)
            act_e.dma_start(w2[0:FW, :], w2_d).then_inc(loaded_const, 16)
            act_e.dma_start(w3[0:FW + 1, :], w3_d).then_inc(loaded_const, 16)
            act_e.dma_start(decay, decay_d).then_inc(loaded_const, 16)
            act_e.dma_start(dft, dft_d).then_inc(loaded_const, 16)
            act_e.dma_start(idft, idft_d).then_inc(loaded_const, 16)
            act_e.wait_ge(rope_arg, 2)
            A(rope_s, ang, ACT.Sin).then_inc(rope_sin, 1)
            A(rope_c, angq, ACT.Sin).then_inc(rope_sin, 1)

            def ffn(f, base):
                def one(done, buf):
                    act_e.wait_ge(chunk_done, done)
                    A(silu[:, buf, :], ps[:, 4 + buf, 0:T], ACT.Silu).then_inc(silu_ready, 1)

                hi_to(base + 3)
                if f:
                    act_e.wait_ge(act_ready, FT - 1)
                one(base + 2, 0)
                hi_to(base + 5)
                if f:
                    act_e.wait_ge(act_ready, FT)
                one(base + 4, 1)
                with act_e.Fori(0, (FT - 2) // 2) as i:
                    for m in (2, 3):
                        for r in range(3 * m, 3 * m + 3):
                            hi(base + r, i, 6)
                        act_e.wait_ge(act_ready, i * 2 + (f * FT + m - 1))
                        one(i * 6 + (base + 3 * m + 1), m % 2)
                todo[0] = base + 3 * FT
                hi_to(base + 3 * FT + 1)

            ffn(0, START["ffn1"])
            act_e.dma_start(mask, mask_d).then_inc(loaded_mask, 16)
            act_e.wait_ge(chunk_done, START["qk"])
            squares(1, acc, T)
            root(1, T)
            hi_to(START["qk"] + 2)
            squares(2, lambda k: real(x, k), T, 0)
            root(2, T)
            act_e.wait_ge(ssq_ready, 3)
            input_hi(KT)

            def between(n):
                if n == 0:
                    act_e.wait_ge(lam_sum, 1)
                    A(small[:, 4:6], ps[:, 0, 0:2], ACT.Exp).then_inc(lam_exp, 1)
                    act_e.wait_ge(lam_e, 1)
                    A(small[:, 16:32], small[:, 32:48], ACT.Exp, scale=-1.0).then_inc(lam_exp, 1)
                if n in (3, 6):
                    act_e.wait_ge(flt_arg, n // 3)
                    A(hdn[0:FW, :], arg[0:FW, :], ACT.Sin).then_inc(flt_sin, 1)

            for n in range(28):
                act_e.wait_ge(chunk_done, START["qk"] + n + 1)
                if n >= 2:
                    act_e.wait_ge(qk_ready, n - 1)
                A(raw[:, n % 2, :], ps[:, 4 + n % 2, 0:T], ACT.Copy).then_inc(raw_copied, 1)
                hi_to(START["qk"] + n + 3)
                between(n)
            hi_to(START["vd"] + 2)
            act_e.wait_ge(chunk_done, START["vd"])
            for b in range(4):
                A(va[:, b // 2, (b % 2) * 512:(b % 2 + 1) * 512], ps[:, b, :], ACT.Copy).then_inc(v_copied, 1)

            hi_to(START["gates"] + 2)

            def da_exps(hd):
                act_e.wait_ge(da_nbias, hd + 1)
                if hd >= 2:
                    act_e.wait_ge(da_mixed, 2 * (hd - 1))
                for c in range(2):
                    for q in range(2):
                        A(da_p[:, hd % 2, 2 * c + q, :], ps[:, 2 * (hd % 2) + c, q * T:(q + 1) * T], ACT.Exp,
                          bias=small[:, 64 + 8 * (hd % 2) + 2 * c + q:65 + 8 * (hd % 2) + 2 * c + q], scale=DH ** -0.5,
                          accum_out=small[:, 80 + 8 * (hd % 2) + 2 * c + q:81 + 8 * (hd % 2) + 2 * c + q]).then_inc(da_exp, 1)

            def gate_copy(n):
                act_e.wait_ge(chunk_done, START["gates"] + n + 1)
                A(sg[:, n, :], gate_bank(n), ACT.Copy).then_inc(gate_copied, 1)
                hi_to(START["gates"] + n + 3)

            da_exps(0)
            for hd in range(DA_H):
                if hd + 1 < DA_H:
                    da_exps(hd + 1)
                gate_copy(hd)
                act_e.wait_ge(da_turned, hd + 1)
                if hd >= 2:
                    act_e.wait_ge(da_out, hd - 1)
                A(da_at[:, hd % 2, :], ps[:, 6, :], ACT.Copy).then_inc(da_tcopied, 1)

            def dl_exps(j):
                act_e.wait_ge(dl_nbias, j + 1)
                o = 98 + 10 * (j % 2)
                for q in range(2):
                    A(dl_p[j % 2][:, :, q, :], dl_p[j % 2][:, :, q, :], ACT.Exp, bias=small[:, o + 2 + q:o + 3 + q], scale=DH ** -0.5,
                      accum_out=small[:, o + 6 + q:o + 7 + q]).then_inc(dl_exp, 1)

            dl_exps(0)
            gate_copy(DA_H)
            for j in range(DIL_H):
                if j + 1 < DIL_H:
                    dl_exps(j + 1)
                if j == 0:
                    gate_copy(DA_H + 1)
                act_e.wait_ge(dl_turned, j + 1)
                if j >= 1:
                    act_e.wait_ge(dl_out, j)
                A(dl_pt[:, :, :, :].rearrange("p a b c -> p a (b c)"), ps[:, 3:6, :], ACT.Copy).then_inc(dl_tcopied, 1)
                if j + 1 < DIL_H:
                    gate_copy(DA_H + 2 + j)
            for hd in range(DA_H):
                act_e.wait_ge(ot_ready, hd + 1)
                A(merged[:, hd, :], ot[:, hd, :], ACT.Square).then_inc(sub_sq, 1)
            act_e.wait_ge(sub_var, 1)
            A(sub_root_t, sub_root_t, ACT.Sqrt).then_inc(sub_std, 1)
            for n in range(13, 16):
                gate_copy(n)
            hi_to(START["proj_a"] + 2)
            for hd in range(DA_H):
                act_e.wait_ge(oa_ready, hd + 1)
                A(oa_parts[:, 0, hd, :], oa[:, hd, :], ACT.Copy).then_inc(oa_hi, 1)
            act_e.wait_ge(gate_copied, 2 * KT)
            A(sg[:, :, :], sg[:, :, :], ACT.Sigmoid).then_inc(sg_ready, 1)
            for n in range(KT):
                hi_to(START["proj_a"] + n + 3)
                act_e.wait_ge(merged_ready, n + 1)
                A(merged_parts[:, 0, n, :], merged[:, n, :], ACT.Copy).then_inc(merged_hi, 1)
            hi_to(START["ffn2"] + 1)
            act_e.wait_ge(chunk_done, START["ffn2"])
            squares(3, acc, T)
            hi_to(START["ffn2"] + 2)
            root(3, T)
            squares(4, lambda k: real(x, k), T, 1 * KT)
            root(4, T)
            act_e.wait_ge(ssq_ready, 5)
            input_hi(2 * KT)
            ffn(1, START["ffn2"])
            act_e.wait_ge(chunk_done, START["rgx"])
            squares(5, acc, T)
            hi_to(START["rgx"] + 2)
            root(5, T)
            act_e.wait_ge(loaded_const, 16 * N_CONST)
            squares(6, lambda k: x[:, k, :], L, 2 * KT)
            root(6, L)
            act_e.wait_ge(ssq_ready, 7)
            input_hi(3 * KT, L)

            for n in range(RT):
                act_e.wait_ge(chunk_done, START["rgx"] + n + 1)
                A(rgx[:, n, :], ps[:, 4 + n % 2, 0:L], ACT.Copy).then_inc(in2_copied, 1)
                hi_to(START["rgx"] + n + 3)
            hi_to(START["rggate"] - 1)
            for d in range(2):
                w = L if d == 0 else T
                for g, buf in ((0, r_g), (1, i_g)):
                    for t in range(RT):
                        n = (2 * d + g) * RT + t
                        act_e.wait_ge(rg_gated, n + 1)
                        A(buf[d][:, t, :], ps[:, 6 + n % 2, 0:w], ACT.Sigmoid, bias=col("rg_gate_b_2", n)).then_inc(in2_copied, 1)
                    if g == 0:
                        hi_to(START["rgg"] + 1 + d)
            for n in range(3):
                act_e.wait_ge(vt_turned, n + 1)
                A(vt(n)[0:LT[n][1], :], ps[0:LT[n][1], n, :], ACT.Copy).then_inc(vt_ready, 1)
            act_e.wait_ge(sp_ready, 2)
            act_e.wait_ge(in2_copied, RT + 4 * RT)
            for d in range(2):
                for t in range(RT):
                    A(m_g[d][:, t, :], r_g[d][:, t, :], ACT.Tanh, scale=small[:, 160 + 8 * d + t:161 + 8 * d + t]).then_inc(rg_tanh, 1)
                if t == RT - 1:
                    hi_to(START["rgg"] + 3 + d)
            act_e.wait_ge(rg_tanh, 2 * RT)

            def rgg_gelu(n):
                act_e.wait_ge(chunk_done, START["rgg"] + n + 1)
                A(gg[:, n, :], ps[:, 4 + n % 4, 0:T], ACT.Gelu_apprx_tanh).then_inc(in2_copied, 1)
                if n >= 2:
                    hi_to(START["rgg"] + n + 3)

            for d in range(2):
                rgg_gelu(2 * d)
                rgg_gelu(2 * d + 1)
                for t in range(RT):
                    A(r_g[d][:, t, :], r_g[d][:, t, :], ACT.Exp, scale=small[:, 176 + 8 * d + t:177 + 8 * d + t]).then_inc(decay_ready, 1)
            for n in range(4, RT):
                rgg_gelu(n)
            for d in range(2):
                act_e.wait_ge(rg_den, d + 1)
                A(m_g[d][:, :, :], m_g[d][:, :, :], ACT.Sqrt).then_inc(rg_sqrt, 1)
            for n in range(16):
                act_e.wait_ge(chunk_done, START["gl"] + n + 1)
                A(sgl[:, n, :], ps[:, 4 + n % 2, 0:T], ACT.Sigmoid, bias=col("b_gate_2", n)).then_inc(in2_copied, 1)
                if n < 13:
                    hi_to(START["gl"] + n + 3)
            act_e.wait_ge(rg_ready, 1)
            A(gg_parts[:, 0, :, :], gg[:, :, :], ACT.Copy).then_inc(gg_hi, 1)
            hi_to(START["rgout"] + 2)
            for n in range(KT):
                hi_to(START["rgout"] + n + 3)
                act_e.wait_ge(merged2_ready, n + 1)
                A(merged2_parts[:, 0, n, :], merged2[:, n, :], ACT.Copy).then_inc(merged2_hi, 1)
            hi_to(START["wq"] + 1)

            squares(7, lambda k: real(x, k), T, 3 * KT)
            act_e.dma_start(keys, keys_d).then_inc(loaded_keys, 16)
            root(7, T)
            hi_to(START["wq"] + 2)
            act_e.wait_ge(ssq_ready, 8)
            input_hi(4 * KT)

            def scores_out(g):
                for t in range(2):
                    act_e.wait_ge(sc_out, 2 * g + t + 1)
                    A(sc[:, t, 4 * g:4 * g + 4, :].rearrange("p a b -> p (a b)"), ps[:, 2 * t + g % 2, :], ACT.Copy).then_inc(sc_copied, 1)

            for n in range(16):
                act_e.wait_ge(chunk_done, START["wq"] + n + 1)
                A(pq[:, n, :], ps[:, 4 + n % 2, 0:T], ACT.Copy).then_inc(pq_copied, 1)
                if n and n % 4 == 0:
                    scores_out(n // 4 - 1)
                hi_to(START["wq"] + n + 3)
            scores_out(3)
            base = START["experts"]

            def ahead(e, dst, i=0, step=0):
                n = base + e + 1
                act_e.wait_ge(chunk_done, i * step + n if step else n)
                A(dst, ps[:, 4 + e % 2, 0:T], ACT.Gelu_apprx_tanh).then_inc(gelu_ready, 1)
                if e + NW <= expert_v(0):
                    hi(base + e + NW, i, step)

            hi_to(base + NW - 1)
            with act_e.Fori(0, NA // 6 - 1) as i:
                for m in range(6):
                    ahead(m, gates_all[:, bass.ds(i * 6 + m, 1), :].rearrange("p a t -> p (a t)"), i, 6)
            act_e.wait_ge(cv_ready, 2)
            A(ew[:, 2, :, :], ew[:, 2, :, :], ACT.Exp).then_inc(ce_ready, 1)
            for e in range(NA - 6, NA):
                ahead(e, gates_all[:, e, :])

            def weigh(q, i=0, step=0):
                act_e.wait_ge(ab_raw, i * step + (q + 1) if step else q + 1)
                for m in range(4):
                    t = 4 * q + m
                    g = gt[:, bass.ds(i * (4 * step) + t, 1)] if step else gt[:, t:t + 1]
                    ins = A(sel_a[:, q % 4, m, :], sel_a[:, q % 4, m, :], ACT.Copy, scale=g)
                ins.then_inc(ab_ready, 1)

            def gates_out(q, i=0, step=0):
                act_e.wait_ge(g_token, i * step + (q + 1) if step else q + 1)
                t = bass.ds(i * (4 * step) + 4 * q, 4) if step else slice(4 * q, 4 * q + 4)
                A(gates_all[:, NA:NK, t], ps[:, 4 + q % 4, :].rearrange("p (t e) -> p e t", t=4)[:, NA:NK, :], ACT.Copy).then_inc(g_copied, 1)

            act_e.wait_ge(ewt_ready, 3)
            weigh(0)
            weigh(1)
            with act_e.Fori(0, QUADS // 4 - 1) as i:
                for m in range(4):
                    weigh(m + 2, i, 4)
                    gates_out(m, i, 4)
            for q in range(QUADS - 4, QUADS):
                if q + 2 < QUADS:
                    weigh(q + 2)
                gates_out(q)
            hi(base + expert_v(1))
            hi(base + expert_v(2))
            with act_e.Fori(0, NA // 6) as i:
                for m in range(6):
                    hi(base + NA + NW + m, i, 6)

            def expert(done, buf):
                act_e.wait_ge(chunk_done, done)
                A(ge_p[:, buf, :], ps[:, 4 + buf, 0:T], ACT.Gelu_apprx_tanh).then_inc(gelu_ready, 1)

            act_e.wait_ge(peer_act, NA)
            expert(base + expert_u(NA) + 1, 0)
            hi(base + 2 * NA + 3)
            expert(base + expert_u(NA + 1) + 1, 1)
            with act_e.Fori(0, N_PAIRS) as i:
                for m in range(2, 8):
                    hi(base + 2 * NA + 2 * m, i, 12)
                    hi(base + 2 * NA + 2 * m + 1, i, 12)
                    act_e.wait_ge(peer_act, i * 6 + (NA + m - 1))
                    expert(i * 12 + (base + expert_u(NA + m) + 1), m % 2)
            squares(8, lambda k: real(x, k), T, 4 * KT)
            root(8, T)

        @block.vector
        def _(dve):
            steps = [0]
            V = nc.vector

            def link(ins):
                steps[0] += 1
                ins.then_inc(dve_step, 1)
                dve.wait_ge(dve_step, steps[0])

            def mean_square(n, w, width=D, half=False):
                dve.wait_ge(ssq_ready, n + 1)
                f = 4.0 if half else 1.0
                for p, c in token_tiles(w):
                    ins = V.tensor_scalar(root_t[0:p, c], ps[0:p, 6, c], f / width, f * EPS, ALU.mult, ALU.add)
                ins.then_inc(var_ready, 1)
                dve.wait_ge(std_ready, n + 1)
                for p, c in token_tiles(w):
                    ins = V.reciprocal(rstd_t[0:p, c], root_t[0:p, c])
                ins.then_inc(rstd_ready, 1)
                dve.wait_ge(rstd_spread, n + 1)

            def norm_in(n, name, src, dst, w):
                mean_square(n, w)
                for k in range(KT):
                    V.scalar_tensor_tensor(dst(k), src(k), col(name, k), rstd(w), ALU.mult, ALU.mult).then_inc(h_ready, 1)

            def norm_out(n, name, half):
                mean_square(n, T, half=half)
                link(V.tensor_copy(rstd_out[:], rstd(T)))
                for k in range(KT + 1):
                    if k < KT:
                        V.scalar_tensor_tensor(h[:, k, 0:T], acc(k), col(name, k), rstd_out[:], ALU.mult, ALU.mult).then_inc(dve_step, 1)
                        steps[0] += 1
                    if k:
                        dve.wait_ge(dve_step, steps[0] - (k < KT))
                        V.tensor_tensor(real(x, k - 1), real(x, k - 1), h[:, k - 1, 0:T], ALU.add).then_inc(x_ready, 1)

            def reduce_angle(a, q):
                link(V.tensor_scalar(q, a, 1.0 / TWO_PI, ROUND, ALU.mult, ALU.add))
                link(V.tensor_scalar(q, q, -ROUND, None, ALU.add))
                link(V.scalar_tensor_tensor(a, q, -PI1, a, ALU.mult, ALU.add))
                link(V.scalar_tensor_tensor(a, q, -PI2, a, ALU.mult, ALU.add))
                link(V.scalar_tensor_tensor(a, q, -PI3, a, ALU.mult, ALU.add))
                return V.tensor_scalar(a, a, PI_IN, -PI_IN, ALU.min, ALU.max)

            def split_gated(buf, src, split, n):
                dve.wait_ge(act_gated, n)
                V.tensor_copy(split[0][:, buf, :], src[:, buf, :]).then_inc(act_hi, 1)
                dve.wait_ge(act_hi, n)
                return V.tensor_tensor(split[1][:, buf, :], src[:, buf, :], split[0][:, buf, :].bitcast(F32), ALU.subtract)

            def input_lo(use, w=T):
                for k in range(KT):
                    dve.wait_ge(h_hi, use * KT + k + 1)
                    V.tensor_tensor(h_parts[1][:, k, L - w:L], h[:, k, L - w:L], h_parts[0][:, k, L - w:L].bitcast(F32), ALU.subtract).then_inc(h_lo, 1)

            def lo(c, i=0, his=0, los=0):
                dve.wait_ge(hi_ready, later(HI[c], i, his))
                V.tensor_tensor(ring_lo[:, c % NS, :], ring[:, c % NS, :], hi_part(c).bitcast(F32), ALU.subtract).then_inc(lo_dve, 1)

            def low_part(parts, whole, n):
                return V.tensor_tensor(parts[:, 1, n, :], whole[:, n, :], parts[:, 0, n, :].bitcast(F32), ALU.subtract)

            dve.wait_ge(loaded_vec, 16 * 3)
            dve.wait_ge(loaded_x, 16)
            norm_in(0, NORMS[0], lambda k: real(x, k), lambda k: real(h, k), T)
            input_lo(0)
            link(V.tensor_copy(ang, posi.bitcast(I32)))
            link(V.tensor_scalar(ang, ang, col("rope_inv"), None, ALU.mult))
            link(reduce_angle(ang, angq))
            link(V.scalar_tensor_tensor(angq, ang, -1.0, ang, ALU.mult, ALU.min))
            link(V.tensor_scalar(angq, angq, math.pi / 2, None, ALU.add))
            V.tensor_scalar(ang, ang, col("rope_sign"), None, ALU.mult).then_inc(rope_arg, 2)
            for n in (1, 2):
                V.tensor_tensor(small[:, n - 1:n], col(f"lambda_q{n}"), col(f"lambda_k{n}"), ALU.mult).then_inc(lam_prod, 1)
            lam = cols[:, COL["rg_lambda_2"]:COL["rg_lambda_2"] + 16]
            V.scalar_tensor_tensor(small[:, 32:48], lam, -1.0, lam, ALU.mult, ALU.max).then_inc(lam_e, 1)
            def ffn(f, base):
                def one(n, buf):
                    dve.wait_ge(silu_ready, n)
                    V.tensor_tensor(act[:, buf, :], silu[:, buf, :], ps[:, 4 + buf, T:2 * T], ALU.mult).then_inc(act_gated, 1)
                    split_gated(buf, act, ffn_act, n).then_inc(act_ready, 1)

                one(f * FT + 1, 0)
                lo(base + 4)
                one(f * FT + 2, 1)
                with dve.Fori(0, (FT - 2) // 2) as i:
                    for m in (2, 3):
                        lo(base + 3 * m + 1, i, 6, 2)
                        dve.wait_ge(chunk_done, i * 6 + (base + 3 * m - 1))
                        one(i * 2 + (f * FT + m + 1), m % 2)
                lo(base + 3 * FT - 1)

            ffn(0, START["ffn1"])
            norm_out(1, NORMS[1], True)
            norm_in(2, NORMS[2], lambda k: real(x, k), lambda k: real(h, k), T)
            input_lo(1)

            def between(n):
                if n in (1, 4):
                    layer = n // 3
                    if n == 1:
                        dve.wait_ge(loaded_const, 16 * N_CONST)
                    dve.wait_ge(flt_pe, layer + 1)
                    b, at = COL[("hy_b1_2", "hy_b2_2")[layer]], COL["hy_freq_2"] + layer
                    link(V.tensor_scalar(arg[0:FW, :], ps[0:FW, 1, 0:L], cols[0:FW, b:b + 1], cols[0:FW, at:at + 1], ALU.add, ALU.mult))
                    reduce_angle(arg[0:FW, :], turn[0:FW, :]).then_inc(flt_arg, 1)
                if n in (7, 10, 13):
                    m = (n - 7) // 3
                    tn = LT[m][1]
                    dve.wait_ge(flt_pe, 3 + m)
                    for d in range(2):
                        link(V.tensor_tensor(kfb[0:tn, d, :], ps[0:tn, 1 + d, :], decay[0:tn, m, d, :], ALU.mult))
                    V.tensor_tensor(ksum[0:tn, m, :], kfb[0:tn, 0, :], kfb[0:tn, 1, :], ALU.add).then_inc(flt_k, 1)
                    V.tensor_tensor(kdif[0:tn, m, :], kfb[0:tn, 0, :], kfb[0:tn, 1, :], ALU.subtract).then_inc(flt_k, 1)
                    dve.wait_ge(flt_k, 2 * m + 2)
                if n in (16, 19, 22):
                    m = (n - 16) // 3
                    fn = LT[m][1]
                    dve.wait_ge(flt_pe, 6 + m)
                    V.tensor_copy(kre[0:fn, m, :], ps[0:fn, 1, :]).then_inc(flt_k, 1)
                    V.tensor_copy(kim[0:fn, m, :], ps[0:fn, 2, :]).then_inc(flt_k, 1)
                if n == 25:
                    dve.wait_ge(lam_exp, 2)
                    link(V.tensor_tensor(small[:, 6:7], small[:, 5:6], small[:, 4:5], ALU.subtract))
                    link(V.tensor_scalar(small[:, 7:8], small[:, 6:7], -LAMBDA_INIT, None, ALU.add))
                    e, w, w2s, pl = small[:, 16:32], small[:, 112:128], small[:, 128:144], small[:, 144:160]
                    link(V.tensor_scalar(w, e, 2.0, None, ALU.add))
                    link(V.reciprocal(w, w))
                    link(V.tensor_tensor(w, w, e, ALU.mult))
                    link(V.tensor_tensor(w2s, w, w, ALU.mult))
                    link(V.tensor_scalar(pl, w2s, 1.0 / 17, 1.0 / 15, ALU.mult, ALU.add))
                    for odd in (13, 11, 9, 7, 5, 3, 1):
                        link(V.tensor_tensor(pl, pl, w2s, ALU.mult))
                        link(V.tensor_scalar(pl, pl, 1.0 / odd, None, ALU.add))
                    link(V.tensor_tensor(pl, pl, w, ALU.mult))
                    link(V.tensor_scalar(w, lam, -1.0, 0.0, ALU.mult, ALU.max))
                    link(V.scalar_tensor_tensor(pl, pl, 2.0, w, ALU.mult, ALU.add))
                    V.tensor_scalar(small[:, 160:176], pl, RG_C, None, ALU.mult).then_inc(sp_ready, 1)
                    V.tensor_scalar(small[:, 176:192], pl, -RG_C, None, ALU.mult).then_inc(sp_ready, 1)

            dve.wait_ge(rope_sin, 2)
            for n in range(28):
                dve.wait_ge(swapped, n + 1)
                link(V.tensor_tensor(rot[:, 0, :], ps[:, 6 + n % 2, 0:T], rope_s, ALU.mult))
                link(V.tensor_tensor(rot[:, 1, :], raw[:, n % 2, :], rope_c, ALU.mult))
                V.tensor_tensor(qk[:, n, :], rot[:, 0, :], rot[:, 1, :], ALU.add).then_inc(qk_ready, 1)
                dve.wait_ge(qk_ready, n + 1)
                between(n)
            dve.wait_ge(chunk_done, START["gates"])
            for b in range(4):
                c0, cn = (b % 2) * 512, (512, 256)[b % 2]
                V.tensor_copy(vd[:, b // 2, c0:c0 + cn], ps[:, 4 + b, 0:cn]).then_inc(v_copied, 1)

            def da_max(hd):
                dve.wait_ge(da_scores, hd + 1)
                o = 8 * (hd % 2)
                link(V.tensor_reduce(small[:, 48 + o:52 + o], ps[:, 2 * (hd % 2):2 * (hd % 2) + 2, :].rearrange("p c (q k) -> p c q k", q=2), AX.X, ALU.max, negate=True))
                V.tensor_scalar(small[:, 64 + o:68 + o], small[:, 48 + o:52 + o], DH ** -0.5, None, ALU.mult).then_inc(da_nbias, 1)

            def da_mix(hd):
                dve.wait_ge(da_exp, 4 * (hd + 1))
                o = 80 + 8 * (hd % 2)
                link(V.reciprocal(small[:, o:o + 4], small[:, o:o + 4]))
                link(V.tensor_scalar(small[:, o + 2:o + 4], small[:, o + 2:o + 4], small[:, 7:8], None, ALU.mult))
                if hd >= 2:
                    dve.wait_ge(da_turned, hd - 1)
                for q in range(2):
                    link(V.tensor_scalar(da_t[:, q, :], da_p[:, hd % 2, 2 + q, :], small[:, o + 2 + q:o + 3 + q], None, ALU.mult))
                    V.scalar_tensor_tensor(da_a[:, hd % 2, q, :], da_p[:, hd % 2, q, :], small[:, o + q:o + q + 1], da_t[:, q, :], ALU.mult, ALU.add).then_inc(da_mixed, 1)

            def da_take(hd):
                dve.wait_ge(da_out, hd + 1)
                V.tensor_copy(ot[:, hd, :], ps[:, 7, 0:T]).then_inc(ot_ready, 1)

            da_max(0)
            for hd in range(DA_H):
                if hd + 1 < DA_H:
                    da_max(hd + 1)
                da_mix(hd)
                if hd:
                    da_take(hd - 1)
            dve.wait_ge(da_mixed, 2 * DA_H)
            dve.wait_ge(loaded_mask, 16)

            def dl_max(j):
                dve.wait_ge(dl_scores, j + 1)
                if j >= 2:
                    dve.wait_ge(dl_turned, j - 1)
                p, o = dl_p[j % 2], 98 + 10 * (j % 2)
                for g in range(3):
                    link(V.tensor_tensor(p[:, g, :, :], ps[:, g, :].rearrange("p (q k) -> p q k", q=2), mask[:, g, :, :], ALU.add))
                for q in range(2):
                    link(V.tensor_reduce(small[:, o + q:o + 1 + q], p[:, :, q, :], AX.XY, ALU.max, negate=True))
                V.tensor_scalar(small[:, o + 2:o + 4], small[:, o:o + 2], DH ** -0.5, None, ALU.mult).then_inc(dl_nbias, 1)

            def dl_probs(j):
                dve.wait_ge(dl_exp, 2 * (j + 1))
                p, o = dl_p[j % 2], 98 + 10 * (j % 2)
                link(V.reciprocal(small[:, o + 8:o + 10], small[:, o + 6:o + 8]))
                for q in range(2):
                    V.tensor_scalar(p[:, :, q, :], p[:, :, q, :], small[:, o + 8 + q:o + 9 + q], None, ALU.mult).then_inc(dl_prob, 1)

            def dl_take(j):
                dve.wait_ge(dl_out, j + 1)
                r0 = DH * (j % 2)
                V.tensor_copy(odt[r0:r0 + DH, j // 2, :], ps[r0:r0 + DH, 7, 0:T]).then_inc(od_ready, 1)

            dl_max(0)
            da_take(DA_H - 1)
            dl_max(1)
            dl_probs(0)
            for j in range(DIL_H):
                if j + 1 < DIL_H:
                    dl_probs(j + 1)
                if j + 2 < DIL_H:
                    dl_max(j + 2)
                dl_take(j)
            dve.wait_ge(sub_sum, 1)
            f = (1.0 - LAMBDA_INIT) ** -2
            V.tensor_scalar(sub_root_t, ps[:, 0, 0:2 * DA_H], f / P, f * EPS, ALU.mult, ALU.add).then_inc(sub_var, 1)
            dve.wait_ge(sub_std, 1)
            V.reciprocal(sub_rstd_t, sub_root_t).then_inc(sub_rstd, 1)
            for hd in range(DA_H):
                dve.wait_ge(sub_spread, hd // 2 + 1)
                V.scalar_tensor_tensor(oa[:, hd, :], ot[:, hd, :], col("g_subln"), acc(hd), ALU.mult, ALU.mult).then_inc(oa_ready, 1)
            for hd in range(DA_H):
                dve.wait_ge(oa_hi, hd + 1)
                low_part(oa_parts, oa, hd).then_inc(oa_lo, 1)
            dve.wait_ge(sg_ready, 1)
            dve.wait_ge(chunk_done, START["proj_a"])
            for n in range(KT):
                dve.wait_ge(chunk_done, START["proj_a"] + n + 1)
                link(V.tensor_tensor(rot[:, 0, :], acc(n), sg[:, 8 + n, :], ALU.mult))
                link(V.tensor_tensor(rot[:, 1, :], ps[:, 4 + n % 2, 0:T], sg[:, n, :], ALU.mult))
                V.tensor_tensor(merged[:, n, :], rot[:, 0, :], rot[:, 1, :], ALU.add).then_inc(merged_ready, 1)
                dve.wait_ge(merged_ready, n + 1)
                if n:
                    dve.wait_ge(merged_hi, n)
                    low_part(merged_parts, merged, n - 1).then_inc(merged_lo, 1)
            dve.wait_ge(merged_hi, KT)
            low_part(merged_parts, merged, KT - 1).then_inc(merged_lo, 1)
            norm_out(3, NORMS[3], False)
            norm_in(4, NORMS[4], lambda k: real(x, k), lambda k: real(h, k), T)
            input_lo(2)
            ffn(1, START["ffn2"])
            norm_out(5, NORMS[5], True)
            norm_in(6, NORMS[6], lambda k: x[:, k, :], lambda k: h[:, k, :], L)
            input_lo(3, L)

            for n in range(RT):
                dve.wait_ge(in2_copied, n + 1)
                for d in range(2):
                    w = [col("rg_conv_w_2", (4 * d + j) * RT + n) for j in range(4)]
                    dst = xc[d][:, n, :]
                    src = rgx[:, n, :] if d == 0 else rgx[:, n, NM:L]
                    link(V.tensor_scalar(dst, src, w[0], col("rg_conv_b_2", d * RT + n), ALU.mult, ALU.add))
                    for j in range(1, 4):
                        if d == 0:
                            link(V.scalar_tensor_tensor(dst[:, j:L], rgx[:, n, 0:L - j], w[j], dst[:, j:L], ALU.mult, ALU.add))
                        else:
                            ins = V.scalar_tensor_tensor(dst[:, 0:T - j], rgx[:, n, NM + j:L], w[j], dst[:, 0:T - j], ALU.mult, ALU.add)
                            if j < 3:
                                link(ins)
                ins.then_inc(rg_conv, 1)
            for n in range(12):
                dve.wait_ge(chunk_done, START["hyena"] + n + 1)
                src = hyena_bank(n)
                part = (2, 1, 0)[n // 4] * HYT + n % 4
                w = [col("hy_conv_w_2", j * 12 + part) for j in range(3)]
                link(V.tensor_scalar(hu[:, n, :], src[:, 0:L], w[1], col("hy_conv_b_2", part), ALU.mult, ALU.add))
                link(V.scalar_tensor_tensor(hu[:, n, 1:L], src[:, 0:L - 1], w[0], hu[:, n, 1:L], ALU.mult, ALU.add))
                V.scalar_tensor_tensor(hu[:, n, 0:L - 1], src[:, 1:L], w[2], hu[:, n, 0:L - 1], ALU.mult, ALU.add).then_inc(hy_conv, 1)
            dve.wait_ge(hy_conv, 12)
            for c in range(HYT):
                V.tensor_tensor(hu[:, c, :], hu[:, c, :], hu[:, 4 + c, :], ALU.mult).then_inc(vx_ready, 1)
            for d in range(2):
                dve.wait_ge(rg_tanh, RT * (d + 1))
                den = i_tmp(d)
                link(V.tensor_scalar(den, m_g[d][:, :, :], 1.0, None, ALU.add))
                link(V.reciprocal(den, den))
                V.scalar_tensor_tensor(m_g[d][:, :, :], m_g[d][:, :, :], 2.0, den, ALU.mult, ALU.mult).then_inc(rg_den, 1)
                dve.wait_ge(rg_den, d + 1)
            dve.wait_ge(decay_ready, 2 * RT)
            for d in range(2):
                dve.wait_ge(rg_sqrt, d + 1)
                f0 = 0 if d == 0 else T - 1
                link(V.memset(m_g[d][:, :, f0:f0 + 1], 1.0))
                link(V.tensor_tensor(i_g[d][:, :, :], i_g[d][:, :, :], xc[d][:, :, :], ALU.mult))
                link(V.tensor_tensor(i_g[d][:, :, :], i_g[d][:, :, :], m_g[d][:, :, :], ALU.mult))
                for t in range(RT):
                    a, b, o = r_g[d][:, t, :], i_g[d][:, t, :], m_g[d][:, t, :]
                    if d:
                        a, b, o = a[:, ::-1], b[:, ::-1], o[:, ::-1]
                    link(V.tensor_tensor_scan(o, a, b, 0.0, ALU.mult, ALU.add))
            link(V.tensor_tensor(m_g[1][:, :, :], m_g[1][:, :, :], m_g[0][:, :, NM:L], ALU.add))
            dve.wait_ge(in2_copied, RT + 4 * RT + RT)
            V.tensor_tensor(gg[:, :, :], gg[:, :, :], m_g[1][:, :, :], ALU.mult).then_inc(rg_ready, 1)
            for n, (f0, fn) in enumerate(LT):
                dve.wait_ge(spec_ready, n + 1)
                ure, uim = ps[0:fn, 0, :], ps[0:fn, 1, :]
                link(V.tensor_tensor(ys[0:fn, n, 0, :], ure, kre[0:fn, n, :], ALU.mult))
                link(V.tensor_tensor(ys[0:fn, n, 1, :], ure, kim[0:fn, n, :], ALU.mult))
                link(V.tensor_tensor(tmp_spec(fn, 0), uim, kim[0:fn, n, :], ALU.mult))
                link(V.tensor_tensor(tmp_spec(fn, 1), uim, kre[0:fn, n, :], ALU.mult))
                V.tensor_tensor(ys[0:fn, n, 0, :], ys[0:fn, n, 0, :], tmp_spec(fn, 0), ALU.subtract).then_inc(ys_ready, 1)
                V.tensor_tensor(ys[0:fn, n, 1, :], ys[0:fn, n, 1, :], tmp_spec(fn, 1), ALU.add).then_inc(ys_ready, 1)
                dve.wait_ge(ys_ready, 2 * n + 2)
            for c in range(HYT):
                dve.wait_ge(conv_out, c + 1)
                link(V.scalar_tensor_tensor(hu[:, 4 + c, 0:T], hu[:, c, NM:L], col("hy_skip_2", c), ps[:, 2 + c % 2, 0:T], ALU.mult, ALU.add))
                V.tensor_tensor(hu[:, 4 + c, 0:T], hu[:, 4 + c, 0:T], hu[:, 8 + c, NM:L], ALU.mult).then_inc(hy_ready, 1)
            dve.wait_ge(gg_hi, 1)
            V.tensor_tensor(gg_parts[:, 1, :, :], gg[:, :, :], gg_parts[:, 0, :, :].bitcast(F32), ALU.subtract).then_inc(gg_lo, 1)
            dve.wait_ge(in2_copied, RT + 4 * RT + RT + 16)
            for n in range(KT):
                dve.wait_ge(chunk_done, START["rgout"] + n + 1)
                link(V.tensor_tensor(tmp_mix(0), acc(n), sgl[:, n, :], ALU.mult))
                link(V.tensor_tensor(tmp_mix(1), ps[:, 4 + n % 2, 0:T], sgl[:, 8 + n, :], ALU.mult))
                V.tensor_tensor(merged2[:, n, :], tmp_mix(0), tmp_mix(1), ALU.add).then_inc(merged2_ready, 1)
                dve.wait_ge(merged2_ready, n + 1)
                if n:
                    dve.wait_ge(merged2_hi, n)
                    low_part(merged2_parts, merged2, n - 1).then_inc(merged2_lo, 1)
            dve.wait_ge(merged2_hi, KT)
            low_part(merged2_parts, merged2, KT - 1).then_inc(merged2_lo, 1)
            for n in range(KT):
                dve.wait_ge(chunk_done, START["out2"] + n + 1)
                V.tensor_tensor(real(x, n), real(x, n), ps[:, 4 + n % 2, 0:T], ALU.add).then_inc(x_ready, 1)
            dve.wait_ge(x_ready, 32)

            norm_in(7, NORMS[7], lambda k: real(x, k), lambda k: real(h, k), T)
            input_lo(4)
            tiu = ti.bitcast(U32)
            ciu = ci.bitcast(U32)

            def top16(vals, idx, src, scratch):
                link(V.max(vals[:, 0:8], src))
                V.max_index(idx[:, 0:8], vals[:, 0:8], src)
                link(V.match_replace(scratch, vals[:, 0:8], src, -3.0e38))
                link(V.max(vals[:, 8:16], scratch))
                link(V.max_index(idx[:, 8:16], vals[:, 8:16], scratch))

            for g in range(4):
                for t in range(2):
                    dve.wait_ge(sc_copied, 2 * g + t + 1)
                    for n in range(4 * g, 4 * g + 4):
                        top16(tv[:, t, n, :], tiu[:, t, n, :], sc[:, t, n, :], scr[:, 0:NK])
            for t in range(2):
                link(V.tensor_copy(tif[:, t, :, :], tiu[:, t, :, :]))
                pair = tv[:, t, :, :].rearrange("p (h c) k -> p h c k", c=2)
                link(V.tensor_tensor(cand[:, t, :, :].rearrange("p h (i j) -> p h i j", i=TOPK),
                                     pair[:, :, 0, :].unsqueeze(3).to_broadcast([P, PH, TOPK, TOPK]),
                                     pair[:, :, 1, :].unsqueeze(2).to_broadcast([P, PH, TOPK, TOPK]), ALU.add))
                for n in range(PH):
                    top16(cv[:, t, n, :], ciu[:, t, n, :], cand[:, t, n, :], scr)
                V.tensor_tensor(ew[:, 2, t, :].rearrange("p (h k) -> p h k", k=TOPK), cv[:, t, :, :],
                                cv[:, t, :, 0:1].to_broadcast([P, PH, TOPK]), ALU.subtract).then_inc(cv_ready, 1)
            dve.wait_ge(iota_ready, 3)
            cijb = cij.bitcast(U32)
            for t in range(2):
                flat = ciu[:, t, :, :].rearrange("p h k -> p (h k)")
                link(V.tensor_scalar(cijb[:, t, 0, :], flat, 4, None, ALU.logical_shift_right))
                link(V.tensor_scalar(cijb[:, t, 1, :], flat, 15, None, ALU.bitwise_and))
                link(V.tensor_copy(cijf[:, t, :, :], cijb[:, t, :, :]))
                for c in range(2):
                    link(V.tensor_tensor(hot, cijf[:, t, c, :].unsqueeze(2).to_broadcast([P, PH * TOPK, TOPK]),
                                         io16.unsqueeze(1).to_broadcast([P, PH * TOPK, TOPK]), ALU.is_equal))
                    keyf = tif[:, t, :, :].rearrange("p (h c) k -> p h c k", c=2)[:, :, c, :]
                    link(V.tensor_tensor(hot.rearrange("p (h k) i -> p h k i", k=TOPK), hot.rearrange("p (h k) i -> p h k i", k=TOPK),
                                         keyf.unsqueeze(2).to_broadcast([P, PH, TOPK, TOPK]), ALU.mult))
                    link(V.tensor_reduce(ew[:, c, t, :], hot, AX.X, ALU.add))
            dve.wait_ge(ce_ready, 1)
            wts = ew[:, 2, :, :].rearrange("p t (h k) -> p (t h) k", k=TOPK)
            link(V.tensor_reduce(small[:, 208:224], wts, AX.X, ALU.add))
            link(V.reciprocal(small[:, 208:224], small[:, 208:224]))
            V.tensor_tensor(wts, wts, small[:, 208:224].unsqueeze(2).to_broadcast([P, 2 * PH, TOPK]), ALU.mult).then_inc(ew_ready, 1)
            for n, dst in enumerate((e1t, e2t, gt)):
                dve.wait_ge(ew_turned, n + 1)
                V.tensor_copy(dst, ps[:, 1 + n, 0:T]).then_inc(ewt_ready, 1)
            dve.wait_ge(ewt_ready, 3)

            def rows(q, i=0, step=0):
                if q >= 4:
                    dve.wait_ge(g_token, i * step + (q - 3) if step else q - 3)
                t = bass.ds(i * (4 * step) + 4 * q, 4) if step else slice(4 * q, 4 * q + 4)
                row = iota.unsqueeze(1).to_broadcast([P, 4, NK])
                V.tensor_tensor(sel_b[:, q % 4, :, :], row, e2t[:, t].unsqueeze(2).to_broadcast([P, 4, NK]), ALU.is_equal)
                V.tensor_tensor(sel_a[:, q % 4, :, :], row, e1t[:, t].unsqueeze(2).to_broadcast([P, 4, NK]), ALU.is_equal).then_inc(ab_raw, 1)

            def gate_first(q, i=0, step=0):
                dve.wait_ge(g_copied, i * step + (q + 1) if step else q + 1)
                t = bass.ds(i * (4 * step) + 4 * q, 4) if step else slice(4 * q, 4 * q + 4)
                V.tensor_tensor(gates_all[:, 0:NA, t], ps[:, 4 + q % 4, :].rearrange("p (t e) -> p e t", t=4)[:, 0:NA, :], gates_all[:, 0:NA, t], ALU.mult).then_inc(g_gated, 1)

            for q in range(4):
                rows(q)
            dve.wait_ge(gelu_ready, NA)
            with dve.Fori(0, QUADS // 4 - 1) as i:
                for m in range(4):
                    rows(m + 4, i, 4)
                    gate_first(m, i, 4)
            for q in range(QUADS - 4, QUADS):
                gate_first(q)
            base = START["experts"]
            dve.wait_ge(g_gated, QUADS)

            def first_key(e, buf, i=0):
                n = base + NA + e - 1
                if e >= 2:
                    dve.wait_ge(chunk_done, i * 6 + n)
                tile = gates_all[:, bass.ds(i * 6 + e, 1), :].rearrange("p a t -> p (a t)") if e >= 2 else gates_all[:, e, :]
                n = 2 * FT + e + 1
                V.tensor_copy(peer_part[0][:, buf, :], tile).then_inc(act_hi, 1)
                dve.wait_ge(act_hi, i * 6 + n if e >= 2 else n)
                V.tensor_tensor(peer_part[1][:, buf, :], tile, peer_part[0][:, buf, :].bitcast(F32), ALU.subtract).then_inc(peer_act, 1)

            def last_first_key(e):
                dve.wait_ge(chunk_done, base + NA + e - 1)
                V.tensor_copy(peer_part[0][:, e % 2, :], gates_all[:, e, :]).then_inc(act_hi, 1)
                dve.wait_ge(act_hi, 2 * FT + e + 1)
                V.tensor_tensor(peer_part[1][:, e % 2, :], gates_all[:, e, :], peer_part[0][:, e % 2, :].bitcast(F32), ALU.subtract).then_inc(peer_act, 1)

            first_key(0, 0)
            first_key(1, 1)
            with dve.Fori(0, NA // 6 - 1) as i:
                for m in range(2, 8):
                    first_key(m, m % 2, i)
            for e in range(NA - 4, NA):
                last_first_key(e)

            def expert(tile, n, buf):
                dve.wait_ge(gelu_ready, n)
                V.tensor_tensor(act_p[:, buf, :], ge_p[:, buf, :], tile, ALU.mult).then_inc(act_gated, 1)
                dve.wait_ge(act_gated, n + (2 * FT - NA))
                V.tensor_copy(peer_part[0][:, buf, :], act_p[:, buf, :]).then_inc(act_hi, 1)
                dve.wait_ge(act_hi, n + 2 * FT)
                V.tensor_tensor(peer_part[1][:, buf, :], act_p[:, buf, :], peer_part[0][:, buf, :].bitcast(F32), ALU.subtract).then_inc(peer_act, 1)

            for e in (NA, NA + 1):
                dve.wait_ge(chunk_done, base + NA + e - 1)
                expert(gates_all[:, e, :], e + 1, e % 2)
                if e == NA:
                    lo(base + expert_v(NA))
            with dve.Fori(0, N_PAIRS) as i:
                for m in range(2, 8):
                    lo(base + expert_v(NA + m - 1), i, 12, 6)
                    dve.wait_ge(chunk_done, i * 12 + (base + expert_v(NA + m - 2) + 1))
                    expert(gates_all[:, bass.ds(i * 6 + (NA + m), 1), :].rearrange("p a t -> p (a t)"), i * 6 + (NA + m + 1), m % 2)
            lo(base + 2 * NK - 1)
            dve.wait_ge(chunk_done, N_CHUNKS)
            for n in range(KT):
                V.tensor_tensor(real(x, n), real(x, n), acc(n), ALU.add).then_inc(x_ready, 1)
            dve.wait_ge(x_ready, 40)
            norm_in(8, NORMS[8], lambda k: real(x, k), lambda k: real(h, k), T)

        @block.tensor
        def _(pe):
            M = nc.tensor.matmul

            def land(c):
                pe.wait_ge(landed[c % NS], 16 * (c // NS + 1))

            def tile_whole(c, out, rhs, nk, slot_cols):
                land(c)
                for k in range(nk):
                    ins = M(out, ring[:, c % NS, slot_cols + k * P:slot_cols + (k + 1) * P], rhs(k), start=(k == 0), stop=(k == nk - 1))
                return ins

            def low(c, i=0, step=0):
                pe.wait_ge(lo_pool if BY[c] == "pool" else lo_dve, later(LO[c], i, step))

            def product(out, c, cols_at, parts, start, stop):
                w_hi, w_lo = hi_part(c)[:, cols_at:cols_at + P], ring_lo[:, c % NS, cols_at:cols_at + P]
                M(out, w_hi, parts[0], start=start, stop=False, skip_group_check=True)
                M(out, w_hi, parts[1], start=False, stop=False, skip_group_check=True)
                return M(out, w_lo, parts[0], start=False, stop=stop, skip_group_check=True)

            def tile(c, out, parts, ready=None):
                low(c)
                for k in range(KT):
                    if ready:
                        pe.wait_ge(ready[0], ready[1] + k + 1)
                    ins = product(out, c, k * P, parts(k), k == 0, k == KT - 1)
                return ins

            def h_real(k):
                return h_parts[0][:, k, NM:L], h_parts[1][:, k, NM:L]

            def h_all(k):
                return h_parts[0][:, k, :], h_parts[1][:, k, :]

            def spread(out, column, tn):
                return M(out, column.to_broadcast([tn, P]), ident[0:tn, 0:tn], start=True, stop=True)

            def sums(n, w):
                if n:
                    pe.wait_ge(var_ready, n)
                tiles = LT[0:2] if w == T else LT
                for k in range(KT):
                    pe.wait_ge(sq_ready, KT * n + k + 1)
                    for t, (t0, tn) in enumerate(tiles):
                        ins = M(ps[0:tn, 6, t:t + 1], sq[:, k, t0:t0 + tn], ones[:, 0:1], start=(k == 0 and t == 0), stop=(k == KT - 1), skip_group_check=True)
                ins.then_inc(ssq_ready, 1)
                pe.wait_ge(rstd_ready, n + 1)
                for t, (t0, tn) in enumerate(tiles):
                    ins = spread(ps[:, 7, t0:t0 + tn], rstd_t[0:tn, t:t + 1], tn)
                ins.then_inc(rstd_spread, 1)

            pe.wait_ge(loaded_vec, 16 * 3)
            sums(0, T)

            def ffn(f, base):
                def first(j, buf, i=0, step=0):
                    for half in range(2):
                        c = ffn_up(base, j) - 1 + half
                        low(c, i, step)
                        for k in range(KT):
                            if j == 0 and half == 0:
                                pe.wait_ge(h_lo, f * 2 * KT + k + 1)
                            ins = product(ps[:, 4 + buf, half * T:(half + 1) * T], c, k * P, h_real(k), k == 0, k == KT - 1)
                        ins.then_inc(chunk_done, 1)

                def second(j, buf, begin, end, i=0, step=0):
                    c = ffn_down(base, j)
                    low(c, i, step)
                    for t in range(KT):
                        ins = product(acc(t), c, t * P, (ffn_act[0][:, buf, :], ffn_act[1][:, buf, :]), begin and t % 2 == 0, end)
                    ins.then_inc(chunk_done, 1)

                first(0, 0)
                first(1, 1)
                pe.wait_ge(act_ready, f * FT + 1)
                second(0, 0, True, False)
                with pe.Fori(0, (FT - 2) // 2) as i:
                    for m in (2, 3):
                        pe.wait_ge(act_ready, i * 2 + (f * FT + m - 1))
                        first(m, m % 2, i, 4)
                        pe.wait_ge(act_ready, i * 2 + (f * FT + m))
                        second(m - 1, (m - 1) % 2, False, False, i, 2)
                pe.wait_ge(act_ready, f * FT + FT)
                second(FT - 1, (FT - 1) % 2, False, True)

            ffn(0, START["ffn1"])
            sums(1, T)
            sums(2, T)
            def swap_tile(n):
                pe.wait_ge(raw_copied, n + 1)
                if n >= 2:
                    pe.wait_ge(qk_ready, n - 1)
                if n == 0:
                    pe.wait_ge(var_ready, 3)
                M(ps[:, 6 + n % 2, 0:T], swap, raw[:, n % 2, :], start=True, stop=True).then_inc(swapped, 1)

            def between(n):
                if n == 2:
                    pe.wait_ge(loaded_const, 16 * N_CONST)
                    pe.wait_ge(iota_ready, 1)
                    M(ps[0:FW, 1, 0:L], w1[0:2 * HB + 1, :], zt[0:2 * HB + 1, :], start=True, stop=True).then_inc(flt_pe, 1)
                if n == 5:
                    pe.wait_ge(flt_sin, 1)
                    M(ps[0:FW, 1, 0:L], w2[0:FW, :], hdn[0:FW, :], start=True, stop=True).then_inc(flt_pe, 1)
                if n in (8, 11, 14):
                    m = (n - 8) // 3
                    t0, tn = LT[m]
                    if m:
                        pe.wait_ge(flt_k, 2 * m)
                    else:
                        pe.wait_ge(flt_sin, 2)
                    for d in range(2):
                        ins = M(ps[0:tn, 1 + d, :], hdn[0:FW + 1, t0:t0 + tn], w3[0:FW + 1, d * HY:(d + 1) * HY], start=True, stop=True)
                    ins.then_inc(flt_pe, 1)
                if n in (17, 20, 23):
                    m = (n - 17) // 3
                    f0, fn = LT[m]
                    pe.wait_ge(flt_k, 6 + 2 * m)
                    for d, src in ((0, ksum), (1, kdif)):
                        for k, (t0, tn) in enumerate(LT):
                            ins = M(ps[0:fn, 1 + d, :], dft[0:tn, k, d, f0:f0 + fn], src[0:tn, k, :], start=(k == 0), stop=(k == 2))
                    ins.then_inc(flt_pe, 1)

            pe.wait_ge(lam_prod, 2)
            M(ps[:, 0, 0:2], ones, small[:, 0:2], start=True, stop=True).then_inc(lam_sum, 1)
            for n in range(28):
                if n >= 2:
                    pe.wait_ge(raw_copied, n - 1)
                tile(START["qk"] + n, ps[:, 4 + n % 2, 0:T], h_real, (h_lo, KT) if n == 0 else None).then_inc(chunk_done, 1)
                if n:
                    swap_tile(n - 1)
                between(n)
            swap_tile(27)
            pe.wait_ge(flt_k, 12)
            pe.wait_ge(lam_exp, 1)
            for name, width, b0 in (("va", D, 0), ("vd", 3 * DIL_H * DH, 4)):
                if b0:
                    pe.wait_ge(qk_ready, 28)
                for k in range(KT):
                    c = START[name] + k
                    low(c)
                    for t in range(2):
                        tokens = slice(NM + t * P, NM + (t + 1) * P)
                        for n in range(2):
                            w = min(512, width - 512 * n)
                            for m, (a, b) in enumerate(((0, hi_part(c)), (0, ring_lo[:, c % NS, :]), (1, hi_part(c)))):
                                ins = M(ps[:, b0 + 2 * t + n, 0:w], h_parts[a][:, k, tokens], b[:, n * 512:n * 512 + w], start=(k == 0 and m == 0), stop=(k == KT - 1 and m == 2))
                    ins.then_inc(chunk_done, 1)
            pe.wait_ge(v_copied, 8)

            def da_score(hd):
                if hd >= 2:
                    pe.wait_ge(da_exp, 4 * (hd - 1))
                for c in range(2):
                    r0 = DH * c
                    for q in range(2):
                        ins = M(ps[:, 2 * (hd % 2) + c, q * T:(q + 1) * T], qk[r0:r0 + DH, hd, q * P:(q + 1) * P], qk[r0:r0 + DH, 8 + hd, :], start=True, stop=True)
                ins.then_inc(da_scores, 1)

            def gate_tile(n):
                if n >= 2:
                    pe.wait_ge(gate_copied, n - 1 if n < DA_H or n >= 14 else n)
                tile(START["gates"] + n, gate_bank(n), h_real).then_inc(chunk_done, 1)

            def da_values(hd):
                pe.wait_ge(da_tcopied, hd + 1)
                if hd:
                    pe.wait_ge(ot_ready, hd)
                for kt in range(2):
                    ins = M(ps[:, 7, 0:T], va[:, kt, hd * P:(hd + 1) * P], da_at[:, hd % 2, kt * T:(kt + 1) * T], start=(kt == 0), stop=(kt == 1))
                ins.then_inc(da_out, 1)

            da_score(0)
            for hd in range(DA_H):
                if hd + 1 < DA_H:
                    da_score(hd + 1)
                gate_tile(hd)
                if hd:
                    da_values(hd - 1)
                pe.wait_ge(da_mixed, 2 * (hd + 1))
                for kt in range(2):
                    for q in range(2):
                        ins = nc.tensor.transpose(ps[:, 6, kt * T + q * P:kt * T + (q + 1) * P], da_a[:, hd % 2, q, kt * P:(kt + 1) * P], ident)
                ins.then_inc(da_turned, 1)

            def dl_score(j):
                r0 = DH * (j % 2)
                if j:
                    pe.wait_ge(dl_nbias, j)
                for g in range(3):
                    n = (DIL_H * g + j) // 2
                    for q in range(2):
                        ins = M(ps[:, g, q * T:(q + 1) * T], qk[r0:r0 + DH, 16 + n, q * P:(q + 1) * P], qk[r0:r0 + DH, 22 + n, :], start=True, stop=True)
                ins.then_inc(dl_scores, 1)

            dl_score(0)
            da_values(DA_H - 1)
            gate_tile(DA_H)
            pe.wait_ge(ot_ready, DA_H)
            for j in range(DIL_H):
                r0 = DH * (j % 2)
                if j == 0:
                    dl_score(1)
                    gate_tile(DA_H + 1)
                pe.wait_ge(dl_prob, 2 * (j + 1))
                for g in range(3):
                    for kt in range(2):
                        for q in range(2):
                            ins = nc.tensor.transpose(ps[:, 3 + g, kt * T + q * P:kt * T + (q + 1) * P], dl_p[j % 2][:, g, q, kt * P:(kt + 1) * P], ident)
                ins.then_inc(dl_turned, 1)
                if j + 2 < DIL_H:
                    dl_score(j + 2)
                if j + 1 < DIL_H:
                    gate_tile(DA_H + 2 + j)
                pe.wait_ge(dl_tcopied, j + 1)
                if j:
                    pe.wait_ge(od_ready, j)
                for n in range(6):
                    g, kt = n // 2, n % 2
                    at = (DIL_H * g + j) * DH
                    ins = M(ps[r0:r0 + DH, 7, 0:T], vd[:, kt, at:at + DH], dl_pt[:, g, kt, :], start=(n == 0), stop=(n == 5))
                ins.then_inc(dl_out, 1)
            for hd in range(DA_H):
                pe.wait_ge(sub_sq, hd + 1)
                for t in range(2):
                    c = 2 * hd + t
                    ins = M(ps[:, 0, c:c + 1], merged[:, hd, t * P:(t + 1) * P], ones[:, 0:1], start=True, stop=True)
            ins.then_inc(sub_sum, 1)
            gate_tile(13)
            pe.wait_ge(sub_rstd, 1)
            for hd in range(DA_H):
                for t in range(2):
                    c = 2 * hd + t
                    ins = spread(acc(hd)[:, t * P:(t + 1) * P], sub_rstd_t[:, c:c + 1], P)
                if hd % 2:
                    ins.then_inc(sub_spread, 1)
            pe.wait_ge(od_ready, DIL_H)
            gate_tile(14)
            gate_tile(15)
            pe.wait_ge(od_ready, DIL_H)
            pe.wait_ge(oa_ready, DA_H)
            for n in range(KT):
                c = START["proj_b"] + n // 4
                ins = tile_whole(c, acc(n), lambda k: odt[:, k, :], 2, (n % 4) * 2 * P)
                if n % 4 == 3:
                    ins.then_inc(chunk_done, 1)
            for n in range(KT):
                if n >= 2:
                    pe.wait_ge(merged_ready, n - 1)
                tile(START["proj_a"] + n, ps[:, 4 + n % 2, 0:T], lambda k: (oa_parts[:, 0, k, :], oa_parts[:, 1, k, :]), (oa_lo, 0) if n == 0 else None).then_inc(chunk_done, 1)
            pe.wait_ge(merged_ready, KT)
            for n in range(KT):
                tile(START["out1"] + n, acc(n), lambda k: (merged_parts[:, 0, k, :], merged_parts[:, 1, k, :]), (merged_lo, 0) if n == 0 else None).then_inc(chunk_done, 1)
            sums(3, T)
            sums(4, T)
            ffn(1, START["ffn2"])
            sums(5, T)
            sums(6, L)

            for n in range(RT):
                if n >= 2:
                    pe.wait_ge(in2_copied, n - 1)
                tile(START["rgx"] + n, ps[:, 4 + n % 2, 0:L], h_all, (h_lo, 3 * KT) if n == 0 else None).then_inc(chunk_done, 1)
            pe.wait_ge(in2_copied, RT)
            for n in range(12):
                if n >= 6:
                    pe.wait_ge(hy_conv, n - 5)
                tile(START["hyena"] + n, hyena_bank(n)[:, 0:L], h_all).then_inc(chunk_done, 1)
            pe.wait_ge(rg_conv, RT)
            pe.wait_ge(var_ready, 7)
            for d in range(2):
                w = L if d == 0 else T
                for g in range(2):
                    c = START["rggate"] + 2 * d + g
                    land(c)
                    for t in range(RT):
                        n = (2 * d + g) * RT + t
                        if n >= 2:
                            pe.wait_ge(in2_copied, RT + n - 1)
                        M(ps[:, 6 + n % 2, 0:w], ring[:, c % NS, t * P:(t + 1) * P], xc[d][:, t, :], start=True, stop=True).then_inc(rg_gated, 1)
                    pe.wait_ge(rg_gated, (2 * d + g + 1) * RT)
                    pe.sem_inc(chunk_done, 1)
            pe.wait_ge(vx_ready, HYT)
            for n, (t0, tn) in enumerate(LT):
                for c in range(HYT):
                    ins = nc.tensor.transpose(ps[0:tn, n, c * P:(c + 1) * P], hu[:, c, t0:t0 + tn], ident)
                ins.then_inc(vt_turned, 1)
            pe.wait_ge(in2_copied, 5 * RT)
            for n in range(RT):
                if n >= 4:
                    pe.wait_ge(in2_copied, 5 * RT + n - 3)
                tile(START["rgg"] + n, ps[:, 4 + n % 4, 0:T], h_real).then_inc(chunk_done, 1)
            pe.wait_ge(vt_ready, 3)
            for n, (f0, fn) in enumerate(LT):
                if n:
                    pe.wait_ge(ys_ready, 2 * n)
                for d in range(2):
                    for m, (t0, tn) in enumerate(LT):
                        ins = M(ps[0:fn, d, :], dft[0:tn, m, d, f0:f0 + fn], vt(m)[0:tn, :], start=(m == 0), stop=(m == 2))
                ins.then_inc(spec_ready, 1)
                for m in (range(10), range(10, 13), range(13, 16))[n]:
                    gl_tile(pe, tile, m)
            pe.wait_ge(ys_ready, 6)
            for c in range(HYT):
                if c >= 2:
                    pe.wait_ge(hy_ready, c - 1)
                for n, (f0, fn) in enumerate(LT):
                    for d in range(2):
                        ins = M(ps[:, 2 + c % 2, 0:T], ys[0:fn, n, d, c * P:(c + 1) * P], idft[0:fn, n, d, :], start=(n == 0 and d == 0), stop=(n == 2 and d == 1))
                ins.then_inc(conv_out, 1)
            pe.wait_ge(hy_ready, HYT)
            for n in range(KT):
                ins = tile_whole(START["hyout"] + n // 2, acc(n), lambda k: hu[:, 4 + k, 0:T], 4, (n % 2) * 4 * P)
                if n % 2:
                    ins.then_inc(chunk_done, 1)
            pe.wait_ge(gg_lo, 1)
            pe.wait_ge(in2_copied, 6 * RT + 16)
            for n in range(KT):
                if n >= 2:
                    pe.wait_ge(merged2_ready, n - 1)
                tile(START["rgout"] + n, ps[:, 4 + n % 2, 0:T], lambda k: (gg_parts[:, 0, k, :], gg_parts[:, 1, k, :])).then_inc(chunk_done, 1)
            pe.wait_ge(merged2_ready, KT)
            for n in range(KT):
                if n >= 2:
                    pe.wait_ge(x_ready, 24 + n - 1)
                tile(START["out2"] + n, ps[:, 4 + n % 2, 0:T], lambda k: (merged2_parts[:, 0, k, :], merged2_parts[:, 1, k, :]), (merged2_lo, 0) if n == 0 else None).then_inc(chunk_done, 1)

            sums(7, T)
            pe.wait_ge(x_ready, 32)
            def key_scores(n):
                g = n // 4
                pe.wait_ge(pq_copied, n + 1)
                if n == 0:
                    pe.wait_ge(loaded_keys, 16)
                if n % 4 == 0 and g >= 2:
                    pe.wait_ge(sc_copied, 2 * (g - 1))
                for t in range(2):
                    ins = M(ps[:, 2 * t + g % 2, (n % 4) * P:(n % 4 + 1) * P], pq[:, n, t * P:(t + 1) * P], keys[:, n, :], start=True, stop=True)
                    if n % 4 == 3:
                        ins.then_inc(sc_out, 1)

            for n in range(16):
                if n >= 2:
                    pe.wait_ge(pq_copied, n - 1)
                tile(START["wq"] + n, ps[:, 4 + n % 2, 0:T], h_real, (h_lo, 4 * KT) if n == 0 else None).then_inc(chunk_done, 1)
                if n:
                    key_scores(n - 1)
            key_scores(15)
            base = START["experts"]

            def first(e, i=0, step=0):
                c = base + expert_u(e)
                low(c, i, step)
                for k in range(KT):
                    ins = product(ps[:, 4 + e % 2, 0:T], c, k * P, h_real(k), k == 0, k == KT - 1)
                ins.then_inc(chunk_done, 1)

            def second(e, begin=False, end=False, i=0, step=0):
                c = base + expert_v(e)
                low(c, i, step)
                pe.wait_ge(peer_act, later(e + 1, i, step))
                for t in range(KT):
                    ins = product(acc(t), c, t * P, (peer_part[0][:, e % 2, :], peer_part[1][:, e % 2, :]), begin and t % 2 == 0, end)
                ins.then_inc(chunk_done, 1)

            first(0)
            first(1)
            with pe.Fori(0, NA // 6 - 1) as i:
                for m in range(2, 8):
                    pe.wait_ge(gelu_ready, i * 6 + (m - 1))
                    first(m, i, 6)
            for e in range(NA - 4, NA):
                pe.wait_ge(gelu_ready, e - 1)
                first(e)
            pe.wait_ge(ew_ready, 1)
            for n in range(3):
                for t in range(2):
                    ins = nc.tensor.transpose(ps[:, 1 + n, t * P:(t + 1) * P], ew[:, n, t, :], ident)
                ins.then_inc(ew_turned, 1)
            pe.wait_ge(gelu_ready, NA)

            def four(q, i=0, step=0):
                pe.wait_ge(ab_ready, i * step + (q + 1) if step else q + 1)
                for m in range(4):
                    ins = M(ps[:, 4 + q % 4, m * P:(m + 1) * P], sel_b[:, q % 4, m, :], sel_a[:, q % 4, m, :], start=True, stop=True)
                ins.then_inc(g_token, 1)

            for q in range(4):
                four(q)
            with pe.Fori(0, QUADS // 4 - 1) as i:
                for m in range(4, 8):
                    pe.wait_ge(g_gated, i * 4 + (m - 3))
                    four(m, i, 4)
            pe.wait_ge(g_gated, QUADS)
            second(0, begin=True)
            for e in range(1, 6):
                second(e)
            with pe.Fori(0, NA // 6 - 1) as i:
                for m in range(6, 12):
                    second(m, i=i, step=6)
            first(NA)
            first(NA + 1)
            second(NA)
            with pe.Fori(0, N_PAIRS) as i:
                for m in range(2, 8):
                    pe.wait_ge(gelu_ready, i * 6 + (NA + m - 1))
                    first(NA + m, i, 6)
                    second(NA + m - 1, i=i, step=6)
            second(NK - 1, end=True)
            sums(8, T)


def _by_tile(w, t=P):
    k, n = w.shape
    return w.reshape(k // P, P, n // t, t).transpose(2, 1, 0, 3).reshape(n // t, P, -1)


def _by_row(w):
    return w.reshape(w.shape[0] // P, P, w.shape[1])


def _stream(i):
    def lagged(first, second):
        out = [first[0]]
        for j in range(1, len(second)):
            out += [first[j], second[j - 1][None]]
        return out + [second[-1][None]]

    def mlp(gu, down):
        up = _by_tile(gu)
        return lagged([np.stack([up[j], up[FT + j]]) for j in range(FT)], _by_row(down))

    w = i["w_in"][0]
    cuts = np.cumsum([0, D, D, D, 768, 768, 768, D, D])
    qa, ka, va, qd, kd, vd, ga, gb = (w[:, a:b] for a, b in zip(cuts[:-1], cuts[1:]))
    w2 = i["w_in_2"][0]
    cuts = np.cumsum([0, HY, HY, HY, D, D, 2 * D])
    x0, x1, v, rx, rg, gl = (w2[:, a:b] for a, b in zip(cuts[:-1], cuts[1:]))
    pad = np.zeros((D, D - 768), np.float32)
    u = i["peer_u_2"][0].reshape(NK, NK, KT, P).transpose(0, 3, 2, 1).reshape(NK, P, D)
    vv = i["peer_v_2"][0].reshape(NK, NK, D)
    parts = (
        mlp(i["w_gu1"][0], i["w_down1"][0])
        + [_by_tile(m) for m in (qa, ka, qd, kd)]
        + [_by_row(va), _by_row(np.concatenate([vd, pad], 1)), _by_tile(ga), _by_tile(gb)]
        + [_by_tile(i["w_proj_b"][0]).reshape(2, 4, P, 2 * P).transpose(0, 2, 1, 3).reshape(2, P, CW)]
        + [_by_tile(i["w_proj_a"][0]), _by_tile(i["w_out"][0])]
        + mlp(i["w_gu2"][0], i["w_down2"][0])
        + [_by_tile(m) for m in (rx, v, x1, x0)]
        + [i["rg_gate_w_2"][0].transpose(0, 1, 3, 2, 4).reshape(4, P, CW)]
        + [_by_tile(rg), _by_tile(gl)]
        + [_by_tile(i["hy_out_2"][0]).reshape(4, 2, P, 4 * P).transpose(0, 2, 1, 3).reshape(4, P, CW)]
        + [_by_tile(i["rg_out_2"][0]), _by_tile(i["w_out_2"][0]), _by_tile(i["peer_wq_2"][0])]
        + [u[:NA], vv[:NA]] + lagged(list(u[NA:, None]), vv[NA:])
    )
    out = np.concatenate(parts, 0)
    assert out.shape == (N_CHUNKS, P, CW), out.shape
    return out


def _columns(i):
    d = np.arange(P) % DH
    inv = (np.float32(THETA) ** (-(np.arange(0, ROT, 2, dtype=np.float32) / np.float32(ROT)))).astype(np.float32)
    table = {
        "rope_inv": np.where(d < ROT, inv[d % (ROT // 2)], 0).astype(np.float32),
        "rope_sign": np.where(d < ROT // 2, -1, 1).astype(np.float32),
    }
    out = []
    for name, n in COLUMNS:
        a = table[name] if name in table else np.asarray(i[name])
        width = min(P, a.size // n)
        c = a.reshape(n, width).T
        if width < P:
            c = np.concatenate([c, np.zeros((P - width, n), np.float32)], 0)
        out.append(c)
    return np.ascontiguousarray(np.concatenate(out, 1))


def _tiled(a):
    out = np.zeros((3 * P,) + a.shape[1:], np.float32)
    out[:L] = a
    return np.ascontiguousarray(np.moveaxis(out.reshape((3, P) + a.shape[1:]), 0, 1))


def _constants():
    f32 = np.float32
    t = np.linspace(0.0, 1.0, L, dtype=f32)[:, None]
    w = (f32(2.0 * math.pi / L) * np.arange(L, dtype=f32))[:, None]
    bands = np.linspace(1e-4, HB - 1, HB, dtype=f32)[None, :]
    z = np.concatenate([t, np.cos(bands * w), -np.sin(bands * w)], 1).astype(f32)
    deltas = np.abs(np.linspace(math.log(1e-2) / 0.3, math.log(1e-2) / 1.5, HY, dtype=f32))
    decay = np.exp(-t * deltas).astype(f32)
    back = decay.copy()
    back[0] = 0.0
    s, f = np.arange(L, dtype=np.float64), np.arange(L, dtype=np.float64) + 0.5
    a = 2.0 * math.pi * np.outer(s, f) / (2 * L)
    dft = np.stack([np.cos(a), -np.sin(a)], 1).astype(f32)
    a = 2.0 * math.pi * np.outer(f, np.arange(NM, L)) / (2 * L)
    idft = (np.stack([np.cos(a), -np.sin(a)], 1) / L).astype(f32)
    q, k = np.arange(T)[:, None], np.arange(T)[None, :]
    mask = []
    for dil, half in DIL:
        seen = ((q - k) % dil == 0) & (abs(q - k) <= half * dil)
        mask.append(np.where(seen, 0.0, NEG * math.sqrt(DH)).astype(f32).reshape(2, P, T).transpose(1, 0, 2))
    swap = np.zeros((P, P), f32)
    d = np.arange(P)
    r = d % DH
    swap[np.where(r < 8, d + 8, np.where(r < ROT, d - 8, d)), d] = 1.0
    sq = np.stack([np.eye(P, dtype=f32), swap, np.ones((P, P), f32)], 1)
    return {"zt": np.ascontiguousarray(z.T), "decay": _tiled(np.stack([decay, back], 1)), "dft": _tiled(dft), "idft": _tiled(idft),
            "mask": np.ascontiguousarray(np.stack(mask, 1)), "squares": np.ascontiguousarray(sq)}


def kernel(**inputs):
    import concourse.bacc as bacc
    from concourse.bass_utils import run_bass_kernel_spmd

    i = {k: np.asarray(v) for k, v in inputs.items()}
    c = _constants()

    def features(a):
        return np.ascontiguousarray(a.T.reshape(KT, P, -1).transpose(1, 0, 2))

    arrays = {
        "x": features(i["x"][0]), "meta": features(i["meta_2"]),
        "positions": np.ascontiguousarray(np.broadcast_to(i["positions"][0], (P, T))),
        "stream": _stream(i), "columns": _columns(i),
        "filter_w1": i["hy_w1_2"][0], "filter_w2": i["hy_w2_2"][0],
        "filter_w3": np.concatenate([i["hy_w3_2"][0], i["hy_b3_2"]], 0),
        "zt": c["zt"], "decay": c["decay"], "dft": c["dft"], "idft": c["idft"], "mask": c["mask"], "squares": c["squares"],
        "keys": np.ascontiguousarray(i["peer_keys_2"][0].reshape(2 * PH, NK, P).transpose(2, 0, 1)),
    }
    nc = bacc.Bacc("TRN2", target_bir_lowering=False, num_devices=1)
    args = [nc.dram_tensor(f"in_{n}", a.shape, mybir.dt.from_np(a.dtype), kind="ExternalInput").ap() for n, a in arrays.items()]
    out = nc.dram_tensor("out", (P, KT, T), F32, kind="ExternalOutput").ap()
    build(nc, *args, out)
    r = run_bass_kernel_spmd(nc, [{f"in_{n}": a for n, a in arrays.items()}], core_ids=[0])
    got = r.results[0]["out"]
    return got.transpose(2, 1, 0).reshape(1, T, D)
```
